# Optimizing a Trainium2 kernel written in Bass

```python
import jax
import jax.numpy as jnp
from jax import lax
import numpy as np

D_MODEL = 1024
BATCH = 1
SEQ = 1024
DEPTH = 1

CHUNK = 64
HEAD_DIM = 64
RWKV_WIDTH = D_MODEL // 2
RWKV_HEADS = RWKV_WIDTH // HEAD_DIM
DSA_WIDTH = D_MODEL - RWKV_WIDTH
DSA_HEADS = DSA_WIDTH // HEAD_DIM
MIX_WIDTH = RWKV_WIDTH + DSA_WIDTH
DECAY_LORA = 64
AAA_LORA = 64
GATE_LORA = 128
GN_EPS = HEAD_DIM * 1e-5
KV_LATENT = 128
IDX_HEADS = 4
IDX_DIM = 64
TOPK_MAX = 256
Q_BLOCK = 128
N_GROUPS = 4
EXPERTS_PER_GROUP = 8
N_EXPERTS = N_GROUPS * EXPERTS_PER_GROUP
D_EXPERT = 512
TOP_K_EXPERT = 2
MOE_BLOCK = 128
NORM_EPS = 1e-6
ADA_INIT = 0.5

RWKV_SPLITS = (RWKV_WIDTH, RWKV_WIDTH, RWKV_WIDTH, DECAY_LORA, AAA_LORA, GATE_LORA)
DSA_SPLITS = (DSA_WIDTH, KV_LATENT, IDX_HEADS * IDX_DIM, IDX_DIM, IDX_HEADS)
RWKV_COLS = sum(RWKV_SPLITS)
IN_COLS = RWKV_COLS + sum(DSA_SPLITS)

kernel_name = 'hybrid_rwkv7_dsa_hmoe_block'

def rms_norm(x, g):
    xf = x.astype(jnp.float32)
    y = xf * lax.rsqrt(jnp.mean(xf * xf, axis=-1, keepdims=True) + NORM_EPS)
    return (y * g.astype(jnp.float32)).astype(x.dtype)

def modulate(h, shift, scale):
    return h * (1 + scale[:, None, :]) + shift[:, None, :]

def split_cols(t, sizes):
    return jnp.split(t, np.cumsum(sizes)[:-1].tolist(), axis=-1)

def rwkv7_time_mix(p, shift_mu, w0, w_decay_up, a0, w_aaa_up, w_gate_up, k_k, k_a, r_k, gn_g, gn_b):
    B, S, _ = p.shape
    f32 = jnp.float32
    p_prev = jnp.pad(p, ((0, 0), (1, 0), (0, 0)))[:, :-1]
    p = p + shift_mu * (p_prev - p)
    r, k, v, wl, al, gl = split_cols(p, RWKV_SPLITS)
    log_w = -jax.nn.softplus(-(w0 + jnp.tanh(wl) @ w_decay_up)) - 0.5
    decay = jnp.exp(-jnp.exp(log_w.astype(f32)))
    a = jax.nn.sigmoid(a0 + al @ w_aaa_up)
    g = jax.nn.sigmoid(gl) @ w_gate_up
    heads = lambda t: t.reshape(B, S, RWKV_HEADS, HEAD_DIM).astype(f32)
    kk = heads(k * k_k)
    kk = kk / jnp.maximum(jnp.sqrt(jnp.sum(kk * kk, axis=-1, keepdims=True)), 1e-12)
    k = k * (1 + (a - 1) * k_a)
    r_h, k_h, v_h, a_h, w_h = heads(r), heads(k), heads(v), heads(a), heads(decay)

    def step(state, inp):
        r_t, w_t, k_t, v_t, kk_t, a_t = inp
        sa = jnp.einsum('bhij,bhj->bhi', state, -kk_t)
        state = (state * w_t[:, :, None, :] + sa[..., None] * (kk_t * a_t)[:, :, None, :]
                 + v_t[..., None] * k_t[:, :, None, :])
        return state, jnp.einsum('bhij,bhj->bhi', state, r_t)

    seq_first = lambda t: jnp.swapaxes(t, 0, 1)
    init = jnp.zeros((B, RWKV_HEADS, HEAD_DIM, HEAD_DIM), f32)
    _, y = lax.scan(step, init, (seq_first(r_h), seq_first(w_h), seq_first(k_h),
                                 seq_first(v_h), seq_first(kk), seq_first(a_h)))
    y = seq_first(y)
    mu = jnp.mean(y, axis=-1, keepdims=True)
    var = jnp.mean(jnp.square(y - mu), axis=-1, keepdims=True)
    y = ((y - mu) * lax.rsqrt(var + GN_EPS)).reshape(B, S, RWKV_WIDTH) * gn_g + gn_b
    bonus = (jnp.sum(r_h * k_h * r_k, axis=-1, keepdims=True) * v_h).reshape(B, S, RWKV_WIDTH)
    return ((y + bonus) * g).astype(p.dtype)

def dsa_mix(q, ckv, q_idx, k_idx, w_idx, kv_norm_g, k_idx_norm_g, w_uk, w_uv):
    B, S, _ = q.shape
    topk = min(TOPK_MAX, S // 4)
    f32 = jnp.float32
    ckv = rms_norm(ckv, kv_norm_g)
    q_lat = jnp.einsum('bshd,chd->bshc', q.reshape(B, S, DSA_HEADS, HEAD_DIM), w_uk)
    q_idx = q_idx.reshape(B, S, IDX_HEADS, IDX_DIM)
    k_idx = rms_norm(k_idx, k_idx_norm_g)
    key_chunk = jnp.arange(S) // CHUNK
    gather = jax.vmap(lambda table, idx: table[idx])

    def block(start):
        qi = lax.dynamic_slice_in_dim(q_idx, start, Q_BLOCK, axis=1)
        wi = lax.dynamic_slice_in_dim(w_idx, start, Q_BLOCK, axis=1)
        ql = lax.dynamic_slice_in_dim(q_lat, start, Q_BLOCK, axis=1)
        q_chunk = (start + jnp.arange(Q_BLOCK)) // CHUNK
        admissible = key_chunk[None, :] <= q_chunk[:, None]
        rel = jax.nn.relu(jnp.einsum('bqhd,bsd->bqhs', qi, k_idx).astype(f32) * IDX_DIM ** -0.5)
        score = jnp.einsum('bqh,bqhs->bqs', wi.astype(f32) * IDX_HEADS ** -0.5, rel)
        score = jnp.where(admissible[None], score, -jnp.inf)
        _, sel = lax.top_k(score, topk)
        valid = (sel // CHUNK) <= q_chunk[None, :, None]
        kv = gather(ckv, sel)
        logits = jnp.einsum('bqhc,bqkc->bqhk', ql, kv).astype(f32) * HEAD_DIM ** -0.5
        logits = jnp.where(valid[:, :, None, :], logits, -jnp.inf)
        prob = jax.nn.softmax(logits, axis=-1).astype(kv.dtype)
        o_lat = jnp.einsum('bqhk,bqkc->bqhc', prob, kv)
        return jnp.einsum('bqhc,chd->bqhd', o_lat, w_uv).reshape(B, Q_BLOCK, DSA_WIDTH)

    out = lax.map(block, jnp.arange(S // Q_BLOCK) * Q_BLOCK)
    return jnp.swapaxes(out, 0, 1).reshape(B, S, DSA_WIDTH)

def hierarchical_moe(h, w_group, b_group, w_expert, b_expert, e_gate, e_up, e_down):
    B, S, D = h.shape
    f32 = jnp.float32
    n_tok = B * S
    xf = h.reshape(n_tok, D)
    g_logits = (xf @ w_group).astype(f32) + b_group.astype(f32)
    g_sel = jnp.argmax(g_logits, axis=-1)
    p_group = jnp.take_along_axis(jax.nn.softmax(g_logits, axis=-1), g_sel[:, None], axis=1)
    e_logits = ((xf @ w_expert).astype(f32) + b_expert.astype(f32)).reshape(n_tok, N_GROUPS, EXPERTS_PER_GROUP)
    e_logits = jnp.take_along_axis(e_logits, g_sel[:, None, None], axis=1)[:, 0]
    top_p, top_i = lax.top_k(jax.nn.softmax(e_logits, axis=-1), TOP_K_EXPERT)
    weight = (p_group * top_p / jnp.sum(top_p, axis=-1, keepdims=True)).reshape(-1)
    expert = (g_sel[:, None] * EXPERTS_PER_GROUP + top_i).reshape(-1)
    token = jnp.repeat(jnp.arange(n_tok), TOP_K_EXPERT)
    n_assign = n_tok * TOP_K_EXPERT
    order = jnp.argsort(expert)
    s_exp, s_tok, s_w = expert[order], token[order], weight[order]
    counts = jnp.bincount(expert, length=N_EXPERTS)
    start = jnp.cumsum(counts) - counts
    padded = (counts + MOE_BLOCK - 1) // MOE_BLOCK * MOE_BLOCK
    pend = jnp.cumsum(padded)
    dest = (pend - padded)[s_exp] + jnp.arange(n_assign) - start[s_exp]
    n_blocks = -(-n_assign // MOE_BLOCK) + N_EXPERTS
    n_rows = n_blocks * MOE_BLOCK
    row_tok = jnp.zeros((n_rows,), jnp.int32).at[dest].set(s_tok)
    row_w = jnp.zeros((n_rows,), f32).at[dest].set(s_w)
    block_exp = jnp.minimum(jnp.searchsorted(pend, jnp.arange(n_blocks) * MOE_BLOCK, side='right'), N_EXPERTS - 1)

    def expert_block(args):
        tok, w, e = args
        xb = xf[tok]
        hid = jax.nn.silu(xb @ e_gate[e]) * (xb @ e_up[e])
        return (hid @ e_down[e]) * w[:, None].astype(xb.dtype)

    y = lax.map(expert_block, (row_tok.reshape(n_blocks, MOE_BLOCK), row_w.reshape(n_blocks, MOE_BLOCK), block_exp))
    out = jnp.zeros_like(xf).at[row_tok].add(y.reshape(n_rows, D))
    return out.reshape(B, S, D)

def setup_inputs(seed: int = 0) -> dict:
    key = jax.random.key(seed)
    ks = iter(jax.random.split(key, 40))
    f32 = jnp.float32
    L = DEPTH
    nrm = lambda shape, scale: jax.random.normal(next(ks), shape, f32) * scale
    gain = lambda shape: 1.0 + nrm(shape, 0.02)
    return {
        'x': nrm((BATCH, SEQ, D_MODEL), 1.0),
        'c': nrm((BATCH, D_MODEL), 1.0),
        'ada_w': nrm((L, D_MODEL, 6 * D_MODEL), ADA_INIT * D_MODEL ** -0.5),
        'ada_b': nrm((L, 6 * D_MODEL), 0.01),
        'norm1_g': gain((L, D_MODEL)),
        'w_in': nrm((L, D_MODEL, IN_COLS), D_MODEL ** -0.5),
        'shift_mu': jax.random.uniform(next(ks), (L, RWKV_COLS), f32),
        'w0': jax.random.uniform(next(ks), (L, RWKV_WIDTH), f32, minval=-6.0, maxval=0.0),
        'w_decay_up': nrm((L, DECAY_LORA, RWKV_WIDTH), 0.5 * DECAY_LORA ** -0.5),
        'a0': nrm((L, RWKV_WIDTH), 0.1),
        'w_aaa_up': nrm((L, AAA_LORA, RWKV_WIDTH), AAA_LORA ** -0.5),
        'w_gate_up': nrm((L, GATE_LORA, RWKV_WIDTH), GATE_LORA ** -0.5),
        'k_k': 0.85 + nrm((L, RWKV_WIDTH), 0.02),
        'k_a': gain((L, RWKV_WIDTH)),
        'r_k': nrm((L, RWKV_HEADS, HEAD_DIM), 0.1),
        'gn_g': gain((L, RWKV_WIDTH)),
        'gn_b': nrm((L, RWKV_WIDTH), 0.01),
        'kv_norm_g': gain((L, KV_LATENT)),
        'k_idx_norm_g': gain((L, IDX_DIM)),
        'w_uk': nrm((L, KV_LATENT, DSA_HEADS, HEAD_DIM), KV_LATENT ** -0.5),
        'w_uv': nrm((L, KV_LATENT, DSA_HEADS, HEAD_DIM), KV_LATENT ** -0.5),
        'w_out': nrm((L, MIX_WIDTH, D_MODEL), MIX_WIDTH ** -0.5),
        'norm2_g': gain((L, D_MODEL)),
        'w_group': nrm((L, D_MODEL, N_GROUPS), D_MODEL ** -0.5),
        'b_group': nrm((L, N_GROUPS), 0.01),
        'w_expert': nrm((L, D_MODEL, N_EXPERTS), D_MODEL ** -0.5),
        'b_expert': nrm((L, N_EXPERTS), 0.01),
        'e_gate': nrm((L, N_EXPERTS, D_MODEL, D_EXPERT), D_MODEL ** -0.5),
        'e_up': nrm((L, N_EXPERTS, D_MODEL, D_EXPERT), D_MODEL ** -0.5),
        'e_down': nrm((L, N_EXPERTS, D_EXPERT, D_MODEL), D_EXPERT ** -0.5),
        'final_ada_w': nrm((D_MODEL, 2 * D_MODEL), ADA_INIT * D_MODEL ** -0.5),
        'final_ada_b': nrm((2 * D_MODEL,), 0.01),
        'final_norm_g': gain((D_MODEL,)),
    }

def reference(x, c, ada_w, ada_b, norm1_g, w_in, shift_mu, w0, w_decay_up, a0, w_aaa_up, w_gate_up,
              k_k, k_a, r_k, gn_g, gn_b, kv_norm_g, k_idx_norm_g, w_uk, w_uv, w_out, norm2_g,
              w_group, b_group, w_expert, b_expert, e_gate, e_up, e_down,
              final_ada_w, final_ada_b, final_norm_g):
    c_act = jax.nn.silu(c)
    for l in range(DEPTH):
        shift1, scale1, gate1, shift2, scale2, gate2 = jnp.split(c_act @ ada_w[l] + ada_b[l], 6, axis=-1)
        h = modulate(rms_norm(x, norm1_g[l]), shift1, scale1)
        proj = h @ w_in[l]
        y_rwkv = rwkv7_time_mix(proj[..., :RWKV_COLS], shift_mu[l], w0[l], w_decay_up[l], a0[l],
                                w_aaa_up[l], w_gate_up[l], k_k[l], k_a[l], r_k[l], gn_g[l], gn_b[l])
        q, ckv, q_idx, k_idx, w_idx = split_cols(proj[..., RWKV_COLS:], DSA_SPLITS)
        y_dsa = dsa_mix(q, ckv, q_idx, k_idx, w_idx, kv_norm_g[l], k_idx_norm_g[l], w_uk[l], w_uv[l])
        mixed = jnp.concatenate([y_rwkv, y_dsa], axis=-1) @ w_out[l]
        x = x + (1 + gate1[:, None, :]) * mixed
        h = modulate(rms_norm(x, norm2_g[l]), shift2, scale2)
        x = x + (1 + gate2[:, None, :]) * hierarchical_moe(h, w_group[l], b_group[l], w_expert[l], b_expert[l],
                                                           e_gate[l], e_up[l], e_down[l])
    shift_f, scale_f = jnp.split(c_act @ final_ada_w + final_ada_b, 2, axis=-1)
    return modulate(rms_norm(x, final_norm_g), shift_f, scale_f)


_drawn_inputs = setup_inputs


def setup_inputs(seed=0):
    import zlib

    import numpy as np

    out = dict(_drawn_inputs(seed))
    spreads = {}
    factors = {'gn_b': 21.764,
     'kv_norm_g': 3.214,
     'k_idx_norm_g': 3.303,
     'b_group': 14.647,
     'b_expert': 13.986,
     'final_ada_b': 4.407,
     'final_norm_g': 22.523,
     'w_decay_up': 3.216,
     'a0': 3.523,
     'k_k': 3.79,
     'k_a': 3.984,
     'gn_g': 11.808,
     'norm2_g': 3.363}
    for name, (base, spread) in spreads.items():
        noise = np.random.default_rng([zlib.crc32(name.encode()), seed]).standard_normal(out[name].shape)
        drawn = base * np.exp(spread * noise) if base else spread * noise
        out[name] = jnp.asarray(drawn.astype(out[name].dtype))
    for name, factor in factors.items():
        out[name] = (out[name] * factor).astype(out[name].dtype)
    return out
```

```python
from contextlib import ExitStack

import numpy as np

import concourse.bass as bass
from concourse import mybir

F32 = mybir.dt.float32
I32 = mybir.dt.int32
BF16 = mybir.dt.bfloat16
ALU = mybir.AluOpType
ACT = mybir.ActivationFunctionType
AX_X = mybir.AxisListType.X

P = 128
SEQ = 1024
D = 1024
KD = D // P
NT = SEQ // P
CHUNK = 64
HEAD = 64
NH = 8
NPAIR = NH // 2
RW = 512
LATENT = 128
IDX_HEADS = 4
TOPK = 256
NG = 4
EPG = 8
NE = NG * EPG
DE = 512
KE = DE // P
NRW = 14
NCT = 20
LEVELS = 6
MANTISSA = 23
SEARCH = (6, 3, 3, 5, 6)
BLK = 128
MAX_BLOCKS = NE + 2 * SEQ // BLK
ROWS = (MAX_BLOCKS + 1) * BLK
NORM_EPS = 1e-6
GN_EPS = HEAD * 1e-5
DECAY = float(np.exp(-0.5))
MASKED = -float(2.0 ** 127)
INADMISSIBLE = -1.0e38
BEYOND = 3.0e38
NEG = -1.0e30
W_GROUPS = [(2304, 452, (18, 19)), (1792, 512, (14, 15, 16, 17)), (1536, 256, (12, 13)),
            (1024, 512, (8, 9, 10, 11)), (512, 512, (4, 5, 6, 7)), (0, 512, (0, 1, 2, 3))]
NROW = LATENT + CHUNK + IDX_HEADS


class Arena:

    def __init__(self, tensor, size):
        self.tensor, self.size, self.at = tensor, size, 0

    def take(self, *shape):
        n = int(np.prod(shape))
        assert self.at + n <= self.size, (self.at, n, self.size)
        piece = self.tensor[:, self.at:self.at + n]
        self.at += n
        if len(shape) == 1:
            return piece
        names = "abcd"[:len(shape)]
        return piece.rearrange(f"p ({' '.join(names)}) -> p {' '.join(names)}", **dict(zip(names, shape)))


class Signals:

    def __init__(self, numbers=None):
        self.numbers, self.seen, self.count, self.sems = numbers, {}, {}, {}

    def phase(self, nc, scope, name):
        self.nc, self.name, self.sems = nc, name, {}
        scope.callback(self.end)

    def end(self):
        self.nc.clear_and_free_semaphores(list(self.sems.values()))
        self.nc.all_engine_barrier()

    def sem(self, name):
        if name not in self.sems:
            self.sems[name] = self.nc.alloc_semaphore(f"{self.name}_{name}")
        return self.sems[name]

    def sig(self, name, *key, by=1):
        k = (self.name, name)
        self.count[k] = self.count.get(k, 0) + by
        assert (self.name, name, *key) not in self.seen, (name, key)
        self.seen[(self.name, name, *key)] = self.count[k]
        return self.sem(name), by

    def at(self, name, *key):
        return self.sem(name), self.numbers[(self.name, name, *key)] if self.numbers else 1


def sparse_attention_moe_layer(nc, x, c, ada_w, ada_b, norm1_g, w_in, shift_mu, w0, w_decay_up, a0, w_aaa_up,
                               w_gate_up, k_k, k_a, r_k, gn_g, gn_b, kv_norm_g, k_idx_norm_g, w_uk, w_uv, w_out,
                               norm2_g, w_group, b_group, w_expert, b_expert, e_gate, e_up, e_down,
                               final_ada_w, final_ada_b, final_norm_g, out, S, phases=5):
    with ExitStack() as ctx:
        def sb(name, shape, dt=F32):
            return ctx.enter_context(nc.sbuf_tensor(name, shape, dt))

        def dram(name, shape, dt=F32):
            return nc.dram_tensor(name, shape, dt, kind="Internal").ap()

        sig, at = S.sig, S.at

        def link(eng, ins, name, *key):
            sem, by = sig(name, *(key or (("step", S.count.get((S.name, name), 0)),)))
            ins.then_inc(sem, by)
            eng.wait_ge(sem, S.count[(S.name, name)])

        readers = {}

        def fill(pe, bank, *reader):
            if (S.name, bank) in readers:
                pe.wait_ge(*at(*readers[(S.name, bank)]))
            readers[(S.name, bank)] = reader

        psum = {}
        for pair in ("P", "T", "X", "W"):
            both = ctx.enter_context(nc.psum_tensor(f"ps{pair}", [P, 1024], F32))
            psum[pair], psum[pair + "0"], psum[pair + "1"] = both[:, :], both[:, 0:512], both[:, 512:1024]

        p_d = dram("proj_T", (NCT, P, SEQ))
        mod_d = dram("mod_rows", (4, D))
        mix_d = dram("mix_T", (KD, P, SEQ))
        x1_d = dram("x1_rows", (SEQ, D))
        xn2_d = dram("xn2_rows", (SEQ, D))
        y_d = dram("expert_rows", (ROWS, D))
        table_d = dram("row_token", (ROWS, 1))

        wdec, waaa, wgate, wuv = (sb(n, [P, RW]) for n in ("wdec", "waaa", "wgate", "wuv"))
        wukT = sb("wukT", [P, NPAIR, P])
        wrt = sb("wrt", [P, KD, NG + NE])
        ident = sb("ident", [P, P])
        m_lvl = sb("m_lvl", [P, LEVELS, P], BF16)
        m_pair = sb("m_pair", [P, 2, P])
        m_low = sb("m_low", [P, P])
        m_bd = sb("m_bd", [P, P])
        blk2 = sb("blk2", [P, 2])
        scan_reset = sb("scan_reset", [P, RW], BF16)
        ones = sb("ones", [P, P])
        before = sb("before", [P, P])
        causal = sb("causal", [P, 256])
        iota8 = sb("iota8", [P, EPG])
        halves = sb("halves", [P, MANTISSA])
        steps = sb("steps", [P, 7])
        token_id = sb("token_id", [P, NT], I32)
        mhalf = sb("mhalf", [P, 16])
        cols = sb("cols", [P, 50])
        c_mu, c_w0, c_a0, c_kk, c_ka, c_rk = (cols[:, a:b] for a, b in ((0, 14), (14, 18), (18, 22), (22, 26), (26, 30), (30, 34)))
        c_g1, c_g2 = cols[:, 34:42], cols[:, 42:50]
        r_gng, r_gnb = sb("r_gng", [P, RW]), sb("r_gnb", [P, RW])
        r_kvg = sb("r_kvg", [P, LATENT + CHUNK])
        r_brt = sb("r_brt", [P, NG + NE])
        mod_cols = sb("mod_cols", [P, 4, KD])
        rowp = sb("rowp", [P, NT, NROW])
        ckv_all = sb("ckv_all", [P, NT, LATENT])
        ckvT, kiT = sb("ckvT", [P, SEQ]), sb("kiT", [P, SEQ])
        Z = sb("Z", [P, 2, NPAIR, P])


        wgt = sb("wgt", [P, NT, 2])
        dest = sb("dest", [P, NT, 2], I32)
        first_block = sb("first_block", [P, NE + 2], I32)
        idx_all = sb("idx_all", [P, MAX_BLOCKS + 1], I32)
        st = sb("st", [P, 96])
        ARENA = 41260
        arena_t = sb("arena", [P, ARENA])

        def g4(ap):
            return ap.rearrange("p (a b) -> p a b", a=4)

        def g8(ap):
            return ap.rearrange("p (a b) -> p a b", a=8)

        def over(ap, n):
            return ap.unsqueeze(2).to_broadcast([ap.shape[0], ap.shape[1], n])

        def each(ap, a):
            return ap.unsqueeze(1).to_broadcast([ap.shape[0], a, ap.shape[1]])

        with ExitStack() as scope:
            S.phase(nc, scope, "project")
            A = Arena(arena_t, ARENA)
            slots = [A.take(KD, 512) for _ in range(4)]
            hT = A.take(KD, SEQ)
            xin = A.take(4, D)
            mrow = A.take(2, D)
            stage = A.take(4, 512)
            cB = A.take(KD, P)
            cT = A.take(4, KD)
            bias = A.take(2, 512)
            junk = A.take(D)
            wuk_sb = A.take(RW)
            gain_f = A.take(D)
            ki_twice = A.take(NT, P)
            kv_sum, kv_var, kv_rs = A.take(2, NT), A.take(2 * NT), A.take(2 * NT)
            stream = [("ada", n) for n in range(4)] + [("win", g) for g in range(6)] + [("ada", n) for n in range(4, 16)]
            place = {name: i for i, name in enumerate(stream)}
            outs = [(g, ct, half) for g, (_, _, tiles) in enumerate(W_GROUPS) for ct in tiles for half in range(2)]
            out_bank = ["P0", "P1", "X0", "X1"]

            def last_use(kind, n):
                if kind == "ada":
                    return at("ada_done", n)
                return at("rows_done", NT - 1) if n == 0 else at("projected", max(i for i, o in enumerate(outs) if o[0] == n))

            def ada_source(n):
                if n < 12:
                    return ada_w[0, :, 512 * n:512 * n + 512], ada_b[:, 512 * n:512 * n + 512]
                m = 512 * (n - 12)
                return final_ada_w[:, m:m + 512], final_ada_b.rearrange("(a n) -> a n", a=1)[:, m:m + 512]

            block = scope.enter_context(nc.Block())

            @block.sync
            def _(sp):
                sp.dma_start(cT[:, 0, :], c.rearrange("a (k p) -> (a p) k", p=P), allow_slow_non_contiguous=True).then_inc(*sig("c_loaded", 0, by=16))
                for i, (kind, n) in enumerate(stream):
                    if kind == "win":
                        col, width, _ = W_GROUPS[n]
                        src = w_in[0, :, col:col + width]
                    else:
                        width = 512
                        src, bias_src = ada_source(n)
                        if n >= 2:
                            sp.wait_ge(*at("row_half", n - 2))
                        sp.dma_start(bias[:, n % 2, :], bias_src.to_broadcast([P, 512])).then_inc(*sig(f"bias_loaded{n % 2}", n, by=16))
                    if i >= 4:
                        sp.wait_ge(*last_use(*stream[i - 4]))
                    sp.dma_start(slots[i % 4][:, :, 0:width], src.rearrange("(k p) n -> p k n", p=P))\
                        .then_inc(*sig(f"slot_loaded{i % 4}", i, by=16))
                    if i == 1:
                        for t in range(4):
                            sp.dma_start(xin[:, t, :], x[0, P * t:P * t + P, :]).then_inc(*sig(f"x_loaded{t % 4}", t, by=16))
                    if i == 5:
                        sp.wait_ge(*at("x_turned_bank", 0, KD - 1))
                        for t in range(4, 8):
                            sp.dma_start(xin[:, t - 4, :], x[0, P * t:P * t + P, :]).then_inc(*sig(f"x_loaded{t % 4}", t, by=16))

            @block.gpsimd
            def _(pool):
                def step(ins):
                    link(pool, ins, "const_step")

                def keep(ap, pattern, base, mult, op=ALU.is_ge, fill_=0.0):
                    step(pool.affine_select(out=ap, in_=ap, compare_op=op, fill=fill_, base=base, pattern=pattern,
                                            channel_multiplier=mult))

                for i, (dst, v) in enumerate(((c_g1, norm1_g), (c_mu, shift_mu), (c_w0, w0), (c_a0, a0), (c_kk, k_k), (c_ka, k_a),
                               (c_rk, r_k.rearrange("a h d -> a (h d)")), (c_g2, norm2_g))):
                    pool.dma_start(dst, v.rearrange("a (k p) -> (a p) k", p=P), allow_slow_non_contiguous=True)\
                        .then_inc(*sig("cols_loaded", i, by=16))
                small = [(wuk_sb, w_uk[0].rearrange("c h d -> c (h d)")),
                         (gain_f, final_norm_g.rearrange("(a n) -> a n", a=1).to_broadcast([P, D])),
                         (wdec[0:64, :], w_decay_up[0]), (waaa[64:128, :], w_aaa_up[0]), (wgate[:, :], w_gate_up[0]),
                         (wuv[:, :], w_uv[0].rearrange("c h d -> c (h d)")),
                         (wrt[:, :, 0:NG], w_group[0].rearrange("(k p) n -> p k n", p=P)),
                         (wrt[:, :, NG:], w_expert[0].rearrange("(k p) n -> p k n", p=P)),
                         (r_gng[:, :], gn_g.to_broadcast([P, RW])), (r_gnb[:, :], gn_b.to_broadcast([P, RW])),
                         (r_kvg[:, 0:LATENT], kv_norm_g.to_broadcast([P, LATENT])),
                         (r_kvg[:, LATENT:], k_idx_norm_g.to_broadcast([P, CHUNK])),
                         (r_brt[:, 0:NG], b_group.to_broadcast([P, NG])), (r_brt[:, NG:], b_expert.to_broadcast([P, NE]))]
                for i, (dst, src) in enumerate(small):
                    pool.dma_start(dst, src).then_inc(*sig("small_loaded", i, by=16))
                step(pool.memset(mhalf[:, :], -0.5))
                step(pool.memset(ident[:, :], 0.0))
                keep(ident[:, :], [[-1, P]], 0, 1, ALU.not_equal, 1.0)
                link(pool, pool.memset(ones[:, :], 1.0), "ident_ready", 0)
                step(pool.memset(wdec[64:128, :], 0.0))
                step(pool.memset(waaa[0:64, :], 0.0))
                for ap in (before[:, :], m_bd[:, :], blk2[:, :], scan_reset[:, :], m_low[:, :], m_pair[:, :, :], m_lvl[:, :, :]):
                    step(pool.memset(ap, 1.0))
                step(pool.memset(causal[:, :], 0.0))
                keep(m_bd[:, 0:64], [[0, 64]], 63, -1)
                keep(m_bd[:, 64:128], [[0, 64]], -64, 1)
                keep(blk2[:, 0:1], [[0, 1]], 63, -1)
                keep(blk2[:, 1:2], [[0, 1]], -64, 1)
                keep(before[:, :], [[1, P]], -1, -1)
                keep(m_pair[:, 0, :], [[1, P]], -1, -1)
                keep(m_pair[:, 1, :], [[1, P]], 0, -1)
                for i in range(2):
                    keep(m_pair[:, i, 64:128], [[0, 64]], -64, 1)
                keep(m_low[:, :], [[-1, P]], -1, 1)
                keep(m_low[:, 0:64], [[0, 64]], 63, -1)
                for l in range(LEVELS):
                    n = 2 ** l
                    v = m_lvl[:, l, :].rearrange("p (b h i) -> p b h i", h=2, i=n)
                    step(pool.memset(v[:, :, 0, :], 0.0))
                    keep(v[:, :, 1, :], [[-2 * n, P // (2 * n)], [0, n]], 0, 1)
                    keep(v[:, :, 1, :], [[2 * n, P // (2 * n)], [0, n]], n - 1, -1)
                step(pool.memset(scan_reset[:, :].rearrange("p (a b) -> p a b", b=CHUNK)[:, :, 0:1], 0.0))
                step(pool.memset(causal[0:64, 192:256], NEG))
                step(pool.iota(token_id[:, :], pattern=[[P, NT]], base=0, channel_multiplier=1))
                for i in range(EPG):
                    step(pool.memset(iota8[:, i:i + 1], float(EPG - i)))
                for i in range(MANTISSA):
                    step(pool.memset(halves[:, i:i + 1], -float(2.0 ** -(i + 1))))
                for i in range(7):
                    step(pool.memset(steps[:, i:i + 1], float(BLK * (i + 1))))
                step(pool.memset(Z[:, :, :, :], 0.0))
                for t in range(NT):
                    pool.wait_ge(*at("x_var", t))
                    pool.tensor_tensor(st[:, 16 + t:17 + t], st[:, 8 + t:9 + t], mhalf[:, 0:1], ALU.pow).then_inc(*sig("x_rstd", t))
                pool.wait_ge(*at("kv_var", 0))
                link(pool, pool.tensor_tensor(kv_rs, kv_var, mhalf[:, 0:2 * NT], ALU.pow), "kv_rs", 0)
                for i, (g, ct, half) in enumerate(outs):
                    pool.wait_ge(*at("staged", i))
                    pool.dma_start(p_d[ct, :, 512 * half:512 * half + 512], stage[:, i % 4, :]).then_inc(*sig(f"stored{i % 4}", i, by=16))
                for i, v in enumerate((2, 5, 6, 7)):
                    pool.wait_ge(*at("mod_row", v))
                    pool.dma_start(mod_d[i:i + 1, :], mrow[0:1, v % 2, :]).then_inc(*sig("row_stored", v, by=16))
                    pool.wait_ge(*at("row_stored", v))
                for i in range(len(outs) - 4, len(outs)):
                    pool.wait_ge(*at(f"stored{i % 4}", i))
                pool.wait_ge(*at("small_loaded", len(small) - 1))

            @block.scalar
            def _(act):
                act.wait_ge(*at("c_loaded", 0))
                act.activation(cT[:, 1, :], cT[:, 0, :], ACT.Exp, scale=-1.0).then_inc(*sig("c_exp", 0))

                for half in range(2):
                    for t in range(4 * half, 4 * half + 4):
                        act.wait_ge(*at(f"x_loaded{t % 4}", t))
                        link(act, act.activation(junk, xin[:, t % 4, :], ACT.Square, accum_out=st[:, t:t + 1]), "x_squares", t)
                    act.wait_ge(*at("mod_cols", 1))
                    for k in range(KD):
                        act.wait_ge(*at("x_turned_bank", half, k))
                        act.activation(hT[:, k, 512 * half:512 * half + 512], psum[f"T{k % 2}"], ACT.Identity,
                                       bias=mod_cols[:, 0, k:k + 1], scale=mod_cols[:, 1, k:k + 1]).then_inc(*sig("h_ready", half, k))
                for t in range(NT):
                    act.wait_ge(*at("rows_ready", t))
                    link(act, act.activation(junk[:, 0:LATENT], rowp[:, t, 0:LATENT], ACT.Square, accum_out=kv_sum[:, 0, t:t + 1]), "kv_sq", t, 0)
                    link(act, act.activation(junk[:, 0:CHUNK], rowp[:, t, LATENT:LATENT + CHUNK], ACT.Square, accum_out=kv_sum[:, 1, t:t + 1]), "kv_sq", t, 1)
                for i, (g, ct, half) in enumerate(outs):
                    act.wait_ge(*at("projected", i))
                    if i >= 4:
                        act.wait_ge(*at(f"stored{i % 4}", i - 4))
                    act.activation(stage[:, i % 4, :], psum[out_bank[i % 4]], ACT.Copy).then_inc(*sig("staged", i))

            @block.vector
            def _(dve):
                def step(ins):
                    link(dve, ins, "dve_step")

                dve.wait_ge(*at("c_exp", 0))
                step(dve.tensor_scalar(cT[:, 2, :], cT[:, 1, :], 1.0, None, ALU.add))
                step(dve.reciprocal(cT[:, 3, :], cT[:, 2, :]))
                step(dve.tensor_tensor(cT[:, 1, :], cT[:, 0, :], cT[:, 3, :], ALU.mult))
                link(dve, dve.tensor_copy(cB, over(cT[:, 1, :], P)), "c_ready", 0)

                def modulation(n):
                    v = n // 2
                    dve.wait_ge(*at("ada_done", n))
                    dve.wait_ge(*at(f"bias_loaded{n % 2}", n))
                    if n % 2 == 0 and v >= 2:
                        if v - 2 in (0, 1, 3, 4):
                            dve.wait_ge(*at("cols_turned", v - 2))
                        else:
                            dve.wait_ge(*at("row_stored", v - 2))
                    piece = mrow[:, v % 2, 512 * (n % 2):512 * (n % 2) + 512]
                    link(dve, dve.tensor_tensor(piece, psum[f"W{n % 2}"], bias[:, n % 2, :], ALU.add), "row_half", n)
                    if n % 2 == 0:
                        return
                    if v in (0, 1, 3, 4):
                        link(dve, dve.tensor_copy(st[:, 95:96], mrow[:, v % 2, 0:1]), "mod_row", v)
                        dve.wait_ge(*at("cols_turned", v))
                        turned = psum["T0"].rearrange("p (k j) -> p k j", j=32)[:, 0:KD, 0]
                        i = (0, 1, None, 2, 3)[v]
                        if i % 2 == 0:
                            link(dve, dve.tensor_copy(mod_cols[:, i, :], turned), "mod_cols", v)
                        else:
                            dve.wait_ge(*at("small_loaded", 13))
                            step(dve.tensor_scalar(mod_cols[:, i, :], turned, 1.0, None, ALU.add))
                            dve.wait_ge(*at("cols_loaded", 7))
                            link(dve, dve.tensor_tensor(mod_cols[:, i, :], mod_cols[:, i, :], c_g1 if v == 1 else c_g2, ALU.mult), "mod_cols", v)
                    elif v in (2, 5):
                        link(dve, dve.tensor_scalar(mrow[:, v % 2, :], mrow[:, v % 2, :], 1.0, None, ALU.add), "mod_row", v)
                    elif v == 6:
                        link(dve, dve.tensor_copy(st[:, 95:96], mrow[:, v % 2, 0:1]), "mod_row", v)
                    else:
                        step(dve.tensor_scalar(mrow[:, v % 2, :], mrow[:, v % 2, :], 1.0, None, ALU.add))
                        dve.wait_ge(*at("small_loaded", 13))
                        link(dve, dve.tensor_tensor(mrow[:, v % 2, :], mrow[:, v % 2, :], gain_f, ALU.mult), "mod_row", v)

                def wuk_turned():
                    dve.wait_ge(*at("wuk_turned", 0))
                    link(dve, dve.tensor_copy(wukT[:, :, :], g4(psum["X0"])), "wuk_ready", 0)

                for n in range(4):
                    modulation(n)
                wuk_turned()
                for half in range(2):
                    for t in range(4 * half, 4 * half + 4):
                        dve.wait_ge(*at("x_squares", t))
                        link(dve, dve.tensor_scalar(st[:, 8 + t:9 + t], st[:, t:t + 1], 1.0 / D, NORM_EPS, ALU.mult, ALU.add), "x_var", t)
                        dve.wait_ge(*at("x_rstd", t))
                        link(dve, dve.tensor_scalar(xin[:, t % 4, :], xin[:, t % 4, :], st[:, 16 + t:17 + t], None, ALU.mult), "xn_ready", t)
                for t in range(NT):
                    dve.wait_ge(*at("rows_done", t))
                    link(dve, dve.tensor_copy(rowp[:, t, :], psum[f"T{t % 2}"][:, 0:NROW]), "rows_ready", t)
                dve.wait_ge(*at("kv_sq", NT - 1, 1))
                step(dve.tensor_scalar(kv_var[:, 0:NT], kv_sum[:, 0, :], 1.0 / LATENT, NORM_EPS, ALU.mult, ALU.add))
                link(dve, dve.tensor_scalar(kv_var[:, NT:], kv_sum[:, 1, :], 1.0 / CHUNK, NORM_EPS, ALU.mult, ALU.add), "kv_var", 0)
                dve.wait_ge(*at("kv_rs", 0))
                for t in range(NT):
                    step(dve.scalar_tensor_tensor(out=ckv_all[:, t, :], in0=rowp[:, t, 0:LATENT], scalar=kv_rs[:, t:t + 1],
                                                  in1=r_kvg[:, 0:LATENT], op0=ALU.mult, op1=ALU.mult))
                    for j in range(2):
                        link(dve, dve.scalar_tensor_tensor(out=ki_twice[:, t, CHUNK * j:CHUNK * j + CHUNK], in0=rowp[:, t, LATENT:LATENT + CHUNK],
                                                           scalar=kv_rs[:, NT + t:NT + t + 1], in1=r_kvg[:, LATENT:], op0=ALU.mult, op1=ALU.mult), "kv_norm", t, j)
                for i in range(4):
                    dve.wait_ge(*at("kv_turned", i))
                    link(dve, dve.tensor_copy((ckvT, kiT)[i // 2][:, 512 * (i % 2):512 * (i % 2) + 512], psum[f"T{i % 2}"]), "kv_T", i)
                for n in range(4, 16):
                    modulation(n)

            @block.tensor
            def _(pe):
                def ada(n):
                    i = place[("ada", n)]
                    pe.wait_ge(*at(f"slot_loaded{i % 4}", i))
                    fill(pe, f"W{n % 2}", "row_half", n)
                    for k in range(KD):
                        mm = pe.matmul(psum[f"W{n % 2}"], cB[:, k, :], slots[i % 4][:, k, :], start=(k == 0), stop=(k == KD - 1))
                    mm.then_inc(*sig("ada_done", n))
                    v = n // 2
                    if n % 2 == 1 and v in (0, 1, 3, 4):
                        pe.wait_ge(*at("mod_row", v))
                        fill(pe, "T0", "mod_cols", v)
                        for k in range(KD):
                            mm = pe.transpose(psum["T0"][:, 32 * k:32 * k + 32], mrow[0:32, v % 2, P * k:P * k + P], ident[0:32, 0:32])
                        mm.then_inc(*sig("cols_turned", v))

                pe.wait_ge(*at("c_ready", 0))
                pe.wait_ge(*at("ident_ready", 0))
                for n in range(4):
                    ada(n)
                pe.wait_ge(*at("small_loaded", 13))
                fill(pe, "X0", "wuk_ready", 0)
                for p in range(NPAIR):
                    mm = pe.transpose(psum["X0"][:, P * p:P * p + P], wuk_sb[:, P * p:P * p + P], ident[:, :])
                mm.then_inc(*sig("wuk_turned", 0))
                for half in range(2):
                    for t in range(4 * half, 4 * half + 4):
                        pe.wait_ge(*at("xn_ready", t))
                    for k in range(KD):
                        fill(pe, f"T{k % 2}", "h_ready", half, k)
                        for j in range(4):
                            mm = pe.transpose(psum[f"T{k % 2}"][:, P * j:P * j + P], xin[:, j, P * k:P * k + P], ident[:, :])
                        mm.then_inc(*sig("x_turned_bank", half, k))
                i = 0
                for g, (col, width, tiles) in enumerate(W_GROUPS):
                    slot_n = place[("win", g)]
                    w = slots[slot_n % 4]
                    pe.wait_ge(*at(f"slot_loaded{slot_n % 4}", slot_n))
                    for n, ct in enumerate(tiles):
                        first = P * n + (LATENT if g == 0 else 0)
                        for half in range(2):
                            pe.wait_ge(*at("h_ready", half, KD - 1))
                            b = out_bank[i % 4]
                            fill(pe, b, "staged", i)
                            for k in range(KD):
                                mm = pe.matmul(psum[b], w[:, k, first:first + P], hT[:, k, 512 * half:512 * half + 512],
                                               start=(k == 0), stop=(k == KD - 1))
                            mm.then_inc(*sig("projected", i))
                            i += 1
                    if g == 0:
                        for t in range(NT):
                            b = f"T{t % 2}"
                            fill(pe, b, "rows_ready", t)
                            for k in range(KD):
                                pe.matmul(psum[b][:, 0:LATENT], hT[:, k, P * t:P * t + P], w[:, k, 0:LATENT],
                                          start=(k == 0), stop=(k == KD - 1))
                            for k in range(KD):
                                mm = pe.matmul(psum[b][:, LATENT:NROW], hT[:, k, P * t:P * t + P], w[:, k, LATENT + 256:452],
                                               start=(k == 0), stop=(k == KD - 1))
                            mm.then_inc(*sig("rows_done", t))
                pe.wait_ge(*at("kv_norm", NT - 1, 1))
                for i in range(4):
                    fill(pe, f"T{i % 2}", "kv_T", i)
                    for t in range(4 * (i % 2), 4 * (i % 2) + 4):
                        mm = pe.transpose(g4(psum[f"T{i % 2}"])[:, t % 4, :], (ckv_all, ki_twice)[i // 2][:, t, :], ident[:, :])
                    mm.then_inc(*sig("kv_turned", i))
                for n in range(4, 16):
                    ada(n)
        if phases == 1:
            return

        with ExitStack() as scope:
            S.phase(nc, scope, "mix")
            A = Arena(arena_t, ARENA)
            raw = A.take(NRW, P + 1)
            pm = A.take(NRW, P)
            qiBD, qBD = A.take(2, 2, P), A.take(NPAIR, 2, P)
            lo, gsig, grow = A.take(P), A.take(P), A.take(RW)
            sgd, cum, invE, av, kkr, kmod, rnb = (A.take(RW) for _ in range(7))
            dx = A.take(NH, CHUNK + 1)
            natA, natR, natB, natK = (A.take(NPAIR, P) for _ in range(4))
            ARbd, Bbd = A.take(NPAIR, 2, 2, P), A.take(NPAIR, 2, P)
            R, V0 = A.take(NH, P), A.take(NH, P)
            Bc, Kc = A.take(NPAIR, 2, P), A.take(NPAIR, 2, P)
            AbT, AkT = A.take(NH, 2, P), A.take(NH, 2, P)
            AA, T, Tt, Xs = (A.take(NH, P) for _ in range(4))
            W = A.take(2, NH, CHUNK)
            G1, Y0, GT = A.take(RW), A.take(RW), A.take(NPAIR, P)
            yb, yc = A.take(RW), A.take(RW)
            mixT, qlT, olT = A.take(KD, P), A.take(NH, P), A.take(NH, P)
            score, keyed = A.take(SEQ), A.take(SEQ)
            smask, junk = (A.take(SEQ // 2).bitcast(BF16) for _ in range(2))
            lg = A.take(2, SEQ)
            PT = A.take(NT, 2, P)
            s_sum, s_dec, s_neg, s_sgn, s_lim, s_lim_e, s_q, s_v, s_need = (A.take(1) for _ in range(9))
            s_step = st[:, 0:MANTISSA]
            exp_i = A.take(2).bitcast(I32)
            keyed_i = keyed.bitcast(I32)
            hats = Xs.rearrange("p a b -> p (a b)")
            hatB, hatK = hats[:, 0:RW], hats[:, RW:2 * RW]
            late = AbT.rearrange("p a b c -> p (a b c)")
            MT = late[:, 0:1024].rearrange("p (a b c) -> p a b c", a=NPAIR, b=2)
            Cs = late[:, 1024:2048].rearrange("p (a b c) -> p a b c", a=NPAIR, b=2)
            s_mx, s_gn, s_kk = st[:, 40:48], st[:, 48:72], st[:, 72:88]
            s_bon = (st[:, 24:32], st[:, 32:40])
            tile = lambda t: slice(P * t, P * t + P)
            block = scope.enter_context(nc.Block())

            def pt_bank(t, h, j):
                return f"T{(h * (t // 4 + 1) + j) % 2}"

            @block.sync
            def _(sp):
                def load_rwkv(t):
                    if t:
                        sp.wait_ge(*at("mixed", t - 1))
                    first = P * t - 1 if t else 0
                    sp.dma_start(raw[:, :, (0 if t else 1):P + 1], p_d[0:NRW, :, first:P * t + P].rearrange("c p s -> p c s"))\
                        .then_inc(*sig("raw_loaded", t, by=16))
                    if t >= 2:
                        if t > 2:
                            sp.wait_ge(*at("idx_done", t - 1, IDX_HEADS - 1))
                        else:
                            sp.wait_ge(*at("bd_zero", 0))
                        for h in range(2):
                            half = slice(64 * h, 64 * h + 64)
                            sp.dma_start(qiBD[half, :, h, :], p_d[18:20, half, tile(t)].rearrange("c p s -> p c s")).then_inc(*sig("qi_loaded", t, h, by=16))

                def load_queries(t):
                    if t:
                        sp.wait_ge(*at("qlat_done", t - 1, 1))
                    else:
                        sp.wait_ge(*at("bd_zero", 0))
                    for h in range(2):
                        half = slice(64 * h, 64 * h + 64)
                        sp.dma_start(qBD[half, :, h, :], p_d[14:18, half, tile(t)].rearrange("c p s -> p c s")).then_inc(*sig("q_loaded", t, h, by=16))

                load_rwkv(0)
                load_queries(0)
                for t in range(NT + 1):
                    if t + 1 < NT:
                        load_rwkv(t + 1)
                    if 1 <= t < NT:
                        load_queries(t)
                    if t < NT:
                        sp.wait_ge(*at("mix_rwkv", t))
                        sp.dma_start(mix_d[0:4, :, tile(t)].rearrange("c p s -> p c s"), mixT[:, 0:4, :]).then_inc(*sig("rwkv_stored", t, by=16))
                    if t:
                        sp.wait_ge(*at("mix_dsa", t - 1))
                        sp.dma_start(mix_d[4:8, :, tile(t - 1)].rearrange("c p s -> p c s"), mixT[:, 4:8, :]).then_inc(*sig("dsa_stored", t - 1, by=16))
                sp.wait_ge(*at("rwkv_stored", NT - 1))
                sp.wait_ge(*at("dsa_stored", NT - 1))

            @block.gpsimd
            def _(pool):
                def step(ins):
                    link(pool, ins, "pool_step")

                def power(dst, src, n, name, *key):
                    link(pool, pool.tensor_tensor(dst, src, mhalf[:, 0:n], ALU.pow), name, *key)

                for ap in (qiBD, ARbd, Bbd, V0, Bc, Kc):
                    step(pool.memset(ap, 0.0))
                step(pool.memset(dx, 1.0))
                step(pool.memset(raw[:, :, 0:1], 0.0))
                link(pool, pool.memset(qBD, 0.0), "bd_zero", 0)
                def prepare(t):
                    pool.wait_ge(*at("mixed", t))
                    if t:
                        pool.wait_ge(*at("nat_b", t - 1))
                    link(pool, pool.tensor_tensor(g4(kkr), pm[:, 4:8, :], over(c_kk, P), ALU.mult), "kkr", t)
                    pool.wait_ge(*at("kk_var", t))
                    power(s_kk[:, 8:16], s_kk[:, 0:8], 8, "kk_rs", t)

                prepare(0)
                for t in range(NT):
                    pool.wait_ge(*at("nat_b", t))
                    for h in range(2):
                        half = slice(64 * h, 64 * h + 64)
                        link(pool, pool.tensor_copy(Bbd[half, :, h, :], natB[half, :, :]), "b_bd", t, h)
                    if t + 1 < NT:
                        prepare(t + 1)
                    pool.wait_ge(*at("y_var", t))
                    power(s_gn[:, 16:24], s_gn[:, 8:16], 8, "y_rs", t)

            @block.scalar
            def _(act):
                def step(ins):
                    link(act, ins, "act_step")

                def search(t):
                    n = P * (t + 1)

                    def weigh(src, scale, limit, more, step_scale=None):
                        step(act.activation(junk[:, 0:n], src[:, 0:n], ACT.Sign, scale=scale, bias=s_neg, accum_out=s_sum))
                        step(act.activation(s_dec, s_sum, ACT.Sign, bias=limit))
                        if more:
                            step(act.activation(s_neg, s_dec, ACT.Identity, scale=step_scale, bias=s_neg))

                    act.wait_ge(*at("score_ready", t))
                    link(act, act.activation(junk[:, 0:n], score[:, 0:n], ACT.Sign, accum_out=s_sum), "sign_sum", t)
                    yield
                    act.wait_ge(*at("exponents", t))
                    for k in range(7, -1, -1):
                        weigh(keyed_i, 1.0, s_lim_e, k > 0, -float(2.0 ** (k - 1)))
                        if k == 0:
                            link(act, act.activation(s_sum, s_dec, ACT.Copy), "exponent_found", t)
                        yield
                    act.wait_ge(*at("mantissa", t))
                    for k in range(1, MANTISSA + 1):
                        weigh(score, s_sgn, s_lim, k < MANTISSA, s_step[:, k:k + 1] if k < MANTISSA else None)
                        if k == MANTISSA:
                            link(act, act.activation(s_sum, s_dec, ACT.Copy), "searched", t)
                        yield

                def attention(t):
                    n = P * (t + 1)
                    for g in range(2):
                        act.wait_ge(*at("qlat_done", t, g))
                        link(act, act.activation(qlT[:, 4 * g:4 * g + 4, :], g4(psum[f"X{g}"]), ACT.Copy, scale=HEAD ** -0.5), "qlat", t, g)
                    yield
                    for h in range(NH + 2):
                        if h < NH:
                            act.wait_ge(*at("logits", t, h))
                            link(act, act.activation(lg[:, h % 2, 0:n], lg[:, h % 2, 0:n], ACT.Exp, bias=s_mx[:, 2 * (h % 2) + 1:2 * (h % 2) + 2],
                                                     accum_out=s_mx[:, 4 + h % 2:5 + h % 2]), "exps", t, h)
                        if h >= 3 and h % 2:
                            act.wait_ge(*at("pv_done", t, h - 3))
                            link(act, act.activation(olT[:, h - 3:h - 1, :], g4(psum["P0"])[:, 0:2, :], ACT.Copy), "o_lat", t, h - 3)
                        if 1 <= h <= NH:
                            for j in range(t // 4 + 1):
                                m = min(4, t + 1 - 4 * j)
                                act.wait_ge(*at("pt_turned", t, h - 1, j))
                                link(act, act.activation(PT[:, 4 * j:4 * j + m, (h - 1) % 2, :], g4(psum[pt_bank(t, h - 1, j)])[:, 0:m, :], ACT.Copy), "probs_T", t, h - 1, j)
                        yield
                    act.wait_ge(*at("uv_done", t))
                    if t:
                        act.wait_ge(*at("dsa_stored", t - 1))
                    link(act, act.activation(mixT[:, 4:8, :], g4(psum["T1"]), ACT.Copy), "mix_dsa", t)

                def prepare(t):
                    act.wait_ge(*at("mixed", t))
                    step(act.activation(lo[0:64, :], pm[0:64, 12, :], ACT.Tanh))
                    step(act.activation(lo[64:128, :], pm[64:128, 12, :], ACT.Copy))
                    link(act, act.activation(gsig, pm[:, 13, :], ACT.Tanh, scale=0.5), "lora_in", t)
                    act.wait_ge(*at("kkr", t))
                    link(act, act.activation(rnb, kkr, ACT.Square), "kk_sq", t)
                    yield
                    act.wait_ge(*at("zdec_done", t))
                    for p in range(NPAIR):
                        link(act, act.activation(g4(sgd)[:, p, :], g4(psum["X0"])[:, p, :], ACT.Tanh, scale=0.5, bias=c_w0[:, p:p + 1]), "dec_tanh", t, p)
                    act.wait_ge(*at("zaaa_done", t))
                    for p in range(NPAIR):
                        link(act, act.activation(g4(av)[:, p, :], g4(psum["X1"])[:, p, :], ACT.Tanh, scale=0.5, bias=c_a0[:, p:p + 1]), "aaa_tanh", t, p)
                    yield

                def decays(t):
                    act.wait_ge(*at("cum", t))
                    if t:
                        act.wait_ge(*at("y_var", t - 1))
                    step(act.activation(dx[:, :, 1:CHUNK + 1], cum.rearrange("p (a b) -> p a b", b=CHUNK), ACT.Exp, scale=-DECAY))
                    link(act, act.activation(invE, cum, ACT.Exp, scale=DECAY), "decays", t)

                for _ in prepare(0):
                    pass
                decays(0)
                for t in range(NT):
                    n = P * (t + 1)
                    turns = attention(t - 1) if t else iter(())
                    ahead = prepare(t + 1) if t + 1 < NT else iter(())
                    act.wait_ge(*at("nat_r", t))
                    for h in range(2):
                        half = slice(64 * h, 64 * h + 64)
                        link(act, act.activation(ARbd[half, :, h, 0, :], natA[half, :, :], ACT.Copy), "ar_bd", t, h, 0)
                        link(act, act.activation(ARbd[half, :, h, 1, :], natR[half, :, :], ACT.Copy), "ar_bd", t, h, 1)
                    if t >= 2:
                        for h in range(IDX_HEADS):
                            act.wait_ge(*at("idx_done", t, h))
                            if h >= 2:
                                act.wait_ge(*at("scored", t, h - 2))
                            else:
                                act.wait_ge(*at("pt_turned", t - 2, 6 + h, (t - 2) // 4))
                            link(act, act.activation(lg[:, h % 2, 0:n], psum["XW"[h % 2]][:, 0:n], ACT.Relu), "relu", t, h)
                    next(turns, None)
                    seek = search(t) if t >= 2 else iter(())

                    def some(count):
                        for _ in range(count):
                            next(seek, None)

                    some(1)
                    act.wait_ge(*at("g_done", t))
                    if t:
                        act.wait_ge(*at("y_out", t - 1))
                    link(act, act.activation(grow, psum["W0"], ACT.Copy), "g_rows", t)
                    next(turns, None)
                    act.wait_ge(*at("v_turned", t))
                    link(act, act.activation(V0[:, :, CHUNK:], g8(psum["T0"]), ACT.Copy), "v_rows", t)
                    act.wait_ge(*at("a_turned", t))
                    link(act, act.activation(R[:, :, 0:CHUNK], g8(psum["T1"]), ACT.Copy), "a_rows", t)
                    act.wait_ge(*at("b_turned", t))
                    for h in range(2):
                        half = slice(64 * h, 64 * h + 64)
                        link(act, act.activation(Bc[half, :, h, :], g4(psum["T0"])[half], ACT.Copy), "b_rows", t, h)
                    act.wait_ge(*at("k_turned", t))
                    for h in range(2):
                        half = slice(64 * h, 64 * h + 64)
                        link(act, act.activation(Kc[half, :, h, :], g4(psum["T1"])[half], ACT.Copy), "k_rows", t, h)
                    next(turns, None)
                    some(8)
                    for l in range(LEVELS - 1):
                        next(turns, None)
                        for g in range(2):
                            act.wait_ge(*at("t_turned", t, l, g))
                            link(act, act.activation(T[:, 4 * g:4 * g + 4, :], g4(psum[f"T{g}"]), ACT.Copy), "t_inv", t, l, g)
                        if l == 0:
                            for g in range(2):
                                act.wait_ge(*at("av_done", t, g))
                                link(act, act.activation(R[:, 4 * g:4 * g + 4, CHUNK:], g4(psum[f"W{g}"])[:, :, CHUNK:], ACT.Copy), "av_rows", t, g)
                        some(SEARCH[l])
                        if l in (1, 2):
                            next(ahead, None)
                    next(turns, None)
                    for g in range(2):
                        act.wait_ge(*at("w_done", t, g))
                        link(act, act.activation(W[:, :, 4 * g:4 * g + 4, :].rearrange("p w h i -> p h w i"),
                                                 psum[f"X{g}"].rearrange("p (h w i) -> p h w i", h=4, w=2), ACT.Copy), "w_rows", t, g)
                    for g in range(2):
                        act.wait_ge(*at("y0_done", t, g))
                        src = psum[f"W{g}"].rearrange("p (h w i) -> p h w i", h=4, w=2)
                        step(act.activation(g8(G1)[:, 4 * g:4 * g + 4, :], src[:, :, 0, :], ACT.Copy))
                        link(act, act.activation(g8(Y0)[:, 4 * g:4 * g + 4, :], src[:, :, 1, :], ACT.Copy), "y0_rows", t, g)
                    next(turns, None)
                    next(turns, None)
                    act.wait_ge(*at("y_centred", t))
                    link(act, act.activation(invE, yc, ACT.Square), "y_sq", t)
                    if t + 1 < NT:
                        decays(t + 1)
                    act.wait_ge(*at("y_turned", t))
                    if t:
                        act.wait_ge(*at("rwkv_stored", t - 1))
                    link(act, act.activation(mixT[:, 0:4, :], g4(psum["T0"]), ACT.Copy), "mix_rwkv", t)
                    next(turns, None)
                for _ in attention(NT - 1):
                    pass

            @block.vector
            def _(dve):
                def step(ins):
                    link(dve, ins, "dve_step")

                def top_k(t):
                    n = P * (t + 1)
                    odds = float(n - 2 * TOPK)
                    dve.wait_ge(*at("sign_sum", t))
                    step(dve.tensor_scalar(s_sgn, s_sum, -(odds + 1.5), 2.0, ALU.is_gt, ALU.mult))
                    step(dve.tensor_scalar(s_sgn, s_sgn, -1.0, None, ALU.add))
                    step(dve.tensor_scalar(s_lim, s_sgn, odds + 1.5, None, ALU.mult))
                    step(dve.tensor_scalar(s_lim_e, s_sgn, odds + 1.0, None, ALU.mult))
                    step(dve.memset(s_neg, -127.5))
                    step(dve.tensor_scalar(keyed[:, 0:n], score[:, 0:n], s_sgn, 0.0, ALU.mult, ALU.max))
                    link(dve, dve.tensor_scalar(keyed_i[:, 0:n], keyed_i[:, 0:n], 23, None, ALU.logical_shift_right), "exponents", t)
                    yield
                    dve.wait_ge(*at("exponent_found", t))
                    step(dve.scalar_tensor_tensor(out=s_q, in0=s_sum, scalar=0.5, in1=s_neg, op0=ALU.mult, op1=ALU.subtract))
                    step(dve.tensor_copy(exp_i[:, 0:1], s_q))
                    step(dve.tensor_scalar(exp_i[:, 1:2], exp_i[:, 0:1], 23, None, ALU.logical_shift_left))
                    q = exp_i[:, 1:2].bitcast(F32)
                    step(dve.tensor_scalar(s_step, halves[:, :], q, None, ALU.mult))
                    link(dve, dve.tensor_tensor(s_neg, s_step[:, 0:1], q, ALU.subtract), "mantissa", t)
                    yield
                    dve.wait_ge(*at("searched", t))
                    step(dve.tensor_scalar(s_q, s_sum, -1.0, -0.5, ALU.add, ALU.mult))
                    step(dve.scalar_tensor_tensor(out=s_v, in0=s_q, scalar=s_step[:, MANTISSA - 1:], in1=s_neg, op0=ALU.mult, op1=ALU.subtract))
                    step(dve.tensor_scalar(keyed[:, 0:n], score[:, 0:n], s_sgn, None, ALU.mult))
                    step(dve.tensor_scalar(smask[:, 0:n], keyed[:, 0:n], s_v, BEYOND, ALU.is_lt, ALU.mult))
                    step(dve.tensor_tensor_reduce(keyed[:, 0:n], keyed[:, 0:n], smask[:, 0:n], 1.0, BEYOND, ALU.add, ALU.min, s_q))
                    step(dve.tensor_tensor(s_v, s_q, s_sgn, ALU.mult))
                    step(dve.tensor_scalar(keyed[:, 0:n], score[:, 0:n], s_v, None, ALU.is_gt))
                    step(dve.tensor_reduce(s_q, keyed[:, 0:n], AX_X, ALU.add))
                    step(dve.tensor_scalar(s_need, s_q, -1.0, float(TOPK), ALU.mult, ALU.add))
                    step(dve.tensor_scalar(smask[:, 0:n], score[:, 0:n], s_v, None, ALU.is_equal))
                    step(dve.tensor_tensor_scan(score[:, 0:n], ones[:, 0:1].to_broadcast([P, n]), smask[:, 0:n], 0.0, ALU.mult, ALU.add))
                    step(dve.scalar_tensor_tensor(out=smask[:, 0:n], in0=score[:, 0:n], scalar=s_need, in1=smask[:, 0:n], op0=ALU.is_le, op1=ALU.mult))
                    step(dve.tensor_tensor(keyed[:, 0:n], keyed[:, 0:n], smask[:, 0:n], ALU.add))
                    link(dve, dve.tensor_scalar(smask[:, 0:n], keyed[:, 0:n], 0.0, NEG, ALU.is_equal, ALU.mult), "selected", t)

                def attention(t):
                    n = P * (t + 1)
                    mask = smask[:, 0:n] if t >= 2 else causal[:, 256 - n:256]
                    for h in range(NH + 1):
                        if h < NH:
                            mx, nmx = s_mx[:, 2 * (h % 2):2 * (h % 2) + 1], s_mx[:, 2 * (h % 2) + 1:2 * (h % 2) + 2]
                            if h >= 2:
                                dve.wait_ge(*at("pt_turned", t, h - 2, t // 4))
                            elif t:
                                dve.wait_ge(*at("pt_turned", t - 1, 6 + h, (t - 1) // 4))
                            dve.wait_ge(*at("lg_done", t, h))
                            link(dve, dve.tensor_tensor_reduce(lg[:, h % 2, 0:n], psum["P"][:, 0:n], mask, 1.0, MASKED, ALU.add, ALU.max, mx), "lg_masked", t, h)
                            link(dve, dve.tensor_scalar(nmx, mx, -1.0, None, ALU.mult), "logits", t, h)
                        if h:
                            b = (h - 1) % 2
                            sm, rs = s_mx[:, 4 + b:5 + b], s_mx[:, 6 + b:7 + b]
                            dve.wait_ge(*at("exps", t, h - 1))
                            step(dve.reciprocal(rs, sm))
                            link(dve, dve.tensor_scalar(lg[:, b, 0:n], lg[:, b, 0:n], rs, None, ALU.mult), "probs", t, h - 1)
                        yield

                step(dve.tensor_scalar(cols[:, 14:22], cols[:, 14:22], 0.5, None, ALU.mult))
                def prepare(t):
                    dve.wait_ge(*at("raw_loaded", t))
                    if t == 0:
                        dve.wait_ge(*at("bd_zero", 0))
                    step(dve.tensor_tensor(pm, raw[:, :, 0:P], raw[:, :, 1:P + 1], ALU.subtract))
                    for c_ in range(NRW):
                        ins = dve.scalar_tensor_tensor(out=pm[:, c_, :], in0=pm[:, c_, :], scalar=c_mu[:, c_:c_ + 1],
                                                       in1=raw[:, c_, 1:P + 1], op0=ALU.mult, op1=ALU.add)
                        if c_ < NRW - 1:
                            step(ins)
                        else:
                            link(dve, ins, "mixed", t)
                    yield
                    dve.wait_ge(*at("lora_in", t))
                    link(dve, dve.tensor_scalar(gsig, gsig, 0.5, 0.5, ALU.mult, ALU.add), "g_sig", t)
                    dve.wait_ge(*at("kk_ss", t))
                    link(dve, dve.tensor_scalar(s_kk[:, 0:8], psum["W1"][:, 0:8], 1e-24, None, ALU.max), "kk_var", t)
                    yield
                    dve.wait_ge(*at("dec_tanh", t, NPAIR - 1))
                    step(dve.tensor_scalar(sgd, sgd, 0.5, 0.5, ALU.mult, ALU.add))
                    link(dve, dve.tensor_tensor_scan(cum, scan_reset[:, :], sgd, 0.0, ALU.mult, ALU.add), "cum", t)
                    dve.wait_ge(*at("aaa_tanh", t, NPAIR - 1))
                    step(dve.tensor_scalar(av, av, 0.5, 0.5, ALU.mult, ALU.add))
                    step(dve.scalar_tensor_tensor(out=g4(kmod), in0=g4(av), scalar=-1.0, in1=over(c_ka, P), op0=ALU.add, op1=ALU.mult))
                    step(dve.scalar_tensor_tensor(out=g4(kmod), in0=g4(kmod), scalar=1.0, in1=pm[:, 4:8, :], op0=ALU.add, op1=ALU.mult))
                    dve.wait_ge(*at("kk_rs", t))
                    link(dve, dve.tensor_copy(g8(rnb), over(s_kk[:, 8:16], HEAD)), "kk_rs_wide", t)
                    step(dve.tensor_tensor(g4(sgd), pm[:, 0:4, :], g4(kmod), ALU.mult))
                    link(dve, dve.tensor_tensor(g4(sgd), g4(sgd), over(c_rk, P), ALU.mult), "bonus", t)
                    yield
                    dve.wait_ge(*at("kk_spread", t))
                    link(dve, dve.tensor_tensor(kkr, kkr, psum["T1"], ALU.mult), "kk", t)
                    dve.wait_ge(*at("bonus_done", t))
                    link(dve, dve.tensor_copy(s_bon[t % 2], psum["W1"][:, 0:8]), "bonus_rows", t)
                    yield

                for _ in prepare(0):
                    pass
                pending = iter(())
                for t in range(NT):
                    n = P * (t + 1)
                    turns = attention(t - 1) if t else iter(())
                    ahead = prepare(t + 1) if t + 1 < NT else iter(())
                    dve.wait_ge(*at("decays", t))
                    E = dx.rearrange("p (a c) i -> p a c i", a=NPAIR)
                    by_chunk = lambda ap: ap.rearrange("p a (c i) -> p a c i", c=2)
                    by8 = lambda ap: ap.rearrange("p a (c i) -> p (a c) i", c=2)
                    step(dve.scalar_tensor_tensor(out=by8(natA), in0=by8(g4(kkr)), scalar=-1.0, in1=dx[:, :, 0:CHUNK], op0=ALU.mult, op1=ALU.mult))
                    link(dve, dve.tensor_tensor(by8(natR), by8(pm[:, 0:4, :]), dx[:, :, 1:], ALU.mult), "nat_r", t)
                    step(dve.tensor_tensor(kkr, kkr, av, ALU.mult))
                    link(dve, dve.tensor_tensor(natB, g4(kkr), g4(invE), ALU.mult), "nat_b", t)
                    link(dve, dve.tensor_tensor(natK, g4(kmod), g4(invE), ALU.mult), "nat_k", t)
                    whole = dx[:, :, CHUNK:CHUNK + 1].to_broadcast([P, NH, CHUNK])
                    link(dve, dve.tensor_tensor(g8(hatB), by8(natB), whole, ALU.mult), "hat_b", t)
                    link(dve, dve.tensor_tensor(g8(hatK), by8(natK), whole, ALU.mult), "hat_k", t)
                    pending = iter(())
                    if t >= 2:
                        step(dve.tensor_scalar(s_gn[:, 0:4], rowp[:, t, LATENT + CHUNK:NROW], 1.0 / 16, None, ALU.mult))
                        for h in range(IDX_HEADS):
                            dve.wait_ge(*at("relu", t, h))
                            if h == 0:
                                ins = dve.tensor_scalar(score[:, 0:n], lg[:, 0, 0:n], s_gn[:, 0:1], None, ALU.mult)
                            else:
                                ins = dve.scalar_tensor_tensor(out=score[:, 0:n], in0=lg[:, h % 2, 0:n], scalar=s_gn[:, h:h + 1],
                                                               in1=score[:, 0:n], op0=ALU.mult, op1=ALU.add)
                            link(dve, ins, "scored", t, h)
                        link(dve, dve.memset(score[0:CHUNK, n - CHUNK:n], INADMISSIBLE), "score_ready", t)
                        pending = top_k(t)

                    next(turns, None)
                    next(turns, None)
                    next(pending, None)
                    for p in range(NPAIR):
                        masks = m_pair[:, :, :].unsqueeze(1).to_broadcast([P, 2, 2, P])
                        for done, dst, ready, b in (("ab_done", AbT, "ab", "X0"), ("ak_done", AkT, "ak", "X1")):
                            dve.wait_ge(*at(done, t, p))
                            link(dve, dve.tensor_tensor(dst[:, 2 * p:2 * p + 2, :, :], psum[b].rearrange("p (h a t) -> p h a t", h=2, a=2), masks, ALU.mult), ready, t, p)
                        if p % 2:
                            dve.wait_ge(*at("aa_done", t, p))
                            link(dve, dve.tensor_tensor(AA[:, 2 * p - 2:2 * p + 2, :], g4(psum[f"W{p // 2}"]), each(m_low[:, :], 4), ALU.mult), "aa", t, p // 2)
                    next(turns, None)
                    next(pending, None)
                    step(dve.tensor_tensor(Tt, AbT[:, :, 0, :], each(m_lvl[:, 0, :], NH), ALU.mult))
                    link(dve, dve.tensor_tensor(Tt, Tt, each(ident[:, :], NH), ALU.add), "tt", t, 0, 1)
                    for l in range(1, LEVELS):
                        for g in range(2):
                            dve.wait_ge(*at("x_done", t, l, g))
                            link(dve, dve.tensor_tensor(Xs[:, 4 * g:4 * g + 4, :], g4(psum[f"X{g}"]), each(m_lvl[:, l, :], 4), ALU.mult), "xs", t, l, g)
                        next(turns, None)
                        for g in range(2):
                            dve.wait_ge(*at("txa_done", t, l, g))
                            link(dve, dve.tensor_tensor(Tt[:, 4 * g:4 * g + 4, :], Tt[:, 4 * g:4 * g + 4, :], g4(psum[f"W{g}"]), ALU.add), "tt", t, l, g)
                        next(ahead, None)
                    next(pending, None)
                    dve.wait_ge(*at("g_turned", t))
                    link(dve, dve.tensor_tensor(GT, g4(psum["T0"]), natR, ALU.add), "gt", t)
                    next(turns, None)
                    for g in range(2):
                        dve.wait_ge(*at("m_done", t, g))
                        link(dve, dve.tensor_tensor(MT[:, 2 * g:2 * g + 2].rearrange("p a c j -> p (a c) j"), g4(psum[f"X{g}"]), each(m_bd[:, :], 4), ALU.mult), "m_bd", t, g)
                    for i in range(2 * NPAIR):
                        m_i = MT[:, i // 2, i % 2, :]
                        ins = dve.scalar_tensor_tensor(out=m_i, in0=ident[:, :], scalar=dx[:, i, CHUNK:CHUNK + 1], in1=m_i, op0=ALU.mult, op1=ALU.add)
                    link(dve, ins, "m", t)
                    for g in range(2):
                        dve.wait_ge(*at("c_done", t, g))
                        link(dve, dve.tensor_tensor(Cs[:, 2 * g:2 * g + 2].rearrange("p a c j -> p (a c) j"), g4(psum[f"W{g}"]), each(m_bd[:, :], 4), ALU.mult), "c", t, g)
                    for c_ in range(2):
                        dve.wait_ge(*at("z_done", t, c_))
                        link(dve, dve.tensor_tensor(Z[:, 1 - c_, :, :], g4(psum["X0"]), Cs[:, :, c_, :], ALU.add), "z", t, c_)
                    dve.wait_ge(*at("y_done", t))
                    dve.wait_ge(*at("y0_rows", t, 1))
                    link(dve, dve.tensor_tensor(yb, psum["P1"], Y0, ALU.add), "y", t)
                    step(dve.tensor_reduce(s_gn[:, 0:8], g8(yb), AX_X, ALU.add))
                    step(dve.tensor_scalar(s_gn[:, 0:8], s_gn[:, 0:8], 1.0 / HEAD, None, ALU.mult))
                    link(dve, dve.tensor_tensor(g8(yc), g8(yb), over(s_gn[:, 0:8], HEAD), ALU.subtract), "y_centred", t)
                    dve.wait_ge(*at("y_sq", t))
                    step(dve.tensor_reduce(s_gn[:, 0:8], g8(invE), AX_X, ALU.add))
                    link(dve, dve.tensor_scalar(s_gn[:, 8:16], s_gn[:, 0:8], 1.0 / HEAD, GN_EPS, ALU.mult, ALU.add), "y_var", t)
                    dve.wait_ge(*at("y_rs", t))
                    step(dve.tensor_tensor(g8(yc), g8(yc), over(s_gn[:, 16:24], HEAD), ALU.mult))
                    step(dve.tensor_tensor(yc, yc, r_gng[:, :], ALU.mult))
                    step(dve.tensor_tensor(yc, yc, r_gnb[:, :], ALU.add))
                    step(dve.tensor_tensor(g8(yb), V0[:, :, CHUNK:], over(s_bon[t % 2], HEAD), ALU.mult))
                    step(dve.tensor_tensor(yc, yc, yb, ALU.add))
                    link(dve, dve.tensor_tensor(yc, yc, grow, ALU.mult), "y_out", t)
                for _ in attention(NT - 1):
                    pass

            @block.tensor
            def _(pe):
                def attention(t):
                    n = P * (t + 1)

                    def logits(h):
                        pe.wait_ge(*at("qlat", t, h // 4))
                        for half in range(t // 4 + 1):
                            m = min(512, n - 512 * half)
                            fill(pe, f"P{half}", "lg_masked", t, h)
                            mm = pe.matmul(psum[f"P{half}"][:, 0:m], qlT[:, h, :], ckvT[:, 512 * half:512 * half + m], start=True, stop=True)
                        mm.then_inc(*sig("lg_done", t, h))

                    for h in range(2):
                        pe.wait_ge(*at("q_loaded", t, h))
                    for g in range(2):
                        fill(pe, f"X{g}", "qlat", t, g)
                        for p in range(2 * g, 2 * g + 2):
                            mm = pe.matmul(psum[f"X{g}"][:, 256 * (p % 2):256 * (p % 2) + 256], wukT[:, p, :], qBD[:, p].rearrange("p h t -> p (h t)"), start=True, stop=True)
                        mm.then_inc(*sig("qlat_done", t, g))
                    logits(0)
                    yield
                    for h in range(NH + 2):
                        if h >= 3 and h % 2:
                            pe.wait_ge(*at("probs_T", t, h - 2, t // 4))
                            fill(pe, "P0", "o_lat", t, h - 3)
                            for kt in range(t + 1):
                                mm = pe.matmul(psum["P0"][:, 0:2 * P], ckv_all[:, kt, :], PT[:, kt, :, :].rearrange("p h t -> p (h t)"), start=(kt == 0), stop=(kt == t))
                            mm.then_inc(*sig("pv_done", t, h - 3))
                        if 1 <= h <= NH:
                            pe.wait_ge(*at("probs", t, h - 1))
                            for j in range(t // 4 + 1):
                                b = pt_bank(t, h - 1, j)
                                fill(pe, b, "probs_T", t, h - 1, j)
                                for kt in range(4 * j, min(4 * j + 4, t + 1)):
                                    mm = pe.transpose(g4(psum[b])[:, kt % 4, :], lg[:, (h - 1) % 2, tile(kt)], ident[:, :])
                                mm.then_inc(*sig("pt_turned", t, h - 1, j))
                        if h + 1 < NH:
                            logits(h + 1)
                        yield
                    pe.wait_ge(*at("o_lat", t, NH - 2))
                    fill(pe, "T1", "mix_dsa", t)
                    for h in range(NH):
                        mm = pe.matmul(g4(psum["T1"])[64 * (h % 2):64 * (h % 2) + 64, h // 2, :], wuv[:, HEAD * h:HEAD * h + HEAD], olT[:, h, :], start=True, stop=True)
                    mm.then_inc(*sig("uv_done", t))

                def prepare(t):
                    pe.wait_ge(*at("lora_in", t))
                    fill(pe, "X0", "dec_tanh", t, NPAIR - 1)
                    for p in range(NPAIR):
                        mm = pe.matmul(g4(psum["X0"])[:, p, :], wdec[:, P * p:P * p + P], lo, start=True, stop=True)
                    mm.then_inc(*sig("zdec_done", t))
                    fill(pe, "X1", "aaa_tanh", t, NPAIR - 1)
                    for p in range(NPAIR):
                        mm = pe.matmul(g4(psum["X1"])[:, p, :], waaa[:, P * p:P * p + P], lo, start=True, stop=True)
                    mm.then_inc(*sig("zaaa_done", t))
                    pe.wait_ge(*at("kk_sq", t))
                    fill(pe, "W1", "kk_var", t)
                    for p in range(NPAIR):
                        mm = pe.matmul(psum["W1"][:, 2 * p:2 * p + 2], g4(rnb)[:, p, :], blk2[:, :], start=True, stop=True)
                    mm.then_inc(*sig("kk_ss", t))
                    yield
                    pe.wait_ge(*at("kk_rs_wide", t))
                    fill(pe, "T1", "kk", t)
                    for p in range(NPAIR):
                        mm = pe.matmul(g4(psum["T1"])[:, p, :], g4(rnb)[:, p, :], ident[:, :], start=True, stop=True)
                    mm.then_inc(*sig("kk_spread", t))
                    pe.wait_ge(*at("bonus", t))
                    fill(pe, "W1", "bonus_rows", t)
                    for p in range(NPAIR):
                        mm = pe.matmul(psum["W1"][:, 2 * p:2 * p + 2], g4(sgd)[:, p, :], blk2[:, :], start=True, stop=True)
                    mm.then_inc(*sig("bonus_done", t))
                    yield

                for _ in prepare(0):
                    pass
                for t in range(NT):
                    n = P * (t + 1)
                    turns = attention(t - 1) if t else iter(())
                    ahead = prepare(t + 1) if t + 1 < NT else iter(())
                    if t >= 2:
                        for h in range(2):
                            pe.wait_ge(*at("qi_loaded", t, h))
                        for h in range(IDX_HEADS):
                            pair = "XW"[h % 2]
                            for half in range(t // 4 + 1):
                                fill(pe, f"{pair}{half}", "relu", t, h)
                                m = min(512, n - 512 * half)
                                mm = pe.matmul(psum[f"{pair}{half}"][:, 0:m], qiBD[:, h // 2, h % 2, :], kiT[:, 512 * half:512 * half + m], start=True, stop=True)
                            mm.then_inc(*sig("idx_done", t, h))
                    next(turns, None)
                    pe.wait_ge(*at("g_sig", t))
                    fill(pe, "W0", "g_rows", t)
                    pe.matmul(psum["W0"], gsig, wgate[:, :], start=True, stop=True).then_inc(*sig("g_done", t))
                    fill(pe, "T0", "v_rows", t)
                    for p in range(NPAIR):
                        mm = pe.transpose(g4(psum["T0"])[:, p, :], pm[:, 8 + p, :], ident[:, :])
                    mm.then_inc(*sig("v_turned", t))
                    next(turns, None)
                    pe.wait_ge(*at("nat_r", t))
                    fill(pe, "T1", "a_rows", t)
                    for p in range(NPAIR):
                        mm = pe.transpose(g4(psum["T1"])[:, p, :], natA[:, p, :], ident[:, :])
                    mm.then_inc(*sig("a_turned", t))
                    pe.wait_ge(*at("hat_b", t))
                    fill(pe, "T0", "b_rows", t, 1)
                    for p in range(NPAIR):
                        mm = pe.transpose(g4(psum["T0"])[:, p, :], g4(hatB)[:, p, :], ident[:, :])
                    mm.then_inc(*sig("b_turned", t))
                    pe.wait_ge(*at("hat_k", t))
                    fill(pe, "T1", "k_rows", t, 1)
                    for p in range(NPAIR):
                        mm = pe.transpose(g4(psum["T1"])[:, p, :], g4(hatK)[:, p, :], ident[:, :])
                    mm.then_inc(*sig("k_turned", t))
                    next(turns, None)
                    pe.wait_ge(*at("ar_bd", t, 1, 1))
                    pe.wait_ge(*at("b_bd", t, 1))
                    for p in range(NPAIR):
                        both = ARbd[:, p].rearrange("p h a t -> p (h a t)")
                        fill(pe, "X0", "ab", t, p)
                        pe.matmul(psum["X0"], natB[:, p, :], both, start=True, stop=True).then_inc(*sig("ab_done", t, p))
                        fill(pe, "X1", "ak", t, p)
                        pe.matmul(psum["X1"], natK[:, p, :], both, start=True, stop=True).then_inc(*sig("ak_done", t, p))
                        if p % 2 == 0:
                            fill(pe, f"W{p // 2}", "aa", t, p // 2)
                        pe.matmul(psum[f"W{p // 2}"][:, 256 * (p % 2):256 * (p % 2) + 256], natA[:, p, :], Bbd[:, p].rearrange("p h t -> p (h t)"),
                                  start=True, stop=True).then_inc(*sig("aa_done", t, p))
                    pe.wait_ge(*at("v_rows", t))
                    for g in range(2):
                        pe.wait_ge(*at("ak", t, 2 * g + 1))
                        fill(pe, f"W{g}", "av_rows", t, g)
                        for h in range(4 * g, 4 * g + 4):
                            mm = pe.matmul(g4(psum[f"W{g}"])[:, h % 4, :], AkT[:, h, 0, :], V0[:, h, :], start=True, stop=True)
                        mm.then_inc(*sig("av_done", t, g))
                    next(turns, None)

                    def turn_inverse(l):
                        for g in range(2):
                            pe.wait_ge(*at("tt", t, l, g if l else 1))
                            fill(pe, f"T{g}", "t_inv", t, l, g)
                            for h in range(4 * g, 4 * g + 4):
                                mm = pe.transpose(g4(psum[f"T{g}"])[:, h % 4, :], Tt[:, h, :], ident[:, :])
                            mm.then_inc(*sig("t_turned", t, l, g))

                    turn_inverse(0)
                    for l in range(1, LEVELS):
                        for g in range(2):
                            pe.wait_ge(*at("tt", t, l - 1, g if l > 1 else 1))
                            pe.wait_ge(*at("aa", t, g))
                            fill(pe, f"X{g}", "xs", t, l, g)
                            for h in range(4 * g, 4 * g + 4):
                                mm = pe.matmul(g4(psum[f"X{g}"])[:, h % 4, :], AA[:, h, :], Tt[:, h, :], start=True, stop=True)
                            mm.then_inc(*sig("x_done", t, l, g))
                        for g in range(2):
                            pe.wait_ge(*at("xs", t, l, g))
                            pe.wait_ge(*at("t_inv", t, l - 1, g))
                            fill(pe, f"W{g}", "tt", t, l, g)
                            for h in range(4 * g, 4 * g + 4):
                                mm = pe.matmul(g4(psum[f"W{g}"])[:, h % 4, :], T[:, h, :], Xs[:, h, :], start=True, stop=True)
                            mm.then_inc(*sig("txa_done", t, l, g))
                        next(turns, None)
                        if l < LEVELS - 1:
                            turn_inverse(l)
                        if l in (2, 4):
                            next(ahead, None)
                    for g in range(2):
                        pe.wait_ge(*at("tt", t, LEVELS - 1, g))
                        pe.wait_ge(*at("a_rows", t))
                        pe.wait_ge(*at("av_rows", t, g))
                        fill(pe, f"X{g}", "w_rows", t, g)
                        for h in range(4 * g, 4 * g + 4):
                            mm = pe.matmul(g4(psum[f"X{g}"])[:, h % 4, :], Tt[:, h, :], R[:, h, :], start=True, stop=True)
                        mm.then_inc(*sig("w_done", t, g))
                    for g in range(2):
                        pe.wait_ge(*at("w_rows", t, g))
                        fill(pe, f"W{g}", "y0_rows", t, g)
                        for h in range(4 * g, 4 * g + 4):
                            o = g4(psum[f"W{g}"])[:, h % 4, :]
                            pe.matmul(o, AbT[:, h, 1, :], W[:, :, h, :], start=True, stop=False)
                            mm = pe.matmul(o, AkT[:, h, 1, :], V0[:, h, :], start=False, stop=True)
                        mm.then_inc(*sig("y0_done", t, g))
                    pe.wait_ge(*at("b_rows", t, 1))
                    for g in range(2):
                        fill(pe, f"X{g}", "m_bd", t, g)
                        for p in range(2 * g, 2 * g + 2):
                            mm = pe.matmul(psum[f"X{g}"][:, 256 * (p % 2):256 * (p % 2) + 256], W[:, 0, 2 * p:2 * p + 2, :].rearrange("p h j -> p (h j)"),
                                           Bc[:, p].rearrange("p c j -> p (c j)"), start=True, stop=True)
                        mm.then_inc(*sig("m_done", t, g))
                    pe.wait_ge(*at("y0_rows", t, 1))
                    fill(pe, "T0", "gt", t)
                    for p in range(NPAIR):
                        mm = pe.transpose(g4(psum["T0"])[:, p, :], g4(G1)[:, p, :], ident[:, :])
                    mm.then_inc(*sig("g_turned", t))
                    pe.wait_ge(*at("k_rows", t, 1))
                    for g in range(2):
                        fill(pe, f"W{g}", "c", t, g)
                        for p in range(2 * g, 2 * g + 2):
                            for c_ in range(2):
                                o = g4(psum[f"W{g}"])[:, 2 * (p % 2) + c_, :]
                                pe.matmul(o, Bc[:, p, c_, :], W[:, 1, 2 * p:2 * p + 2, :], start=True, stop=False)
                                mm = pe.matmul(o, Kc[:, p, c_, :], V0[:, 2 * p:2 * p + 2, CHUNK:], start=False, stop=True)
                        mm.then_inc(*sig("c_done", t, g))
                    next(turns, None)
                    pe.wait_ge(*at("gt", t))
                    pe.wait_ge(*at("m", t))
                    fill(pe, "P1", "y", t)
                    for c_ in range(2):
                        if t or c_:
                            pe.wait_ge(*(at("z", t, 0) if c_ else at("z", t - 1, 1)))
                        for p in range(NPAIR):
                            mm = pe.matmul(g4(psum["P1"])[64 * c_:64 * c_ + 64, p, :], GT[:, p, 64 * c_:64 * c_ + 64], Z[:, c_, p, :], start=True, stop=True)
                        if c_:
                            mm.then_inc(*sig("y_done", t))
                        fill(pe, "X0", "z", t, c_)
                        for p in range(NPAIR):
                            mm = pe.matmul(g4(psum["X0"])[:, p, :], MT[:, p, c_, :], Z[:, c_, p, :], start=True, stop=True)
                        mm.then_inc(*sig("z_done", t, c_))
                    next(turns, None)
                    pe.wait_ge(*at("y_out", t))
                    fill(pe, "T0", "mix_rwkv", t)
                    for p in range(NPAIR):
                        mm = pe.transpose(g4(psum["T0"])[:, p, :], g4(yc)[:, p, :], ident[:, :])
                    mm.then_inc(*sig("y_turned", t))

                    next(turns, None)
                for _ in attention(NT - 1):
                    pass
        if phases == 2:
            return

        with ExitStack() as scope:
            S.phase(nc, scope, "route")
            A = Arena(arena_t, ARENA)
            wout = A.take(KD, D)
            mixT, xin, x1, xn, h2T = (A.take(2, D) for _ in range(5))
            gate_row, junk = A.take(D), A.take(D)
            L = A.take(NT, NG + NE)
            E12, M = A.take(NT, 2, NE), A.take(NT, NE)
            macc = A.take(NT + 1, NE)
            gcand, ghot, el, cand, h1, h2 = A.take(NT, NG), A.take(NT, NG), A.take(NT, EPG), A.take(NT, EPG), A.take(NT, EPG), A.take(NT, EPG)
            esel = A.take(NT, NG, EPG)
            gm, pg, v1, v2, e2, den = (A.take(NT) for _ in range(6))
            more, nblk, last, begin = A.take(NE, 7), A.take(NE + 2), A.take(NE), A.take(NE)
            RS, picked, destf = A.take(NT, NE), A.take(NT, 2, NE), A.take(NT, 2)
            token_f, table, zeros = A.take(NT), A.take(P), A.take(MAX_BLOCKS + 1)
            s_x = st[:, 0:32]
            kt = lambda ap, t: ap[:, t % 2, :].rearrange("p (k s) -> p k s", k=KD)
            tile = lambda t: slice(P * t, P * t + P)
            groups = lambda ap: ap.rearrange("p t (g e) -> p t g e", g=NG)
            block = scope.enter_context(nc.Block())

            @block.sync
            def _(sp):
                sp.dma_start(gate_row, mod_d[0:1, :].to_broadcast([P, D])).then_inc(*sig("gate_loaded", 0, by=16))

                def load(t):
                    if t >= 2:
                        sp.wait_ge(*at("out_done", t - 2))
                    sp.dma_start(kt(mixT, t), mix_d[:, :, tile(t)].rearrange("c p s -> p c s")).then_inc(*sig(f"mix_loaded{t % 2}", t, by=16))
                    if t >= 2:
                        sp.wait_ge(*at("x1", t - 2))
                    sp.dma_start(xin[:, t % 2, :], x[0, tile(t), :]).then_inc(*sig(f"x_loaded{t % 2}", t, by=16))

                load(0)
                sp.dma_start(wout, w_out[0].rearrange("(k p) n -> p k n", p=P)).then_inc(*sig("wout_loaded", 0, by=16))
                for t in range(NT):
                    if t + 1 < NT:
                        load(t + 1)
                    sp.wait_ge(*at("x1", t))
                    sp.dma_start(x1_d[tile(t), :], x1[:, t % 2, :]).then_inc(*sig(f"x1_stored{t % 2}", t, by=16))
                    sp.wait_ge(*at("xn", t))
                    sp.dma_start(xn2_d[tile(t), :], xn[:, t % 2, :]).then_inc(*sig(f"xn_stored{t % 2}", t, by=16))
                for t in (NT - 2, NT - 1):
                    sp.wait_ge(*at(f"x1_stored{t % 2}", t))
                    sp.wait_ge(*at(f"xn_stored{t % 2}", t))

            @block.gpsimd
            def _(pool):
                link(pool, pool.memset(zeros, 0.0), "zeros", 0)
                pool.dma_start(table_d.rearrange("(p b) o -> p (b o)", p=P), zeros).then_inc(*sig("table_zero", 0, by=16))
                link(pool, pool.tensor_copy(token_f, token_id[:, :]), "tokens", 0)
                for t in range(NT):
                    pool.wait_ge(*at("x_var", t))
                    pool.tensor_tensor(s_x[:, 16 + t:17 + t], s_x[:, 8 + t:9 + t], mhalf[:, 0:1], ALU.pow).then_inc(*sig("x_rstd", t))
                pool.wait_ge(*at("table_zero", 0))
                pool.wait_ge(*at("dest", 0))
                for t in range(NT):
                    for j in range(2):
                        pool.indirect_dma_start(table_d[:, :], bass.IndirectOffsetOnAxis(ap=dest[:, t, j:j + 1], axis=0), token_f[:, t:t + 1], None)\
                            .then_inc(*sig("scattered", t, j, by=16))
                pool.wait_ge(*at("scattered", NT - 1, 1))
                pool.dma_start(table[0:MAX_BLOCKS + 1, :], table_d.rearrange("(b p) o -> b (p o)", p=P)).then_inc(*sig("table_loaded", 0, by=16))

            @block.scalar
            def _(act):
                for t in range(NT):
                    act.wait_ge(*at("x1", t))
                    link(act, act.activation(junk, x1[:, t % 2, :], ACT.Square, accum_out=s_x[:, t:t + 1]), "x_squares", t)
                    for k in range(KD):
                        if k % 4 == 0:
                            act.wait_ge(*at("xn_turned", t, k // 4))
                        link(act, act.activation(kt(h2T, t)[:, k, :], g4(psum[f"T{k // 4}"])[:, k % 4, :], ACT.Identity,
                                                 bias=mod_cols[:, 2, k:k + 1], scale=mod_cols[:, 3, k:k + 1]), "h2T", t, k)
                act.wait_ge(*at("gdiff", 0))
                link(act, act.activation(gcand, gcand, ACT.Exp), "gexp", 0)
                act.wait_ge(*at("ediff", 0))
                link(act, act.activation(e2, e2, ACT.Exp), "eexp", 0)

            @block.vector
            def _(dve):
                def step(ins):
                    link(dve, ins, "dve_step")

                dve.wait_ge(*at("gate_loaded", 0))
                for t in range(NT):
                    b = t % 2
                    dve.wait_ge(*at("out_done", t))
                    dve.wait_ge(*at(f"x_loaded{b}", t))
                    if t >= 2:
                        dve.wait_ge(*at(f"x1_stored{b}", t - 2))
                        dve.wait_ge(*at("x_squares", t - 2))
                    step(dve.tensor_tensor(x1[:, b, :], psum["P"], gate_row, ALU.mult))
                    link(dve, dve.tensor_tensor(x1[:, b, :], x1[:, b, :], xin[:, b, :], ALU.add), "x1", t)
                    dve.wait_ge(*at("x_squares", t))
                    link(dve, dve.tensor_scalar(s_x[:, 8 + t:9 + t], s_x[:, t:t + 1], 1.0 / D, NORM_EPS, ALU.mult, ALU.add), "x_var", t)
                    dve.wait_ge(*at("x_rstd", t))
                    if t >= 2:
                        dve.wait_ge(*at(f"xn_stored{b}", t - 2))
                        dve.wait_ge(*at("xn_turned", t - 2, 1))
                    link(dve, dve.tensor_scalar(xn[:, b, :], x1[:, b, :], s_x[:, 16 + t:17 + t], None, ALU.mult), "xn", t)
                    if t:
                        dve.wait_ge(*at("logits", t - 1))
                        link(dve, dve.tensor_tensor(L[:, t - 1, :], psum["X0"][:, 0:NG + NE], r_brt[:, :], ALU.add), "L", t - 1)
                dve.wait_ge(*at("logits", NT - 1))
                link(dve, dve.tensor_tensor(L[:, NT - 1, :], psum["X0"][:, 0:NG + NE], r_brt[:, :], ALU.add), "L", NT - 1)

                def first_of(hot, cand_, values, top, n):
                    step(dve.tensor_reduce(top, values, AX_X, ALU.max))
                    step(dve.tensor_tensor(cand_, values, over(top, n), ALU.is_equal))
                    step(dve.tensor_tensor(cand_, cand_, each(iota8[:, EPG - n:], NT), ALU.mult))
                    step(dve.tensor_reduce(den, cand_, AX_X, ALU.max))
                    step(dve.tensor_tensor(hot, cand_, over(den, n), ALU.is_equal))

                first_of(ghot, gcand, L[:, :, 0:NG], gm, NG)
                link(dve, dve.tensor_tensor(gcand, L[:, :, 0:NG], over(gm, NG), ALU.subtract), "gdiff", 0)
                dve.wait_ge(*at("gexp", 0))
                step(dve.tensor_reduce(den, gcand, AX_X, ALU.add))
                step(dve.reciprocal(pg, den))
                ghot_wide = ghot.unsqueeze(3).to_broadcast([P, NT, NG, EPG])
                step(dve.tensor_tensor(esel, groups(L[:, :, NG:]), ghot_wide, ALU.mult))
                step(dve.tensor_reduce(el, esel.rearrange("p t g e -> p t e g"), AX_X, ALU.add))
                first_of(h1, cand, el, v1, EPG)
                step(dve.scalar_tensor_tensor(out=el, in0=h1, scalar=MASKED, in1=el, op0=ALU.mult, op1=ALU.add))
                first_of(h2, cand, el, v2, EPG)
                link(dve, dve.tensor_tensor(e2, v2, v1, ALU.subtract), "ediff", 0)
                dve.wait_ge(*at("eexp", 0))
                step(dve.tensor_scalar(den, e2, 1.0, None, ALU.add))
                step(dve.reciprocal(v1, den))
                step(dve.tensor_tensor(wgt[:, :, 0], pg, v1, ALU.mult))
                step(dve.tensor_tensor(wgt[:, :, 1], wgt[:, :, 0], e2, ALU.mult))
                for j, hot in enumerate((h1, h2)):
                    step(dve.tensor_tensor(groups(E12[:, :, j, :]), ghot_wide, hot.unsqueeze(2).to_broadcast([P, NT, NG, EPG]), ALU.mult))
                step(dve.tensor_tensor(M, E12[:, :, 0, :], E12[:, :, 1, :], ALU.add))
                step(dve.memset(macc[:, 0, :], 0.0))
                for t in range(NT):
                    link(dve, dve.tensor_tensor(macc[:, t + 1, :], macc[:, t, :], M[:, t, :], ALU.add), "macc", t)
                dve.wait_ge(*at("ranks", 0))
                counts = psum["W0"][:, NT * NE:(NT + 1) * NE]
                step(dve.tensor_tensor(more, over(counts, 7), each(steps[:, :], NE), ALU.is_gt))
                step(dve.tensor_reduce(last, more, AX_X, ALU.add))
                step(dve.tensor_scalar(last, last, 1.0, None, ALU.add))
                step(dve.memset(nblk[:, 0:1], 0.0))
                step(dve.tensor_tensor_scan(nblk[:, 1:NE + 1], ones[:, 0:NE], last, 0.0, ALU.mult, ALU.add))
                step(dve.tensor_scalar(nblk[:, NE + 1:], nblk[:, NE:NE + 1], -1.0, float(MAX_BLOCKS + 1), ALU.mult, ALU.add))
                step(dve.tensor_copy(first_block[:, :], nblk))
                step(dve.tensor_scalar(begin, nblk[:, 0:NE], float(BLK), None, ALU.mult))
                step(dve.tensor_tensor(RS, psum["W0"][:, 0:NT * NE].rearrange("p (t e) -> p t e", t=NT), each(begin, NT), ALU.add))
                step(dve.tensor_tensor(picked, E12, RS.unsqueeze(2).to_broadcast([P, NT, 2, NE]), ALU.mult))
                step(dve.tensor_reduce(destf, picked, AX_X, ALU.add))
                link(dve, dve.tensor_copy(dest[:, :, :], destf), "dest", 0)
                dve.wait_ge(*at("table_turned", 0))
                link(dve, dve.tensor_copy(idx_all[:, :], psum["W1"][:, 0:MAX_BLOCKS + 1]), "idx_all", 0)

            @block.tensor
            def _(pe):
                pe.wait_ge(*at("wout_loaded", 0))

                def project_out(t):
                    pe.wait_ge(*at(f"mix_loaded{t % 2}", t))
                    for half in range(2):
                        fill(pe, f"P{half}", "x1", t)
                        for k in range(KD):
                            mm = pe.matmul(psum[f"P{half}"], kt(mixT, t)[:, k, :], wout[:, k, 512 * half:512 * half + 512], start=(k == 0), stop=(k == KD - 1))
                    mm.then_inc(*sig("out_done", t))

                project_out(0)
                for t in range(NT):
                    if t + 1 < NT:
                        project_out(t + 1)
                    pe.wait_ge(*at("xn", t))
                    for g in range(2):
                        fill(pe, f"T{g}", "h2T", t, 4 * g + 3)
                        for k in range(4 * g, 4 * g + 4):
                            mm = pe.transpose(g4(psum[f"T{g}"])[:, k % 4, :], kt(xn, t)[:, k, :], ident[:, :])
                        mm.then_inc(*sig("xn_turned", t, g))
                    pe.wait_ge(*at("h2T", t, KD - 1))
                    fill(pe, "X0", "L", t)
                    for k in range(KD):
                        mm = pe.matmul(psum["X0"][:, 0:NG + NE], kt(h2T, t)[:, k, :], wrt[:, k, :], start=(k == 0), stop=(k == KD - 1))
                    mm.then_inc(*sig("logits", t))
                for t in range(NT):
                    pe.wait_ge(*at("macc", t))
                    o = psum["W0"][:, NE * t:NE * t + NE]
                    pe.matmul(o, ones[:, :], macc[:, t, :], start=True, stop=False)
                    pe.matmul(o, before[:, :], M[:, t, :], start=False, stop=True)
                pe.matmul(psum["W0"][:, NT * NE:NT * NE + NE], ones[:, :], macc[:, NT, :], start=True, stop=True).then_inc(*sig("ranks", 0))
                pe.wait_ge(*at("table_loaded", 0))
                pe.transpose(psum["W1"][:, 0:MAX_BLOCKS + 1], table[0:MAX_BLOCKS + 1, :], ident[0:MAX_BLOCKS + 1, 0:MAX_BLOCKS + 1]).then_inc(*sig("table_turned", 0))
        if phases == 3:
            return

        with ExitStack() as scope:
            S.phase(nc, scope, "experts")
            A = Arena(arena_t, ARENA)
            gate_w = [A.take(KD, DE) for _ in range(2)]
            up_w = [A.take(KD, DE) for _ in range(2)]
            down_w = [A.take(KE, D) for _ in range(2)]
            rows, xT, y_sb = A.take(D), A.take(KD, P), A.take(D)
            th, hid, hidT = A.take(DE), A.take(DE), A.take(KE, P)
            nothing = A.take(D)
            index_now = A.take(1).bitcast(I32)
            q = S.sem
            block = scope.enter_context(nc.Block())

            def bounds(eng, e):
                return (eng.value_load(first_block[0:1, bass.ds(e, 1)], min_val=0, max_val=MAX_BLOCKS),
                        eng.value_load(first_block[0:1, bass.ds(e + 1, 1)], min_val=1, max_val=MAX_BLOCKS))

            @block.sync
            def _(sp):
                sp.sem_inc(q("y_stored"), 16)
                def load(e, u):
                    sp.dma_start(gate_w[u], e_gate[0, bass.ds(e, 1)].rearrange("a (k p) n -> p (a k) n", p=P)).then_inc((q("gate_loaded0"), q("gate_loaded1"))[u], 16)
                    sp.dma_start(up_w[u], e_up[0, bass.ds(e, 1)].rearrange("a (k p) n -> p (a k) n", p=P)).then_inc((q("up_loaded0"), q("up_loaded1"))[u], 16)
                    sp.dma_start(down_w[u], e_down[0, bass.ds(e, 1)].rearrange("a (k p) n -> p (a k) n", p=P)).then_inc((q("down_loaded0"), q("down_loaded1"))[u], 16)

                def store_blocks(e):
                    first, end = bounds(sp, e)
                    with sp.Fori(first, end) as b:
                        sp.wait_ge(q("y0_ready"), b + 2)
                        sp.wait_ge(q("y1_ready"), b + 2)
                        sp.dma_start(y_d[bass.ds(b * BLK, BLK), :], y_sb).then_inc(q("y_stored"), 16)
                    return end

                load(0, 0)
                load(1, 1)
                with sp.Fori(0, NE // 2 - 1) as pair:
                    for u in range(2):
                        end = store_blocks(pair * 2 + u)
                        sp.wait_ge(q("y1_done"), end + 1)
                        load(pair * 2 + u + 2, u)
                for u in range(2):
                    store_blocks(NE - 2 + u)

            @block.gpsimd
            def _(pool):
                total = pool.value_load(first_block[0:1, NE:NE + 1], min_val=1, max_val=MAX_BLOCKS)
                with pool.Fori(0, total + 1) as b:
                    pool.wait_ge(q("turned"), b + 1)
                    pool.sem_inc(q("rows_seen"))
                    pool.tensor_copy(index_now, idx_all[:, bass.ds(b, 1)]).then_inc(q("index_ready"), 1)
                    pool.wait_ge(q("index_ready"), b + 1)
                    pool.sem_inc(q("index_seen"))
                    pool.indirect_dma_start(rows, None, xn2_d[:, :], bass.IndirectOffsetOnAxis(ap=index_now, axis=0)).then_inc(q("gathered"), 16)
                pool.wait_ge(q("gathered"), (total + 1) * 16)

            @block.scalar
            def _(act):
                act.sem_inc(q("y1_ready"))
                total = act.value_load(first_block[0:1, NE:NE + 1], min_val=1, max_val=MAX_BLOCKS)
                act.wait_ge(q("zeros_ready"), 1)
                with act.Fori(total, MAX_BLOCKS + 1) as b:
                    act.dma_start(y_d[bass.ds(b * BLK, BLK), :], nothing).then_inc(q("rest_stored"), 16)
                with act.Fori(0, total) as b:
                    act.wait_ge(q("gate_done"), b + 1)
                    act.wait_ge(q("half_gated"), b + 1)
                    act.activation(th, psum["X0"], ACT.Tanh, scale=0.5).then_inc(q("tanh_done"), 1)
                    act.wait_ge(q("y1_done"), b + 2)
                    act.wait_ge(q("y_stored"), (b + 1) * 16)
                    act.activation(y_sb[:, 512:], psum["P1"], ACT.Copy).then_inc(q("y1_ready"), 1)

            @block.vector
            def _(dve):
                for sem in (q("half_gated"), q("hidden"), q("y0_ready")):
                    dve.sem_inc(sem)
                dve.memset(nothing, 0.0).then_inc(q("zeros_ready"), 1)
                total = dve.value_load(first_block[0:1, NE:NE + 1], min_val=1, max_val=MAX_BLOCKS)

                def scale_rows(b):
                    dve.wait_ge(q("turned"), b + 2)
                    dve.tensor_tensor(xT, psum["T"].rearrange("p (k s) -> p k s", k=KD), over(mod_cols[:, 3, :], P), ALU.mult).then_inc(q("xT_scaled"), 1)
                    dve.wait_ge(q("xT_scaled"), b + 1)
                    dve.tensor_tensor(xT, xT, over(mod_cols[:, 2, :], P), ALU.add).then_inc(q("xT_ready"), 1)

                scale_rows(0)
                with dve.Fori(0, total) as b:
                    dve.wait_ge(q("tanh_done"), b + 1)
                    dve.wait_ge(q("hid_turned"), b + 1)
                    dve.scalar_tensor_tensor(out=hid, in0=th, scalar=1.0, in1=psum["X0"], op0=ALU.add, op1=ALU.mult).then_inc(q("half_gated"), 1)
                    dve.wait_ge(q("half_gated"), b + 2)
                    dve.wait_ge(q("up_done"), b + 1)
                    dve.scalar_tensor_tensor(out=hid, in0=hid, scalar=0.5, in1=psum["X1"], op0=ALU.mult, op1=ALU.mult).then_inc(q("hidden"), 1)
                    dve.wait_ge(q("y1_done"), b + 1)
                    dve.wait_ge(q("hid_turned"), b + 2)
                    dve.tensor_copy(hidT, g4(psum["W0"])).then_inc(q("hidT_ready"), 1)
                    scale_rows(b + 1)
                    dve.wait_ge(q("y0_done"), b + 1)
                    dve.wait_ge(q("y_stored"), (b + 1) * 16)
                    dve.tensor_copy(y_sb[:, 0:512], psum["P0"]).then_inc(q("y0_ready"), 1)
                left = dve.value_load(first_block[0:1, NE + 1:NE + 2], min_val=1, max_val=MAX_BLOCKS)
                dve.wait_ge(q("y_stored"), (total + 1) * 16)
                dve.wait_ge(q("rest_stored"), left * 16)
                dve.tensor_copy(hid[:, 0:1], y_sb[:, 0:1])

            @block.tensor
            def _(pe):
                for sem in (q("turned"), q("hid_turned"), q("y1_done")):
                    pe.sem_inc(sem)
                def turn_rows(b):
                    pe.wait_ge(q("gathered"), (b + 1) * 16)
                    for k in range(KD):
                        mm = pe.transpose(psum["T"][:, P * k:P * k + P], rows[:, P * k:P * k + P], ident[:, :])
                    mm.then_inc(q("turned"), 1)

                turn_rows(0)
                with pe.Fori(0, NE // 2) as pair:
                    for u in range(2):
                        nth = (pair + 1) * 16
                        first, end = bounds(pe, pair * 2 + u)
                        with pe.Fori(first, end) as b:
                            pe.wait_ge((q("gate_loaded0"), q("gate_loaded1"))[u], nth)
                            pe.wait_ge((q("up_loaded0"), q("up_loaded1"))[u], nth)
                            pe.wait_ge((q("down_loaded0"), q("down_loaded1"))[u], nth)
                            pe.wait_ge(q("xT_ready"), b + 1)
                            pe.wait_ge(q("hidden"), b + 1)
                            for bank, w, done in (("X0", gate_w[u], q("gate_done")), ("X1", up_w[u], q("up_done"))):
                                for k in range(KD):
                                    mm = pe.matmul(psum[bank], xT[:, k, :], w[:, k, :], start=(k == 0), stop=(k == KD - 1))
                                mm.then_inc(done, 1)
                            turn_rows(b + 1)
                            pe.wait_ge(q("hidden"), b + 2)
                            for f in range(KE):
                                mm = pe.transpose(g4(psum["W0"])[:, f, :], hid[:, P * f:P * f + P], ident[:, :])
                            mm.then_inc(q("hid_turned"), 1)
                            pe.wait_ge(q("hidT_ready"), b + 1)
                            for half, drained, done in ((0, q("y0_ready"), q("y0_done")), (1, q("y1_ready"), q("y1_done"))):
                                pe.wait_ge(drained, b + 1)
                                for f in range(KE):
                                    mm = pe.matmul(psum[f"P{half}"], hidT[:, f, :], down_w[u][:, f, 512 * half:512 * half + 512], start=(f == 0), stop=(f == KE - 1))
                                mm.then_inc(done, 1)
        if phases == 4:
            return

        with ExitStack() as scope:
            S.phase(nc, scope, "finish")
            A = Arena(arena_t, ARENA)
            first, second, x1, res, normed = (A.take(2, D) for _ in range(5))
            gate_row, shift_row, gain_row, junk = (A.take(D) for _ in range(4))
            s_x = st[:, 0:32]
            tile = lambda t: slice(P * t, P * t + P)
            block = scope.enter_context(nc.Block())

            @block.sync
            def _(sp):
                for i, dst in ((1, gate_row), (2, shift_row), (3, gain_row)):
                    sp.dma_start(dst, mod_d[i:i + 1, :].to_broadcast([P, D])).then_inc(*sig("rows_loaded", i, by=16))

                def load(t):
                    if t >= 2:
                        sp.wait_ge(*at("x2", t - 2))
                    sp.dma_start(x1[:, t % 2, :], x1_d[tile(t), :]).then_inc(*sig(f"x1_loaded{t % 2}", t, by=16))

                load(0)
                for t in range(NT):
                    if t + 1 < NT:
                        load(t + 1)
                    sp.wait_ge(*at("out", t))
                    sp.dma_start(out[0, tile(t), :], normed[:, t % 2, :]).then_inc(*sig(f"out_stored{t % 2}", t, by=16))
                for t in (NT - 2, NT - 1):
                    sp.wait_ge(*at(f"out_stored{t % 2}", t))

            @block.gpsimd
            def _(pool):
                def gather(t):
                    for j, (dst, used) in enumerate(((first, "moe"), (second, "moe"))):
                        if t >= 2:
                            pool.wait_ge(*at(used, t - 2))
                        pool.indirect_dma_start(dst[:, t % 2, :], None, y_d[:, :], bass.IndirectOffsetOnAxis(ap=dest[:, t, j:j + 1], axis=0))\
                            .then_inc(*sig(f"gathered{j}{t % 2}", t, by=16))

                gather(0)
                for t in range(NT):
                    if t + 1 < NT:
                        gather(t + 1)
                    pool.wait_ge(*at("x_var", t))
                    pool.tensor_tensor(s_x[:, 16 + t:17 + t], s_x[:, 8 + t:9 + t], mhalf[:, 0:1], ALU.pow).then_inc(*sig("x_rstd", t))

            @block.scalar
            def _(act):
                for t in range(NT):
                    act.wait_ge(*at(f"gathered0{t % 2}", t))
                    link(act, act.activation(first[:, t % 2, :], first[:, t % 2, :], ACT.Copy, scale=wgt[:, t, 0:1]), "weighted_first", t)
                    act.wait_ge(*at("x2", t))
                    link(act, act.activation(junk, res[:, t % 2, :], ACT.Square, accum_out=s_x[:, t:t + 1]), "x_squares", t)

            @block.vector
            def _(dve):
                def step(ins):
                    link(dve, ins, "dve_step")

                dve.wait_ge(*at("rows_loaded", 3))
                for t in range(NT):
                    b = t % 2
                    dve.wait_ge(*at("weighted_first", t))
                    dve.wait_ge(*at(f"gathered1{b}", t))
                    if t >= 2:
                        dve.wait_ge(*at("x_squares", t - 2))
                    link(dve, dve.scalar_tensor_tensor(out=res[:, b, :], in0=second[:, b, :], scalar=wgt[:, t, 1:2], in1=first[:, b, :], op0=ALU.mult, op1=ALU.add), "moe", t)
                    step(dve.tensor_tensor(res[:, b, :], res[:, b, :], gate_row, ALU.mult))
                    dve.wait_ge(*at(f"x1_loaded{b}", t))
                    link(dve, dve.tensor_tensor(res[:, b, :], res[:, b, :], x1[:, b, :], ALU.add), "x2", t)
                    dve.wait_ge(*at("x_squares", t))
                    link(dve, dve.tensor_scalar(s_x[:, 8 + t:9 + t], s_x[:, t:t + 1], 1.0 / D, NORM_EPS, ALU.mult, ALU.add), "x_var", t)
                    dve.wait_ge(*at("x_rstd", t))
                    if t >= 2:
                        dve.wait_ge(*at(f"out_stored{b}", t - 2))
                    step(dve.scalar_tensor_tensor(out=normed[:, b, :], in0=res[:, b, :], scalar=s_x[:, 16 + t:17 + t], in1=gain_row, op0=ALU.mult, op1=ALU.mult))
                    link(dve, dve.tensor_tensor(normed[:, b, :], normed[:, b, :], shift_row, ALU.add), "out", t)


_INS = ['x', 'c', 'ada_w', 'ada_b', 'norm1_g', 'w_in', 'shift_mu', 'w0', 'w_decay_up', 'a0', 'w_aaa_up', 'w_gate_up',
        'k_k', 'k_a', 'r_k', 'gn_g', 'gn_b', 'kv_norm_g', 'k_idx_norm_g', 'w_uk', 'w_uv', 'w_out', 'norm2_g',
        'w_group', 'b_group', 'w_expert', 'b_expert', 'e_gate', 'e_up', 'e_down',
        'final_ada_w', 'final_ada_b', 'final_norm_g']


def kernel(**inputs):
    import numpy as _np
    import concourse.bacc as _bacc
    from concourse import mybir as _mybir
    from concourse.bass_utils import run_bass_kernel_spmd as _run

    arrays = {f"in_{name}_dram": _np.ascontiguousarray(inputs[name]) for name in _INS}
    numbers = None
    for _ in range(2):
        nc = _bacc.Bacc("TRN2", target_bir_lowering=False, num_devices=1)
        args = [nc.dram_tensor(n, a.shape, _mybir.dt.from_np(a.dtype), kind="ExternalInput").ap() for n, a in arrays.items()]
        args.append(nc.dram_tensor("out_0_dram", (1, SEQ, D), _mybir.dt.float32, kind="ExternalOutput").ap())
        signals = Signals(numbers)
        sparse_attention_moe_layer(nc, *args, signals)
        numbers = signals.seen
    r = _run(nc, [arrays], core_ids=[0])
    return r.results[0]["out_0_dram"]
```

```python
from contextlib import ExitStack

import numpy as np

import concourse.bass as bass
from concourse import mybir

F32 = mybir.dt.float32
I32 = mybir.dt.int32
BF16 = mybir.dt.bfloat16
ALU = mybir.AluOpType
ACT = mybir.ActivationFunctionType
AX_X = mybir.AxisListType.X

P = 128
SEQ = 1024
D = 1024
KD = D // P
NT = SEQ // P
CHUNK = 64
HEAD = 64
NH = 8
NPAIR = NH // 2
RW = 512
LATENT = 128
IDX_HEADS = 4
TOPK = 256
NG = 4
EPG = 8
NE = NG * EPG
DE = 512
KE = DE // P
NRW = 14
NCT = 20
LEVELS = 6
MANTISSA = 23
SEARCH = (5, 4, 2, 6, 6)
BLK = 64
SLOTS = 3
MAX_BLOCKS = NE + 2 * SEQ // BLK
ARENA = 41240
WEIGHTS_AT = ARENA - 2 * KD * DE - KE * D
ALL_BLOCKS = MAX_BLOCKS + 2
ROWS = ALL_BLOCKS * BLK
NORM_EPS = 1e-6
GN_EPS = HEAD * 1e-5
DECAY = float(np.exp(-0.5))
MASKED = -float(2.0 ** 127)
INADMISSIBLE = -1.0e38
BEYOND = 3.0e38
NEG = -1.0e30
W_GROUPS = [(2304, 452, (18, 19)), (1792, 512, (14, 15, 16, 17)), (1536, 256, (12, 13)),
            (1024, 512, (8, 9, 10, 11)), (512, 512, (4, 5, 6, 7)), (0, 512, (0, 1, 2, 3))]
NROW = LATENT + CHUNK + IDX_HEADS


class Arena:

    def __init__(self, tensor, size):
        self.tensor, self.size, self.at = tensor, size, 0

    def take(self, *shape):
        n = int(np.prod(shape))
        assert self.at + n <= self.size, (self.at, n, self.size)
        piece = self.tensor[:, self.at:self.at + n]
        self.at += n
        if len(shape) == 1:
            return piece
        names = "abcd"[:len(shape)]
        return piece.rearrange(f"p ({' '.join(names)}) -> p {' '.join(names)}", **dict(zip(names, shape)))


class Signals:

    def __init__(self, numbers=None):
        self.numbers, self.seen, self.count, self.sems = numbers, {}, {}, {}

    def phase(self, nc, scope, name):
        self.nc, self.name, self.sems = nc, name, {}
        scope.callback(self.end)

    def end(self):
        self.nc.clear_and_free_semaphores(list(self.sems.values()))
        self.nc.all_engine_barrier()

    def sem(self, name):
        if name not in self.sems:
            self.sems[name] = self.nc.alloc_semaphore(f"{self.name}_{name}")
        return self.sems[name]

    def sig(self, name, *key, by=1):
        k = (self.name, name)
        self.count[k] = self.count.get(k, 0) + by
        assert (self.name, name, *key) not in self.seen, (name, key)
        self.seen[(self.name, name, *key)] = self.count[k]
        return self.sem(name), by

    def at(self, name, *key):
        return self.sem(name), self.numbers[(self.name, name, *key)] if self.numbers else 1


def sparse_attention_moe_layer(nc, x, c, ada_w, ada_b, norm1_g, w_in, shift_mu, w0, w_decay_up, a0, w_aaa_up,
                               w_gate_up, k_k, k_a, r_k, gn_g, gn_b, kv_norm_g, k_idx_norm_g, w_uk, w_uv, w_out,
                               norm2_g, w_group, b_group, w_expert, b_expert, e_gate, e_up, e_down,
                               final_ada_w, final_ada_b, final_norm_g, out, S):
    with ExitStack() as ctx:
        def sb(name, shape, dt=F32):
            return ctx.enter_context(nc.sbuf_tensor(name, shape, dt))

        def dram(name, shape, dt=F32):
            return nc.dram_tensor(name, shape, dt, kind="Internal").ap()

        sig, at = S.sig, S.at

        def link(eng, ins, name, *key):
            sem, by = sig(name, *(key or (("step", S.count.get((S.name, name), 0)),)))
            ins.then_inc(sem, by)
            eng.wait_ge(sem, S.count[(S.name, name)])

        readers = {}

        def fill(pe, bank, *reader):
            if (S.name, bank) in readers:
                pe.wait_ge(*at(*readers[(S.name, bank)]))
            readers[(S.name, bank)] = reader

        psum = {}
        for pair in ("P", "T", "X", "W"):
            both = ctx.enter_context(nc.psum_tensor(f"ps{pair}", [P, 1024], F32))
            psum[pair], psum[pair + "0"], psum[pair + "1"] = both[:, :], both[:, 0:512], both[:, 512:1024]

        p_d = dram("proj_T", (NCT, P, SEQ))
        mod_d = dram("mod_rows", (4, D))
        mix_d = dram("mix_T", (KD, P, SEQ))
        x1_d = dram("x1_rows", (SEQ, D))
        xn2_d = dram("xn2_rows", (SEQ, D))
        y_d = dram("expert_rows", (ROWS, D))
        table_d = dram("row_token", (ROWS, 1))

        wdec, waaa, wgate, wuv = (sb(n, [P, RW]) for n in ("wdec", "waaa", "wgate", "wuv"))
        wukT = sb("wukT", [P, NPAIR, P])
        wrt = sb("wrt", [P, KD, NG + NE])
        ident = sb("ident", [P, P])
        m_lvl = sb("m_lvl", [P, LEVELS, P], BF16)
        m_pair = sb("m_pair", [P, 2, P])
        m_low = sb("m_low", [P, P])
        m_bd = sb("m_bd", [P, P])
        blk2 = sb("blk2", [P, 2])
        scan_reset = sb("scan_reset", [P, RW], BF16)
        ones = sb("ones", [P, P])
        before = sb("before", [P, P])
        causal = sb("causal", [P, 256])
        iota8 = sb("iota8", [P, EPG])
        halves = sb("halves", [P, MANTISSA])
        steps = sb("steps", [P, SEQ // BLK - 1])
        token_id = sb("token_id", [P, NT], I32)
        mhalf = sb("mhalf", [P, 16])
        cols = sb("cols", [P, 50])
        c_mu, c_w0, c_a0, c_kk, c_ka, c_rk = (cols[:, a:b] for a, b in ((0, 14), (14, 18), (18, 22), (22, 26), (26, 30), (30, 34)))
        c_g1, c_g2 = cols[:, 34:42], cols[:, 42:50]
        r_gng, r_gnb = sb("r_gng", [P, RW]), sb("r_gnb", [P, RW])
        r_kvg = sb("r_kvg", [P, LATENT + CHUNK])
        r_brt = sb("r_brt", [P, NG + NE])
        mod_cols = sb("mod_cols", [P, 4, KD])
        rowp = sb("rowp", [P, NT, NROW])
        ckv_all = sb("ckv_all", [P, NT, LATENT])
        ckvT, kiT = sb("ckvT", [P, SEQ]), sb("kiT", [P, SEQ])
        Z = sb("Z", [P, 2, NPAIR, P])


        wgt = sb("wgt", [P, NT, 2])
        dest = sb("dest", [P, NT, 2], I32)
        first_block = sb("first_block", [P, NE + 1], I32)
        idx_all = sb("idx_all", [BLK, ALL_BLOCKS], I32)
        st = sb("st", [P, 96])
        arena_t = sb("arena", [P, ARENA])

        def g4(ap):
            return ap.rearrange("p (a b) -> p a b", a=4)

        def g8(ap):
            return ap.rearrange("p (a b) -> p a b", a=8)

        def over(ap, n):
            return ap.unsqueeze(2).to_broadcast([ap.shape[0], ap.shape[1], n])

        def each(ap, a):
            return ap.unsqueeze(1).to_broadcast([ap.shape[0], a, ap.shape[1]])

        with ExitStack() as scope:
            S.phase(nc, scope, "project")
            A = Arena(arena_t, ARENA)
            slots = [A.take(KD, 512) for _ in range(4)]
            hT = A.take(KD, SEQ)
            xin = A.take(4, D)
            mrow = A.take(2, 512)
            stage = A.take(4, 512)
            cB = A.take(KD, P)
            cT = A.take(4, KD)
            bias = A.take(2, 512)
            junk = A.take(D)
            wuk_sb = A.take(RW)
            gain_f = A.take(512)
            ki_twice = A.take(NT, P)
            kv_sum, kv_var, kv_rs = A.take(2, NT), A.take(2 * NT), A.take(2 * NT)
            stream = [("ada", n) for n in range(4)] + [("win", g) for g in range(6)] + [("ada", n) for n in range(4, 16)]
            place = {name: i for i, name in enumerate(stream)}
            outs = [(g, ct, half) for g, (_, _, tiles) in enumerate(W_GROUPS) for ct in tiles for half in range(2)]
            out_bank = ["P0", "P1", "X0", "X1"]

            def last_use(kind, n):
                if kind == "ada":
                    return at("ada_done", n // 2)
                return at("rows_done", NT - 1) if n == 0 else at("projected", max(i for i, o in enumerate(outs) if o[0] == n))

            def ada_source(n):
                if n < 12:
                    return ada_w[0, :, 512 * n:512 * n + 512], ada_b[:, 512 * n:512 * n + 512]
                m = 512 * (n - 12)
                return final_ada_w[:, m:m + 512], final_ada_b.rearrange("(a n) -> a n", a=1)[:, m:m + 512]

            block = scope.enter_context(nc.Block())

            @block.sync
            def _(sp):
                sp.dma_start(cT[:, 0, :], c.rearrange("a (k p) -> (a p) k", p=P), allow_slow_non_contiguous=True).then_inc(*sig("c_loaded", 0, by=16))
                for i, (kind, n) in enumerate(stream):
                    if kind == "win":
                        col, width, _ = W_GROUPS[n]
                        src = w_in[0, :, col:col + width]
                    else:
                        width = 512
                        src, bias_src = ada_source(n)
                        v, h = n // 2, n % 2
                        if v >= 2:
                            sp.wait_ge(*at("row", v - 2))
                        sp.dma_start(bias[64 * h:64 * h + 64, v % 2, :], bias_src.to_broadcast([64, 512])).then_inc(*sig(f"bias_loaded{v % 2}{h}", n, by=16))
                    if i >= 4:
                        sp.wait_ge(*last_use(*stream[i - 4]))
                    sp.dma_start(slots[i % 4][:, :, 0:width], src.rearrange("(k p) n -> p k n", p=P))\
                        .then_inc(*sig(f"slot_loaded{i % 4}", i, by=16))
                    if i == 1:
                        for t in range(4):
                            sp.dma_start(xin[:, t, :], x[0, P * t:P * t + P, :]).then_inc(*sig(f"x_loaded{t % 4}", t, by=16))
                    if i == 5:
                        sp.wait_ge(*at("x_turned_bank", 0, KD - 1))
                        for t in range(4, 8):
                            sp.dma_start(xin[:, t - 4, :], x[0, P * t:P * t + P, :]).then_inc(*sig(f"x_loaded{t % 4}", t, by=16))

            @block.gpsimd
            def _(pool):
                def step(ins):
                    link(pool, ins, "const_step")

                def keep(ap, pattern, base, mult, op=ALU.is_ge, fill_=0.0):
                    step(pool.affine_select(out=ap, in_=ap, compare_op=op, fill=fill_, base=base, pattern=pattern,
                                            channel_multiplier=mult))

                for i, (dst, v) in enumerate(((c_g1, norm1_g), (c_mu, shift_mu), (c_w0, w0), (c_a0, a0), (c_kk, k_k), (c_ka, k_a),
                               (c_rk, r_k.rearrange("a h d -> a (h d)")), (c_g2, norm2_g))):
                    pool.dma_start(dst, v.rearrange("a (k p) -> (a p) k", p=P), allow_slow_non_contiguous=True)\
                        .then_inc(*sig("cols_loaded", i, by=16))
                small = [(wuk_sb, w_uk[0].rearrange("c h d -> c (h d)")),
                         (gain_f[0:64], final_norm_g.rearrange("(a n) -> a n", a=1)[:, 0:512].to_broadcast([64, 512])),
                         (gain_f[64:128], final_norm_g.rearrange("(a n) -> a n", a=1)[:, 512:].to_broadcast([64, 512])),
                         (wdec[0:64, :], w_decay_up[0]), (waaa[64:128, :], w_aaa_up[0]), (wgate[:, :], w_gate_up[0]),
                         (wuv[:, :], w_uv[0].rearrange("c h d -> c (h d)")),
                         (wrt[:, :, 0:NG], w_group[0].rearrange("(k p) n -> p k n", p=P)),
                         (wrt[:, :, NG:], w_expert[0].rearrange("(k p) n -> p k n", p=P)),
                         (r_gng[:, :], gn_g.to_broadcast([P, RW])), (r_gnb[:, :], gn_b.to_broadcast([P, RW])),
                         (r_kvg[:, 0:LATENT], kv_norm_g.to_broadcast([P, LATENT])),
                         (r_kvg[:, LATENT:], k_idx_norm_g.to_broadcast([P, CHUNK])),
                         (r_brt[:, 0:NG], b_group.to_broadcast([P, NG])), (r_brt[:, NG:], b_expert.to_broadcast([P, NE]))]
                for i, (dst, src) in enumerate(small):
                    pool.dma_start(dst, src).then_inc(*sig("small_loaded", i, by=16))
                step(pool.memset(mhalf[:, :], -0.5))
                step(pool.memset(ident[:, :], 0.0))
                keep(ident[:, :], [[-1, P]], 0, 1, ALU.not_equal, 1.0)
                link(pool, pool.memset(ones[:, :], 1.0), "ident_ready", 0)
                step(pool.memset(wdec[64:128, :], 0.0))
                step(pool.memset(waaa[0:64, :], 0.0))
                for ap in (before[:, :], m_bd[:, :], blk2[:, :], scan_reset[:, :], m_low[:, :], m_pair[:, :, :], m_lvl[:, :, :]):
                    step(pool.memset(ap, 1.0))
                step(pool.memset(causal[:, :], 0.0))
                keep(m_bd[:, 0:64], [[0, 64]], 63, -1)
                keep(m_bd[:, 64:128], [[0, 64]], -64, 1)
                keep(blk2[:, 0:1], [[0, 1]], 63, -1)
                keep(blk2[:, 1:2], [[0, 1]], -64, 1)
                keep(before[:, :], [[1, P]], -1, -1)
                keep(m_pair[:, 0, :], [[1, P]], -1, -1)
                keep(m_pair[:, 1, :], [[1, P]], 0, -1)
                for i in range(2):
                    keep(m_pair[:, i, 64:128], [[0, 64]], -64, 1)
                keep(m_low[:, :], [[-1, P]], -1, 1)
                keep(m_low[:, 0:64], [[0, 64]], 63, -1)
                for l in range(LEVELS):
                    n = 2 ** l
                    v = m_lvl[:, l, :].rearrange("p (b h i) -> p b h i", h=2, i=n)
                    step(pool.memset(v[:, :, 0, :], 0.0))
                    keep(v[:, :, 1, :], [[-2 * n, P // (2 * n)], [0, n]], 0, 1)
                    keep(v[:, :, 1, :], [[2 * n, P // (2 * n)], [0, n]], n - 1, -1)
                step(pool.memset(scan_reset[:, :].rearrange("p (a b) -> p a b", b=CHUNK)[:, :, 0:1], 0.0))
                step(pool.memset(causal[0:64, 192:256], NEG))
                step(pool.iota(token_id[:, :], pattern=[[P, NT]], base=0, channel_multiplier=1))
                for i in range(EPG):
                    step(pool.memset(iota8[:, i:i + 1], float(EPG - i)))
                for i in range(MANTISSA):
                    step(pool.memset(halves[:, i:i + 1], -float(2.0 ** -(i + 1))))
                for i in range(SEQ // BLK - 1):
                    step(pool.memset(steps[:, i:i + 1], float(BLK * (i + 1))))
                step(pool.memset(Z[:, :, :, :], 0.0))
                for t in range(NT):
                    pool.wait_ge(*at("x_var", t))
                    pool.tensor_tensor(st[:, 16 + t:17 + t], st[:, 8 + t:9 + t], mhalf[:, 0:1], ALU.pow).then_inc(*sig("x_rstd", t))
                pool.wait_ge(*at("kv_var", 0))
                link(pool, pool.tensor_tensor(kv_rs, kv_var, mhalf[:, 0:2 * NT], ALU.pow), "kv_rs", 0)
                for i, (g, ct, half) in enumerate(outs):
                    pool.wait_ge(*at("staged", i))
                    pool.dma_start(p_d[ct, :, 512 * half:512 * half + 512], stage[:, i % 4, :]).then_inc(*sig(f"stored{i % 4}", i, by=16))
                    if i < ROWS // P:
                        pool.dma_start(y_d[P * i:P * i + P, :], Z[:, :, :, :].rearrange("p a b c -> p (a b c)")).then_inc(*sig("rows_zero", i, by=16))
                for i, v in enumerate((2, 5, 6, 7)):
                    pool.wait_ge(*at("mod_row", v))
                    for h in range(2):
                        pool.dma_start(mod_d[i:i + 1, 512 * h:512 * h + 512], mrow[64 * h:64 * h + 1, v % 2, :]).then_inc(*sig("row_stored", v, h, by=16))
                    pool.wait_ge(*at("row_stored", v, 1))
                for i in range(len(outs) - 4, len(outs)):
                    pool.wait_ge(*at(f"stored{i % 4}", i))
                pool.wait_ge(*at("small_loaded", len(small) - 1))
                pool.wait_ge(*at("rows_zero", ROWS // P - 1))

            @block.scalar
            def _(act):
                act.wait_ge(*at("c_loaded", 0))
                act.activation(cT[:, 1, :], cT[:, 0, :], ACT.Exp, scale=-1.0).then_inc(*sig("c_exp", 0))

                for half in range(2):
                    for t in range(4 * half, 4 * half + 4):
                        act.wait_ge(*at(f"x_loaded{t % 4}", t))
                        link(act, act.activation(junk, xin[:, t % 4, :], ACT.Square, accum_out=st[:, t:t + 1]), "x_squares", t)
                    act.wait_ge(*at("mod_cols", 1))
                    for k in range(KD):
                        act.wait_ge(*at("x_turned_bank", half, k))
                        act.activation(hT[:, k, 512 * half:512 * half + 512], psum[f"T{k % 2}"], ACT.Identity,
                                       bias=mod_cols[:, 0, k:k + 1], scale=mod_cols[:, 1, k:k + 1]).then_inc(*sig("h_ready", half, k))
                for t in range(NT):
                    act.wait_ge(*at("rows_ready", t))
                    link(act, act.activation(junk[:, 0:LATENT], rowp[:, t, 0:LATENT], ACT.Square, accum_out=kv_sum[:, 0, t:t + 1]), "kv_sq", t, 0)
                    link(act, act.activation(junk[:, 0:CHUNK], rowp[:, t, LATENT:LATENT + CHUNK], ACT.Square, accum_out=kv_sum[:, 1, t:t + 1]), "kv_sq", t, 1)
                for i, (g, ct, half) in enumerate(outs):
                    act.wait_ge(*at("projected", i))
                    if i >= 4:
                        act.wait_ge(*at(f"stored{i % 4}", i - 4))
                    act.activation(stage[:, i % 4, :], psum[out_bank[i % 4]], ACT.Copy).then_inc(*sig("staged", i))

            @block.vector
            def _(dve):
                def step(ins):
                    link(dve, ins, "dve_step")

                dve.wait_ge(*at("c_exp", 0))
                step(dve.tensor_scalar(cT[:, 2, :], cT[:, 1, :], 1.0, None, ALU.add))
                step(dve.reciprocal(cT[:, 3, :], cT[:, 2, :]))
                step(dve.tensor_tensor(cT[:, 1, :], cT[:, 0, :], cT[:, 3, :], ALU.mult))
                link(dve, dve.tensor_copy(cB, over(cT[:, 1, :], P)), "c_ready", 0)

                def modulation(v):
                    dve.wait_ge(*at("ada_done", v))
                    for h in range(2):
                        dve.wait_ge(*at(f"bias_loaded{v % 2}{h}", 2 * v + h))
                    if v >= 2:
                        if v - 2 in (0, 1, 3, 4):
                            dve.wait_ge(*at("cols_turned", v - 2))
                        else:
                            dve.wait_ge(*at("row_stored", v - 2, 1))
                    link(dve, dve.tensor_tensor(mrow[:, v % 2, :], psum[f"W{v % 2}"], bias[:, v % 2, :], ALU.add), "row", v)
                    if v in (0, 1, 3, 4):
                        link(dve, dve.tensor_copy(st[:, 95:96], mrow[:, v % 2, 0:1]), "mod_row", v)
                        dve.wait_ge(*at("cols_turned", v))
                        turned = psum["T0"].rearrange("p (j h r) -> p h j r", j=4, h=2)[:, :, :, 0]
                        halves_of = lambda ap: ap.rearrange("p (h j) -> p h j", h=2)
                        i = (0, 1, None, 2, 3)[v]
                        if i % 2 == 0:
                            link(dve, dve.tensor_copy(halves_of(mod_cols[:, i, :]), turned), "mod_cols", v)
                        else:
                            dve.wait_ge(*at("small_loaded", 14))
                            step(dve.tensor_scalar(halves_of(mod_cols[:, i, :]), turned, 1.0, None, ALU.add))
                            dve.wait_ge(*at("cols_loaded", 7))
                            link(dve, dve.tensor_tensor(mod_cols[:, i, :], mod_cols[:, i, :], c_g1 if v == 1 else c_g2, ALU.mult), "mod_cols", v)
                    elif v in (2, 5):
                        link(dve, dve.tensor_scalar(mrow[:, v % 2, :], mrow[:, v % 2, :], 1.0, None, ALU.add), "mod_row", v)
                    elif v == 6:
                        link(dve, dve.tensor_copy(st[:, 95:96], mrow[:, v % 2, 0:1]), "mod_row", v)
                    else:
                        step(dve.tensor_scalar(mrow[:, v % 2, :], mrow[:, v % 2, :], 1.0, None, ALU.add))
                        dve.wait_ge(*at("small_loaded", 14))
                        link(dve, dve.tensor_tensor(mrow[:, v % 2, :], mrow[:, v % 2, :], gain_f, ALU.mult), "mod_row", v)

                def wuk_turned():
                    dve.wait_ge(*at("wuk_turned", 0))
                    link(dve, dve.tensor_copy(wukT[:, :, :], g4(psum["X0"])), "wuk_ready", 0)

                for v in range(2):
                    modulation(v)
                wuk_turned()
                for half in range(2):
                    for t in range(4 * half, 4 * half + 4):
                        dve.wait_ge(*at("x_squares", t))
                        link(dve, dve.tensor_scalar(st[:, 8 + t:9 + t], st[:, t:t + 1], 1.0 / D, NORM_EPS, ALU.mult, ALU.add), "x_var", t)
                        dve.wait_ge(*at("x_rstd", t))
                        link(dve, dve.tensor_scalar(xin[:, t % 4, :], xin[:, t % 4, :], st[:, 16 + t:17 + t], None, ALU.mult), "xn_ready", t)
                for t in range(NT):
                    dve.wait_ge(*at("rows_done", t))
                    link(dve, dve.tensor_copy(rowp[:, t, :], psum[f"T{t % 2}"][:, 0:NROW]), "rows_ready", t)
                dve.wait_ge(*at("kv_sq", NT - 1, 1))
                step(dve.tensor_scalar(kv_var[:, 0:NT], kv_sum[:, 0, :], 1.0 / LATENT, NORM_EPS, ALU.mult, ALU.add))
                link(dve, dve.tensor_scalar(kv_var[:, NT:], kv_sum[:, 1, :], 1.0 / CHUNK, NORM_EPS, ALU.mult, ALU.add), "kv_var", 0)
                dve.wait_ge(*at("kv_rs", 0))
                for t in range(NT):
                    step(dve.scalar_tensor_tensor(out=ckv_all[:, t, :], in0=rowp[:, t, 0:LATENT], scalar=kv_rs[:, t:t + 1],
                                                  in1=r_kvg[:, 0:LATENT], op0=ALU.mult, op1=ALU.mult))
                    for j in range(2):
                        link(dve, dve.scalar_tensor_tensor(out=ki_twice[:, t, CHUNK * j:CHUNK * j + CHUNK], in0=rowp[:, t, LATENT:LATENT + CHUNK],
                                                           scalar=kv_rs[:, NT + t:NT + t + 1], in1=r_kvg[:, LATENT:], op0=ALU.mult, op1=ALU.mult), "kv_norm", t, j)
                for i in range(4):
                    dve.wait_ge(*at("kv_turned", i))
                    link(dve, dve.tensor_copy((ckvT, kiT)[i // 2][:, 512 * (i % 2):512 * (i % 2) + 512], psum[f"T{i % 2}"]), "kv_T", i)
                for v in range(2, 8):
                    modulation(v)

            @block.tensor
            def _(pe):
                def ada(v):
                    fill(pe, f"W{v % 2}", "row", v)
                    for n in (2 * v, 2 * v + 1):
                        pe.wait_ge(*at(f"slot_loaded{place[('ada', n)] % 4}", place[("ada", n)]))
                    for k in range(KD):
                        for h in range(2):
                            mm = pe.matmul(psum[f"W{v % 2}"][64 * h:64 * h + 64, :], cB[:, k, 0:64], slots[place[("ada", 2 * v + h)] % 4][:, k, :],
                                           start=(k == 0), stop=(k == KD - 1))
                    mm.then_inc(*sig("ada_done", v))
                    if v in (0, 1, 3, 4):
                        pe.wait_ge(*at("mod_row", v))
                        fill(pe, "T0", "mod_cols", v)
                        for j in range(4):
                            mm = pe.transpose(g4(psum["T0"])[:, j, :], mrow[:, v % 2, P * j:P * j + P], ident[:, :])
                        mm.then_inc(*sig("cols_turned", v))

                pe.wait_ge(*at("c_ready", 0))
                pe.wait_ge(*at("ident_ready", 0))
                for v in range(2):
                    ada(v)
                pe.wait_ge(*at("small_loaded", 14))
                fill(pe, "X0", "wuk_ready", 0)
                for p in range(NPAIR):
                    mm = pe.transpose(psum["X0"][:, P * p:P * p + P], wuk_sb[:, P * p:P * p + P], ident[:, :])
                mm.then_inc(*sig("wuk_turned", 0))
                for half in range(2):
                    for t in range(4 * half, 4 * half + 4):
                        pe.wait_ge(*at("xn_ready", t))
                    for k in range(KD):
                        fill(pe, f"T{k % 2}", "h_ready", half, k)
                        for j in range(4):
                            mm = pe.transpose(psum[f"T{k % 2}"][:, P * j:P * j + P], xin[:, j, P * k:P * k + P], ident[:, :])
                        mm.then_inc(*sig("x_turned_bank", half, k))
                i = 0
                for g, (col, width, tiles) in enumerate(W_GROUPS):
                    slot_n = place[("win", g)]
                    w = slots[slot_n % 4]
                    pe.wait_ge(*at(f"slot_loaded{slot_n % 4}", slot_n))
                    for n, ct in enumerate(tiles):
                        first = P * n + (LATENT if g == 0 else 0)
                        for half in range(2):
                            pe.wait_ge(*at("h_ready", half, KD - 1))
                            b = out_bank[i % 4]
                            fill(pe, b, "staged", i)
                            for k in range(KD):
                                mm = pe.matmul(psum[b], w[:, k, first:first + P], hT[:, k, 512 * half:512 * half + 512],
                                               start=(k == 0), stop=(k == KD - 1))
                            mm.then_inc(*sig("projected", i))
                            i += 1
                    if g == 0:
                        for t in range(NT):
                            b = f"T{t % 2}"
                            fill(pe, b, "rows_ready", t)
                            for k in range(KD):
                                pe.matmul(psum[b][:, 0:LATENT], hT[:, k, P * t:P * t + P], w[:, k, 0:LATENT],
                                          start=(k == 0), stop=(k == KD - 1))
                            for k in range(KD):
                                mm = pe.matmul(psum[b][:, LATENT:NROW], hT[:, k, P * t:P * t + P], w[:, k, LATENT + 256:452],
                                               start=(k == 0), stop=(k == KD - 1))
                            mm.then_inc(*sig("rows_done", t))
                pe.wait_ge(*at("kv_norm", NT - 1, 1))
                for i in range(4):
                    fill(pe, f"T{i % 2}", "kv_T", i)
                    for t in range(4 * (i % 2), 4 * (i % 2) + 4):
                        mm = pe.transpose(g4(psum[f"T{i % 2}"])[:, t % 4, :], (ckv_all, ki_twice)[i // 2][:, t, :], ident[:, :])
                    mm.then_inc(*sig("kv_turned", i))
                for v in range(2, 8):
                    ada(v)

        with ExitStack() as scope:
            S.phase(nc, scope, "mix")
            A = Arena(arena_t, ARENA)
            raw = A.take(NRW, P + 1)
            pm = A.take(NRW, P)
            qiBD, qBD = A.take(2, 2, P), A.take(NPAIR, 2, P)
            lo, gsig, grow = A.take(P), A.take(P), A.take(RW)
            sgd, cum, invE, av, kkr, kmod, rnb = (A.take(RW) for _ in range(7))
            dx = A.take(NH, CHUNK + 1)
            natA, natR, natB, natK = (A.take(NPAIR, P) for _ in range(4))
            ARbd, Bbd = A.take(NPAIR, 2, 2, P), A.take(NPAIR, 2, P)
            R, V0 = A.take(NH, P), A.take(NH, P)
            Bc, Kc = A.take(NPAIR, 2, P), A.take(NPAIR, 2, P)
            AbT, AkT = A.take(NH, 2, P), A.take(NH, 2, P)
            AA, T, Tt, Xs = (A.take(NH, P) for _ in range(4))
            W = A.take(2, NH, CHUNK)
            G1, Y0, GT = A.take(RW), A.take(RW), A.take(NPAIR, P)
            yb, yc = A.take(RW), A.take(RW)
            mixT, qlT, olT = A.take(KD, P), A.take(NH, P), A.take(NH, P)
            score, keyed = A.take(SEQ), A.take(SEQ)
            smask, junk = (A.take(SEQ // 2).bitcast(BF16) for _ in range(2))
            lg = A.take(2, SEQ)
            PT = A.take(NT, 2, P)
            s_sum, s_dec, s_neg, s_sgn, s_lim, s_lim_e, s_q, s_v, s_need = (st[:, i:i + 1] for i in (23, *range(88, 96)))
            s_step = st[:, 0:MANTISSA]
            exp_i = A.take(2).bitcast(I32)
            keyed_i = keyed.bitcast(I32)
            hats = Xs.rearrange("p a b -> p (a b)")
            hatB, hatK = hats[:, 0:RW], hats[:, RW:2 * RW]
            late = AbT.rearrange("p a b c -> p (a b c)")
            MT = late[:, 0:1024].rearrange("p (a b c) -> p a b c", a=NPAIR, b=2)
            Cs = late[:, 1024:2048].rearrange("p (a b c) -> p a b c", a=NPAIR, b=2)
            s_mx, s_gn, s_kk = st[:, 40:48], st[:, 48:72], st[:, 72:88]
            s_bon = (st[:, 24:32], st[:, 32:40])
            tile = lambda t: slice(P * t, P * t + P)
            block = scope.enter_context(nc.Block())

            def pt_bank(t, h, j):
                return f"T{(h * (t // 4 + 1) + j) % 2}"

            @block.sync
            def _(sp):
                def load_rwkv(t):
                    if t:
                        sp.wait_ge(*at("mixed", t - 1))
                    first = P * t - 1 if t else 0
                    sp.dma_start(raw[:, :, (0 if t else 1):P + 1], p_d[0:NRW, :, first:P * t + P].rearrange("c p s -> p c s"))\
                        .then_inc(*sig("raw_loaded", t, by=16))
                    if t >= 2:
                        if t > 2:
                            sp.wait_ge(*at("idx_done", t - 1, IDX_HEADS - 1))
                        else:
                            sp.wait_ge(*at("bd_zero", 0))
                        for h in range(2):
                            half = slice(64 * h, 64 * h + 64)
                            sp.dma_start(qiBD[half, :, h, :], p_d[18:20, half, tile(t)].rearrange("c p s -> p c s")).then_inc(*sig("qi_loaded", t, h, by=16))

                def load_queries(t):
                    if t:
                        sp.wait_ge(*at("qlat_done", t - 1, 1))
                    else:
                        sp.wait_ge(*at("bd_zero", 0))
                    for h in range(2):
                        half = slice(64 * h, 64 * h + 64)
                        sp.dma_start(qBD[half, :, h, :], p_d[14:18, half, tile(t)].rearrange("c p s -> p c s")).then_inc(*sig("q_loaded", t, h, by=16))

                load_rwkv(0)
                load_queries(0)
                for t in range(NT + 1):
                    if t + 1 < NT:
                        load_rwkv(t + 1)
                    if 1 <= t < NT:
                        load_queries(t)
                    if t < NT:
                        sp.wait_ge(*at("mix_rwkv", t))
                        sp.dma_start(mix_d[0:4, :, tile(t)].rearrange("c p s -> p c s"), mixT[:, 0:4, :]).then_inc(*sig("rwkv_stored", t, by=16))
                    if t:
                        sp.wait_ge(*at("mix_dsa", t - 1))
                        sp.dma_start(mix_d[4:8, :, tile(t - 1)].rearrange("c p s -> p c s"), mixT[:, 4:8, :]).then_inc(*sig("dsa_stored", t - 1, by=16))
                sp.wait_ge(*at("rwkv_stored", NT - 1))
                sp.wait_ge(*at("dsa_stored", NT - 1))

            @block.gpsimd
            def _(pool):
                def step(ins):
                    link(pool, ins, "pool_step")

                def power(dst, src, n, name, *key):
                    link(pool, pool.tensor_tensor(dst, src, mhalf[:, 0:n], ALU.pow), name, *key)

                for ap in (qiBD, ARbd, Bbd, V0, Bc, Kc):
                    step(pool.memset(ap, 0.0))
                step(pool.memset(dx, 1.0))
                step(pool.memset(raw[:, :, 0:1], 0.0))
                link(pool, pool.memset(qBD, 0.0), "bd_zero", 0)
                def prepare(t):
                    pool.wait_ge(*at("raw_loaded", t))
                    if t:
                        pool.wait_ge(*at("nat_b", t - 1))
                        pool.wait_ge(*at("v_turned", t - 1))
                    step(pool.tensor_tensor(pm, raw[:, :, 0:P], raw[:, :, 1:P + 1], ALU.subtract))
                    step(pool.tensor_tensor(pm, pm, over(c_mu, P), ALU.mult))
                    link(pool, pool.tensor_tensor(pm, pm, raw[:, :, 1:P + 1], ALU.add), "mixed", t)
                    link(pool, pool.tensor_tensor(g4(kkr), pm[:, 4:8, :], over(c_kk, P), ALU.mult), "kkr", t)
                    pool.wait_ge(*at("kk_var", t))
                    power(s_kk[:, 8:16], s_kk[:, 0:8], 8, "kk_rs", t)

                prepare(0)
                for t in range(NT):
                    pool.wait_ge(*at("nat_b", t))
                    for h in range(2):
                        half = slice(64 * h, 64 * h + 64)
                        link(pool, pool.tensor_copy(Bbd[half, :, h, :], natB[half, :, :]), "b_bd", t, h)
                    if t + 1 < NT:
                        prepare(t + 1)
                    pool.wait_ge(*at("y_var", t))
                    power(s_gn[:, 16:24], s_gn[:, 8:16], 8, "y_rs", t)

            @block.scalar
            def _(act):
                def step(ins):
                    link(act, ins, "act_step")

                def search(t):
                    n = P * (t + 1)

                    def weigh(src, scale, limit, more, step_scale=None):
                        step(act.activation(junk[:, 0:n], src[:, 0:n], ACT.Sign, scale=scale, bias=s_neg, accum_out=s_sum))
                        step(act.activation(s_dec, s_sum, ACT.Sign, bias=limit))
                        if more:
                            step(act.activation(s_neg, s_dec, ACT.Identity, scale=step_scale, bias=s_neg))

                    act.wait_ge(*at("score_ready", t))
                    link(act, act.activation(junk[:, 0:n], score[:, 0:n], ACT.Sign, accum_out=s_sum), "sign_sum", t)
                    yield
                    act.wait_ge(*at("exponents", t))
                    for k in range(7, -1, -1):
                        weigh(keyed_i, 1.0, s_lim_e, k > 0, -float(2.0 ** (k - 1)))
                        if k == 0:
                            link(act, act.activation(s_sum, s_dec, ACT.Copy), "exponent_found", t)
                        yield
                    act.wait_ge(*at("mantissa", t))
                    for k in range(1, MANTISSA + 1):
                        weigh(score, s_sgn, s_lim, k < MANTISSA, s_step[:, k:k + 1] if k < MANTISSA else None)
                        if k == MANTISSA:
                            link(act, act.activation(s_sum, s_dec, ACT.Copy), "searched", t)
                        yield

                def attention(t):
                    n = P * (t + 1)
                    for g in range(2):
                        act.wait_ge(*at("qlat_done", t, g))
                        link(act, act.activation(qlT[:, 4 * g:4 * g + 4, :], g4(psum[f"X{g}"]), ACT.Copy, scale=HEAD ** -0.5), "qlat", t, g)
                    yield
                    for h in range(NH + 2):
                        if h < NH:
                            act.wait_ge(*at("logits", t, h))
                            link(act, act.activation(lg[:, h % 2, 0:n], lg[:, h % 2, 0:n], ACT.Exp, bias=s_mx[:, 2 * (h % 2) + 1:2 * (h % 2) + 2],
                                                     accum_out=s_mx[:, 4 + h % 2:5 + h % 2]), "exps", t, h)
                        if h >= 3 and h % 2:
                            act.wait_ge(*at("pv_done", t, h - 3))
                            link(act, act.activation(olT[:, h - 3:h - 1, :], g4(psum["P0"])[:, 0:2, :], ACT.Copy), "o_lat", t, h - 3)
                        if 1 <= h <= NH:
                            for j in range(t // 4 + 1):
                                m = min(4, t + 1 - 4 * j)
                                act.wait_ge(*at("pt_turned", t, h - 1, j))
                                link(act, act.activation(PT[:, 4 * j:4 * j + m, (h - 1) % 2, :], g4(psum[pt_bank(t, h - 1, j)])[:, 0:m, :], ACT.Copy), "probs_T", t, h - 1, j)
                        yield
                    act.wait_ge(*at("uv_done", t))
                    if t:
                        act.wait_ge(*at("dsa_stored", t - 1))
                    link(act, act.activation(mixT[:, 4:8, :], g4(psum["T1"]), ACT.Copy), "mix_dsa", t)

                def prepare(t):
                    act.wait_ge(*at("mixed", t))
                    step(act.activation(lo[0:64, :], pm[0:64, 12, :], ACT.Tanh))
                    step(act.activation(lo[64:128, :], pm[64:128, 12, :], ACT.Copy))
                    link(act, act.activation(gsig, pm[:, 13, :], ACT.Tanh, scale=0.5), "lora_in", t)
                    act.wait_ge(*at("kkr", t))
                    link(act, act.activation(rnb, kkr, ACT.Square), "kk_sq", t)
                    yield
                    if t == 0:
                        act.wait_ge(*at("offsets_halved", 0))
                    act.wait_ge(*at("zdec_done", t))
                    for p in range(NPAIR):
                        link(act, act.activation(g4(sgd)[:, p, :], g4(psum["X0"])[:, p, :], ACT.Tanh, scale=0.5, bias=c_w0[:, p:p + 1]), "dec_tanh", t, p)
                    act.wait_ge(*at("zaaa_done", t))
                    for p in range(NPAIR):
                        link(act, act.activation(g4(av)[:, p, :], g4(psum["X1"])[:, p, :], ACT.Tanh, scale=0.5, bias=c_a0[:, p:p + 1]), "aaa_tanh", t, p)
                    yield

                def index_relu(t, first, end):
                    n = P * (t + 1)
                    if t >= 2:
                        for h in range(first, end):
                            act.wait_ge(*at("idx_done", t, h))
                            if h >= 2:
                                act.wait_ge(*at("scored", t, h - 2))
                            else:
                                act.wait_ge(*at("pt_turned", t - 2, 6 + h, (t - 2) // 4))
                            link(act, act.activation(lg[:, h % 2, 0:n], psum["XW"[h % 2]][:, 0:n], ACT.Relu), "relu", t, h)

                def decays(t):
                    act.wait_ge(*at("cum", t))
                    if t:
                        act.wait_ge(*at("y_var", t - 1))
                    step(act.activation(dx[:, :, 1:CHUNK + 1], cum.rearrange("p (a b) -> p a b", b=CHUNK), ACT.Exp, scale=-DECAY))
                    link(act, act.activation(invE, cum, ACT.Exp, scale=DECAY), "decays", t)

                for _ in prepare(0):
                    pass
                decays(0)
                for t in range(NT):
                    n = P * (t + 1)
                    turns = attention(t - 1) if t else iter(())
                    ahead = prepare(t + 1) if t + 1 < NT else iter(())
                    act.wait_ge(*at("nat_r", t))
                    for h in range(2):
                        half = slice(64 * h, 64 * h + 64)
                        link(act, act.activation(ARbd[half, :, h, 0, :], natA[half, :, :], ACT.Copy), "ar_bd", t, h, 0)
                        link(act, act.activation(ARbd[half, :, h, 1, :], natR[half, :, :], ACT.Copy), "ar_bd", t, h, 1)
                    index_relu(t, 2, 4)
                    next(turns, None)
                    seek = search(t) if t >= 2 else iter(())

                    def some(count):
                        for _ in range(count):
                            next(seek, None)

                    some(1)
                    act.wait_ge(*at("g_done", t))
                    if t:
                        act.wait_ge(*at("y_out", t - 1))
                    link(act, act.activation(grow, psum["W0"], ACT.Copy), "g_rows", t)
                    next(turns, None)
                    act.wait_ge(*at("v_turned", t))
                    link(act, act.activation(V0[:, :, CHUNK:], g8(psum["T0"]), ACT.Copy), "v_rows", t)
                    act.wait_ge(*at("a_turned", t))
                    link(act, act.activation(R[:, :, 0:CHUNK], g8(psum["T1"]), ACT.Copy), "a_rows", t)
                    act.wait_ge(*at("b_turned", t))
                    for h in range(2):
                        half = slice(64 * h, 64 * h + 64)
                        link(act, act.activation(Bc[half, :, h, :], g4(psum["T0"])[half], ACT.Copy), "b_rows", t, h)
                    act.wait_ge(*at("k_turned", t))
                    for h in range(2):
                        half = slice(64 * h, 64 * h + 64)
                        link(act, act.activation(Kc[half, :, h, :], g4(psum["T1"])[half], ACT.Copy), "k_rows", t, h)
                    next(turns, None)
                    some(8)
                    for l in range(LEVELS - 1):
                        next(turns, None)
                        if l == 0:
                            for g in range(2):
                                act.wait_ge(*at("av_done", t, g))
                                link(act, act.activation(R[:, 4 * g:4 * g + 4, CHUNK:], g4(psum[f"W{g}"])[:, :, CHUNK:], ACT.Copy), "av_rows", t, g)
                        some(SEARCH[l])
                        if l in (1, 2):
                            next(ahead, None)
                    next(turns, None)
                    for g in range(2):
                        act.wait_ge(*at("w_done", t, g))
                        link(act, act.activation(W[:, :, 4 * g:4 * g + 4, :].rearrange("p w h i -> p h w i"),
                                                 psum[f"X{g}"].rearrange("p (h w i) -> p h w i", h=4, w=2), ACT.Copy), "w_rows", t, g)
                    for g in range(2):
                        act.wait_ge(*at("y0_done", t, g))
                        src = psum[f"W{g}"].rearrange("p (h w i) -> p h w i", h=4, w=2)
                        step(act.activation(g8(G1)[:, 4 * g:4 * g + 4, :], src[:, :, 0, :], ACT.Copy))
                        link(act, act.activation(g8(Y0)[:, 4 * g:4 * g + 4, :], src[:, :, 1, :], ACT.Copy), "y0_rows", t, g)
                    next(turns, None)
                    next(turns, None)
                    act.wait_ge(*at("y_centred", t))
                    link(act, act.activation(invE, yc, ACT.Square), "y_sq", t)
                    if t + 1 < NT:
                        decays(t + 1)
                        index_relu(t + 1, 0, 2)
                    act.wait_ge(*at("y_turned", t))
                    if t:
                        act.wait_ge(*at("rwkv_stored", t - 1))
                    link(act, act.activation(mixT[:, 0:4, :], g4(psum["T0"]), ACT.Copy), "mix_rwkv", t)
                    next(turns, None)
                for _ in attention(NT - 1):
                    pass

            @block.vector
            def _(dve):
                def step(ins):
                    link(dve, ins, "dve_step")

                def top_k(t):
                    n = P * (t + 1)
                    odds = float(n - 2 * TOPK)
                    dve.wait_ge(*at("sign_sum", t))
                    step(dve.tensor_scalar(s_sgn, s_sum, -(odds + 1.5), 2.0, ALU.is_gt, ALU.mult))
                    step(dve.tensor_scalar(s_sgn, s_sgn, -1.0, None, ALU.add))
                    step(dve.tensor_scalar(s_lim, s_sgn, odds + 1.5, None, ALU.mult))
                    step(dve.tensor_scalar(s_lim_e, s_sgn, odds + 1.0, None, ALU.mult))
                    step(dve.memset(s_neg, -127.5))
                    step(dve.tensor_scalar(keyed[:, 0:n], score[:, 0:n], s_sgn, 0.0, ALU.mult, ALU.max))
                    link(dve, dve.tensor_scalar(keyed_i[:, 0:n], keyed_i[:, 0:n], 23, None, ALU.logical_shift_right), "exponents", t)
                    yield
                    dve.wait_ge(*at("exponent_found", t))
                    step(dve.scalar_tensor_tensor(out=s_q, in0=s_sum, scalar=0.5, in1=s_neg, op0=ALU.mult, op1=ALU.subtract))
                    step(dve.tensor_copy(exp_i[:, 0:1], s_q))
                    step(dve.tensor_scalar(exp_i[:, 1:2], exp_i[:, 0:1], 23, None, ALU.logical_shift_left))
                    q = exp_i[:, 1:2].bitcast(F32)
                    step(dve.tensor_scalar(s_step, halves[:, :], q, None, ALU.mult))
                    link(dve, dve.tensor_tensor(s_neg, s_step[:, 0:1], q, ALU.subtract), "mantissa", t)
                    yield
                    dve.wait_ge(*at("searched", t))
                    step(dve.tensor_scalar(s_q, s_sum, -1.0, -0.5, ALU.add, ALU.mult))
                    step(dve.scalar_tensor_tensor(out=s_v, in0=s_q, scalar=s_step[:, MANTISSA - 1:], in1=s_neg, op0=ALU.mult, op1=ALU.subtract))
                    step(dve.tensor_scalar(keyed[:, 0:n], score[:, 0:n], s_sgn, None, ALU.mult))
                    step(dve.tensor_scalar(smask[:, 0:n], keyed[:, 0:n], s_v, BEYOND, ALU.is_lt, ALU.mult))
                    step(dve.tensor_tensor_reduce(keyed[:, 0:n], keyed[:, 0:n], smask[:, 0:n], 1.0, BEYOND, ALU.add, ALU.min, s_q))
                    step(dve.tensor_tensor(s_v, s_q, s_sgn, ALU.mult))
                    step(dve.tensor_scalar(keyed[:, 0:n], score[:, 0:n], s_v, None, ALU.is_gt))
                    step(dve.tensor_reduce(s_q, keyed[:, 0:n], AX_X, ALU.add))
                    step(dve.tensor_scalar(s_need, s_q, -1.0, float(TOPK), ALU.mult, ALU.add))
                    step(dve.tensor_scalar(smask[:, 0:n], score[:, 0:n], s_v, None, ALU.is_equal))
                    step(dve.tensor_tensor_scan(score[:, 0:n], ones[:, 0:1].to_broadcast([P, n]), smask[:, 0:n], 0.0, ALU.mult, ALU.add))
                    step(dve.scalar_tensor_tensor(out=smask[:, 0:n], in0=score[:, 0:n], scalar=s_need, in1=smask[:, 0:n], op0=ALU.is_le, op1=ALU.mult))
                    step(dve.tensor_tensor(keyed[:, 0:n], keyed[:, 0:n], smask[:, 0:n], ALU.add))
                    link(dve, dve.tensor_scalar(smask[:, 0:n], keyed[:, 0:n], 0.0, NEG, ALU.is_equal, ALU.mult), "selected", t)

                def attention(t):
                    n = P * (t + 1)
                    mask = smask[:, 0:n] if t >= 2 else causal[:, 256 - n:256]
                    for h in range(NH + 1):
                        if h < NH:
                            mx, nmx = s_mx[:, 2 * (h % 2):2 * (h % 2) + 1], s_mx[:, 2 * (h % 2) + 1:2 * (h % 2) + 2]
                            if h >= 2:
                                dve.wait_ge(*at("pt_turned", t, h - 2, t // 4))
                            elif t:
                                dve.wait_ge(*at("pt_turned", t - 1, 6 + h, (t - 1) // 4))
                            dve.wait_ge(*at("lg_done", t, h))
                            link(dve, dve.tensor_tensor_reduce(lg[:, h % 2, 0:n], psum["P"][:, 0:n], mask, 1.0, MASKED, ALU.add, ALU.max, mx), "lg_masked", t, h)
                            link(dve, dve.tensor_scalar(nmx, mx, -1.0, None, ALU.mult), "logits", t, h)
                        if h:
                            b = (h - 1) % 2
                            sm, rs = s_mx[:, 4 + b:5 + b], s_mx[:, 6 + b:7 + b]
                            dve.wait_ge(*at("exps", t, h - 1))
                            step(dve.reciprocal(rs, sm))
                            link(dve, dve.tensor_scalar(lg[:, b, 0:n], lg[:, b, 0:n], rs, None, ALU.mult), "probs", t, h - 1)
                        yield

                link(dve, dve.tensor_scalar(cols[:, 14:22], cols[:, 14:22], 0.5, None, ALU.mult), "offsets_halved", 0)
                def prepare(t):
                    dve.wait_ge(*at("lora_in", t))
                    link(dve, dve.tensor_scalar(gsig, gsig, 0.5, 0.5, ALU.mult, ALU.add), "g_sig", t)
                    dve.wait_ge(*at("kk_ss", t))
                    link(dve, dve.tensor_scalar(s_kk[:, 0:8], psum["W1"][:, 0:8], 1e-24, None, ALU.max), "kk_var", t)
                    yield
                    dve.wait_ge(*at("dec_tanh", t, NPAIR - 1))
                    step(dve.tensor_scalar(sgd, sgd, 0.5, 0.5, ALU.mult, ALU.add))
                    link(dve, dve.tensor_tensor_scan(cum, scan_reset[:, :], sgd, 0.0, ALU.mult, ALU.add), "cum", t)
                    dve.wait_ge(*at("aaa_tanh", t, NPAIR - 1))
                    step(dve.tensor_scalar(av, av, 0.5, 0.5, ALU.mult, ALU.add))
                    step(dve.scalar_tensor_tensor(out=g4(kmod), in0=g4(av), scalar=-1.0, in1=over(c_ka, P), op0=ALU.add, op1=ALU.mult))
                    step(dve.scalar_tensor_tensor(out=g4(kmod), in0=g4(kmod), scalar=1.0, in1=pm[:, 4:8, :], op0=ALU.add, op1=ALU.mult))
                    dve.wait_ge(*at("kk_rs", t))
                    link(dve, dve.tensor_copy(g8(rnb), over(s_kk[:, 8:16], HEAD)), "kk_rs_wide", t)
                    step(dve.tensor_tensor(g4(sgd), pm[:, 0:4, :], g4(kmod), ALU.mult))
                    link(dve, dve.tensor_tensor(g4(sgd), g4(sgd), over(c_rk, P), ALU.mult), "bonus", t)
                    yield
                    dve.wait_ge(*at("kk_spread", t))
                    link(dve, dve.tensor_tensor(kkr, kkr, psum["T1"], ALU.mult), "kk", t)
                    dve.wait_ge(*at("bonus_done", t))
                    link(dve, dve.tensor_copy(s_bon[t % 2], psum["W1"][:, 0:8]), "bonus_rows", t)
                    yield

                for _ in prepare(0):
                    pass
                pending = iter(())
                for t in range(NT):
                    n = P * (t + 1)
                    turns = attention(t - 1) if t else iter(())
                    ahead = prepare(t + 1) if t + 1 < NT else iter(())
                    dve.wait_ge(*at("decays", t))
                    E = dx.rearrange("p (a c) i -> p a c i", a=NPAIR)
                    by_chunk = lambda ap: ap.rearrange("p a (c i) -> p a c i", c=2)
                    by8 = lambda ap: ap.rearrange("p a (c i) -> p (a c) i", c=2)
                    step(dve.scalar_tensor_tensor(out=by8(natA), in0=by8(g4(kkr)), scalar=-1.0, in1=dx[:, :, 0:CHUNK], op0=ALU.mult, op1=ALU.mult))
                    link(dve, dve.tensor_tensor(by8(natR), by8(pm[:, 0:4, :]), dx[:, :, 1:], ALU.mult), "nat_r", t)
                    step(dve.tensor_tensor(kkr, kkr, av, ALU.mult))
                    link(dve, dve.tensor_tensor(natB, g4(kkr), g4(invE), ALU.mult), "nat_b", t)
                    link(dve, dve.tensor_tensor(natK, g4(kmod), g4(invE), ALU.mult), "nat_k", t)
                    whole = dx[:, :, CHUNK:CHUNK + 1].to_broadcast([P, NH, CHUNK])
                    link(dve, dve.tensor_tensor(g8(hatB), by8(natB), whole, ALU.mult), "hat_b", t)
                    link(dve, dve.tensor_tensor(g8(hatK), by8(natK), whole, ALU.mult), "hat_k", t)
                    pending = iter(())
                    if t >= 2:
                        step(dve.tensor_scalar(s_gn[:, 0:4], rowp[:, t, LATENT + CHUNK:NROW], 1.0 / 16, None, ALU.mult))
                        for h in range(IDX_HEADS):
                            dve.wait_ge(*at("relu", t, h))
                            if h == 0:
                                ins = dve.tensor_scalar(score[:, 0:n], lg[:, 0, 0:n], s_gn[:, 0:1], None, ALU.mult)
                            else:
                                ins = dve.scalar_tensor_tensor(out=score[:, 0:n], in0=lg[:, h % 2, 0:n], scalar=s_gn[:, h:h + 1],
                                                               in1=score[:, 0:n], op0=ALU.mult, op1=ALU.add)
                            link(dve, ins, "scored", t, h)
                        link(dve, dve.memset(score[0:CHUNK, n - CHUNK:n], INADMISSIBLE), "score_ready", t)
                        pending = top_k(t)

                    next(turns, None)
                    next(turns, None)
                    next(pending, None)
                    for p in range(NPAIR):
                        masks = m_pair[:, :, :].unsqueeze(1).to_broadcast([P, 2, 2, P])
                        for done, dst, ready, b in (("ab_done", AbT, "ab", "X0"), ("ak_done", AkT, "ak", "X1")):
                            dve.wait_ge(*at(done, t, p))
                            link(dve, dve.tensor_tensor(dst[:, 2 * p:2 * p + 2, :, :], psum[b].rearrange("p (h a t) -> p h a t", h=2, a=2), masks, ALU.mult), ready, t, p)
                        if p % 2:
                            dve.wait_ge(*at("aa_done", t, p))
                            link(dve, dve.tensor_tensor(AA[:, 2 * p - 2:2 * p + 2, :], g4(psum[f"W{p // 2}"]), each(m_low[:, :], 4), ALU.mult), "aa", t, p // 2)
                    next(turns, None)
                    next(pending, None)
                    step(dve.tensor_tensor(Tt, AbT[:, :, 0, :], each(m_lvl[:, 0, :], NH), ALU.mult))
                    link(dve, dve.tensor_tensor(Tt, Tt, each(ident[:, :], NH), ALU.add), "tt", t, 0, 1)

                    def turned_inverse(l):
                        for g in range(2):
                            dve.wait_ge(*at("t_turned", t, l, g))
                            link(dve, dve.tensor_copy(T[:, 4 * g:4 * g + 4, :], g4(psum[f"T{g}"])), "t_inv", t, l, g)

                    turned_inverse(0)
                    for l in range(1, LEVELS):
                        for g in range(2):
                            dve.wait_ge(*at("x_done", t, l, g))
                            link(dve, dve.tensor_tensor(Xs[:, 4 * g:4 * g + 4, :], g4(psum[f"X{g}"]), each(m_lvl[:, l, :], 4), ALU.mult), "xs", t, l, g)
                        next(turns, None)
                        for g in range(2):
                            dve.wait_ge(*at("txa_done", t, l, g))
                            link(dve, dve.tensor_tensor(Tt[:, 4 * g:4 * g + 4, :], Tt[:, 4 * g:4 * g + 4, :], g4(psum[f"W{g}"]), ALU.add), "tt", t, l, g)
                        if l < LEVELS - 1:
                            turned_inverse(l)
                        if l >= 2:
                            next(ahead, None)
                    next(pending, None)
                    dve.wait_ge(*at("g_turned", t))
                    link(dve, dve.tensor_tensor(GT, g4(psum["T0"]), natR, ALU.add), "gt", t)
                    next(turns, None)
                    for g in range(2):
                        dve.wait_ge(*at("m_done", t, g))
                        link(dve, dve.tensor_tensor(MT[:, 2 * g:2 * g + 2].rearrange("p a c j -> p (a c) j"), g4(psum[f"X{g}"]), each(m_bd[:, :], 4), ALU.mult), "m_bd", t, g)
                    for i in range(2 * NPAIR):
                        m_i = MT[:, i // 2, i % 2, :]
                        ins = dve.scalar_tensor_tensor(out=m_i, in0=ident[:, :], scalar=dx[:, i, CHUNK:CHUNK + 1], in1=m_i, op0=ALU.mult, op1=ALU.add)
                    link(dve, ins, "m", t)
                    for g in range(2):
                        dve.wait_ge(*at("c_done", t, g))
                        link(dve, dve.tensor_tensor(Cs[:, 2 * g:2 * g + 2].rearrange("p a c j -> p (a c) j"), g4(psum[f"W{g}"]), each(m_bd[:, :], 4), ALU.mult), "c", t, g)
                    for c_ in range(2):
                        dve.wait_ge(*at("z_done", t, c_))
                        link(dve, dve.tensor_tensor(Z[:, 1 - c_, :, :], g4(psum["X0"]), Cs[:, :, c_, :], ALU.add), "z", t, c_)
                    dve.wait_ge(*at("y_done", t))
                    dve.wait_ge(*at("y0_rows", t, 1))
                    link(dve, dve.tensor_tensor(yb, psum["P1"], Y0, ALU.add), "y", t)
                    step(dve.tensor_reduce(s_gn[:, 0:8], g8(yb), AX_X, ALU.add))
                    step(dve.tensor_scalar(s_gn[:, 0:8], s_gn[:, 0:8], 1.0 / HEAD, None, ALU.mult))
                    link(dve, dve.tensor_tensor(g8(yc), g8(yb), over(s_gn[:, 0:8], HEAD), ALU.subtract), "y_centred", t)
                    dve.wait_ge(*at("y_sq", t))
                    step(dve.tensor_reduce(s_gn[:, 0:8], g8(invE), AX_X, ALU.add))
                    link(dve, dve.tensor_scalar(s_gn[:, 8:16], s_gn[:, 0:8], 1.0 / HEAD, GN_EPS, ALU.mult, ALU.add), "y_var", t)
                    dve.wait_ge(*at("y_rs", t))
                    step(dve.tensor_tensor(g8(yc), g8(yc), over(s_gn[:, 16:24], HEAD), ALU.mult))
                    step(dve.tensor_tensor(yc, yc, r_gng[:, :], ALU.mult))
                    step(dve.tensor_tensor(yc, yc, r_gnb[:, :], ALU.add))
                    step(dve.tensor_tensor(g8(yb), V0[:, :, CHUNK:], over(s_bon[t % 2], HEAD), ALU.mult))
                    step(dve.tensor_tensor(yc, yc, yb, ALU.add))
                    link(dve, dve.tensor_tensor(yc, yc, grow, ALU.mult), "y_out", t)
                for _ in attention(NT - 1):
                    pass

            @block.tensor
            def _(pe):
                def attention(t):
                    n = P * (t + 1)

                    def logits(h):
                        pe.wait_ge(*at("qlat", t, h // 4))
                        for half in range(t // 4 + 1):
                            m = min(512, n - 512 * half)
                            fill(pe, f"P{half}", "lg_masked", t, h)
                            mm = pe.matmul(psum[f"P{half}"][:, 0:m], qlT[:, h, :], ckvT[:, 512 * half:512 * half + m], start=True, stop=True)
                        mm.then_inc(*sig("lg_done", t, h))

                    for h in range(2):
                        pe.wait_ge(*at("q_loaded", t, h))
                    for g in range(2):
                        fill(pe, f"X{g}", "qlat", t, g)
                        for p in range(2 * g, 2 * g + 2):
                            mm = pe.matmul(psum[f"X{g}"][:, 256 * (p % 2):256 * (p % 2) + 256], wukT[:, p, :], qBD[:, p].rearrange("p h t -> p (h t)"), start=True, stop=True)
                        mm.then_inc(*sig("qlat_done", t, g))
                    logits(0)
                    yield
                    for h in range(NH + 2):
                        if h >= 3 and h % 2:
                            pe.wait_ge(*at("probs_T", t, h - 2, t // 4))
                            fill(pe, "P0", "o_lat", t, h - 3)
                            for kt in range(t + 1):
                                mm = pe.matmul(psum["P0"][:, 0:2 * P], ckv_all[:, kt, :], PT[:, kt, :, :].rearrange("p h t -> p (h t)"), start=(kt == 0), stop=(kt == t))
                            mm.then_inc(*sig("pv_done", t, h - 3))
                        if 1 <= h <= NH:
                            pe.wait_ge(*at("probs", t, h - 1))
                            for j in range(t // 4 + 1):
                                b = pt_bank(t, h - 1, j)
                                fill(pe, b, "probs_T", t, h - 1, j)
                                for kt in range(4 * j, min(4 * j + 4, t + 1)):
                                    mm = pe.transpose(g4(psum[b])[:, kt % 4, :], lg[:, (h - 1) % 2, tile(kt)], ident[:, :])
                                mm.then_inc(*sig("pt_turned", t, h - 1, j))
                        if h + 1 < NH:
                            logits(h + 1)
                        yield
                    pe.wait_ge(*at("o_lat", t, NH - 2))
                    fill(pe, "T1", "mix_dsa", t)
                    for h in range(NH):
                        mm = pe.matmul(g4(psum["T1"])[64 * (h % 2):64 * (h % 2) + 64, h // 2, :], wuv[:, HEAD * h:HEAD * h + HEAD], olT[:, h, :], start=True, stop=True)
                    mm.then_inc(*sig("uv_done", t))

                def index_scores(t, first, end):
                    n = P * (t + 1)
                    if t >= 2:
                        for h in range(2):
                            pe.wait_ge(*at("qi_loaded", t, h))
                        for h in range(first, end):
                            pair = "XW"[h % 2]
                            for half in range(t // 4 + 1):
                                fill(pe, f"{pair}{half}", "relu", t, h)
                                m = min(512, n - 512 * half)
                                mm = pe.matmul(psum[f"{pair}{half}"][:, 0:m], qiBD[:, h // 2, h % 2, :], kiT[:, 512 * half:512 * half + m], start=True, stop=True)
                            mm.then_inc(*sig("idx_done", t, h))

                def prepare(t):
                    pe.wait_ge(*at("lora_in", t))
                    fill(pe, "X0", "dec_tanh", t, NPAIR - 1)
                    for p in range(NPAIR):
                        mm = pe.matmul(g4(psum["X0"])[:, p, :], wdec[:, P * p:P * p + P], lo, start=True, stop=True)
                    mm.then_inc(*sig("zdec_done", t))
                    fill(pe, "X1", "aaa_tanh", t, NPAIR - 1)
                    for p in range(NPAIR):
                        mm = pe.matmul(g4(psum["X1"])[:, p, :], waaa[:, P * p:P * p + P], lo, start=True, stop=True)
                    mm.then_inc(*sig("zaaa_done", t))
                    pe.wait_ge(*at("kk_sq", t))
                    fill(pe, "W1", "kk_var", t)
                    for p in range(NPAIR):
                        mm = pe.matmul(psum["W1"][:, 2 * p:2 * p + 2], g4(rnb)[:, p, :], blk2[:, :], start=True, stop=True)
                    mm.then_inc(*sig("kk_ss", t))
                    yield
                    pe.wait_ge(*at("kk_rs_wide", t))
                    fill(pe, "T1", "kk", t)
                    for p in range(NPAIR):
                        mm = pe.matmul(g4(psum["T1"])[:, p, :], g4(rnb)[:, p, :], ident[:, :], start=True, stop=True)
                    mm.then_inc(*sig("kk_spread", t))
                    pe.wait_ge(*at("bonus", t))
                    fill(pe, "W1", "bonus_rows", t)
                    for p in range(NPAIR):
                        mm = pe.matmul(psum["W1"][:, 2 * p:2 * p + 2], g4(sgd)[:, p, :], blk2[:, :], start=True, stop=True)
                    mm.then_inc(*sig("bonus_done", t))
                    yield

                for _ in prepare(0):
                    pass
                for t in range(NT):
                    n = P * (t + 1)
                    turns = attention(t - 1) if t else iter(())
                    ahead = prepare(t + 1) if t + 1 < NT else iter(())
                    index_scores(t, 2, 4)
                    next(turns, None)
                    pe.wait_ge(*at("g_sig", t))
                    fill(pe, "W0", "g_rows", t)
                    pe.matmul(psum["W0"], gsig, wgate[:, :], start=True, stop=True).then_inc(*sig("g_done", t))
                    fill(pe, "T0", "v_rows", t)
                    for p in range(NPAIR):
                        mm = pe.transpose(g4(psum["T0"])[:, p, :], pm[:, 8 + p, :], ident[:, :])
                    mm.then_inc(*sig("v_turned", t))
                    next(turns, None)
                    pe.wait_ge(*at("nat_r", t))
                    fill(pe, "T1", "a_rows", t)
                    for p in range(NPAIR):
                        mm = pe.transpose(g4(psum["T1"])[:, p, :], natA[:, p, :], ident[:, :])
                    mm.then_inc(*sig("a_turned", t))
                    pe.wait_ge(*at("hat_b", t))
                    fill(pe, "T0", "b_rows", t, 1)
                    for p in range(NPAIR):
                        mm = pe.transpose(g4(psum["T0"])[:, p, :], g4(hatB)[:, p, :], ident[:, :])
                    mm.then_inc(*sig("b_turned", t))
                    pe.wait_ge(*at("hat_k", t))
                    fill(pe, "T1", "k_rows", t, 1)
                    for p in range(NPAIR):
                        mm = pe.transpose(g4(psum["T1"])[:, p, :], g4(hatK)[:, p, :], ident[:, :])
                    mm.then_inc(*sig("k_turned", t))
                    next(turns, None)
                    pe.wait_ge(*at("ar_bd", t, 1, 1))
                    pe.wait_ge(*at("b_bd", t, 1))
                    for p in range(NPAIR):
                        both = ARbd[:, p].rearrange("p h a t -> p (h a t)")
                        fill(pe, "X0", "ab", t, p)
                        pe.matmul(psum["X0"], natB[:, p, :], both, start=True, stop=True).then_inc(*sig("ab_done", t, p))
                        fill(pe, "X1", "ak", t, p)
                        pe.matmul(psum["X1"], natK[:, p, :], both, start=True, stop=True).then_inc(*sig("ak_done", t, p))
                        if p % 2 == 0:
                            fill(pe, f"W{p // 2}", "aa", t, p // 2)
                        pe.matmul(psum[f"W{p // 2}"][:, 256 * (p % 2):256 * (p % 2) + 256], natA[:, p, :], Bbd[:, p].rearrange("p h t -> p (h t)"),
                                  start=True, stop=True).then_inc(*sig("aa_done", t, p))
                    pe.wait_ge(*at("v_rows", t))
                    for g in range(2):
                        pe.wait_ge(*at("ak", t, 2 * g + 1))
                        fill(pe, f"W{g}", "av_rows", t, g)
                        for h in range(4 * g, 4 * g + 4):
                            mm = pe.matmul(g4(psum[f"W{g}"])[:, h % 4, :], AkT[:, h, 0, :], V0[:, h, :], start=True, stop=True)
                        mm.then_inc(*sig("av_done", t, g))
                    next(turns, None)

                    def turn_inverse(l):
                        for g in range(2):
                            pe.wait_ge(*at("tt", t, l, g if l else 1))
                            fill(pe, f"T{g}", "t_inv", t, l, g)
                            for h in range(4 * g, 4 * g + 4):
                                mm = pe.transpose(g4(psum[f"T{g}"])[:, h % 4, :], Tt[:, h, :], ident[:, :])
                            mm.then_inc(*sig("t_turned", t, l, g))

                    turn_inverse(0)
                    for l in range(1, LEVELS):
                        for g in range(2):
                            pe.wait_ge(*at("tt", t, l - 1, g if l > 1 else 1))
                            pe.wait_ge(*at("aa", t, g))
                            fill(pe, f"X{g}", "xs", t, l, g)
                            for h in range(4 * g, 4 * g + 4):
                                mm = pe.matmul(g4(psum[f"X{g}"])[:, h % 4, :], AA[:, h, :], Tt[:, h, :], start=True, stop=True)
                            mm.then_inc(*sig("x_done", t, l, g))
                        for g in range(2):
                            pe.wait_ge(*at("xs", t, l, g))
                            pe.wait_ge(*at("t_inv", t, l - 1, g))
                            fill(pe, f"W{g}", "tt", t, l, g)
                            for h in range(4 * g, 4 * g + 4):
                                mm = pe.matmul(g4(psum[f"W{g}"])[:, h % 4, :], T[:, h, :], Xs[:, h, :], start=True, stop=True)
                            mm.then_inc(*sig("txa_done", t, l, g))
                        next(turns, None)
                        if l < LEVELS - 1:
                            turn_inverse(l)
                        if l in (2, 4):
                            next(ahead, None)
                    for g in range(2):
                        pe.wait_ge(*at("tt", t, LEVELS - 1, g))
                        pe.wait_ge(*at("a_rows", t))
                        pe.wait_ge(*at("av_rows", t, g))
                        fill(pe, f"X{g}", "w_rows", t, g)
                        for h in range(4 * g, 4 * g + 4):
                            mm = pe.matmul(g4(psum[f"X{g}"])[:, h % 4, :], Tt[:, h, :], R[:, h, :], start=True, stop=True)
                        mm.then_inc(*sig("w_done", t, g))
                    for g in range(2):
                        pe.wait_ge(*at("w_rows", t, g))
                        fill(pe, f"W{g}", "y0_rows", t, g)
                        for h in range(4 * g, 4 * g + 4):
                            o = g4(psum[f"W{g}"])[:, h % 4, :]
                            pe.matmul(o, AbT[:, h, 1, :], W[:, :, h, :], start=True, stop=False)
                            mm = pe.matmul(o, AkT[:, h, 1, :], V0[:, h, :], start=False, stop=True)
                        mm.then_inc(*sig("y0_done", t, g))
                    pe.wait_ge(*at("b_rows", t, 1))
                    for g in range(2):
                        fill(pe, f"X{g}", "m_bd", t, g)
                        for p in range(2 * g, 2 * g + 2):
                            mm = pe.matmul(psum[f"X{g}"][:, 256 * (p % 2):256 * (p % 2) + 256], W[:, 0, 2 * p:2 * p + 2, :].rearrange("p h j -> p (h j)"),
                                           Bc[:, p].rearrange("p c j -> p (c j)"), start=True, stop=True)
                        mm.then_inc(*sig("m_done", t, g))
                    pe.wait_ge(*at("y0_rows", t, 1))
                    fill(pe, "T0", "gt", t)
                    for p in range(NPAIR):
                        mm = pe.transpose(g4(psum["T0"])[:, p, :], g4(G1)[:, p, :], ident[:, :])
                    mm.then_inc(*sig("g_turned", t))
                    pe.wait_ge(*at("k_rows", t, 1))
                    for g in range(2):
                        fill(pe, f"W{g}", "c", t, g)
                        for p in range(2 * g, 2 * g + 2):
                            for c_ in range(2):
                                o = g4(psum[f"W{g}"])[:, 2 * (p % 2) + c_, :]
                                pe.matmul(o, Bc[:, p, c_, :], W[:, 1, 2 * p:2 * p + 2, :], start=True, stop=False)
                                mm = pe.matmul(o, Kc[:, p, c_, :], V0[:, 2 * p:2 * p + 2, CHUNK:], start=False, stop=True)
                        mm.then_inc(*sig("c_done", t, g))
                    next(turns, None)
                    pe.wait_ge(*at("gt", t))
                    pe.wait_ge(*at("m", t))
                    fill(pe, "P1", "y", t)
                    for c_ in range(2):
                        if t or c_:
                            pe.wait_ge(*(at("z", t, 0) if c_ else at("z", t - 1, 1)))
                        for p in range(NPAIR):
                            mm = pe.matmul(g4(psum["P1"])[64 * c_:64 * c_ + 64, p, :], GT[:, p, 64 * c_:64 * c_ + 64], Z[:, c_, p, :], start=True, stop=True)
                        if c_:
                            mm.then_inc(*sig("y_done", t))
                        fill(pe, "X0", "z", t, c_)
                        for p in range(NPAIR):
                            mm = pe.matmul(g4(psum["X0"])[:, p, :], MT[:, p, c_, :], Z[:, c_, p, :], start=True, stop=True)
                        mm.then_inc(*sig("z_done", t, c_))
                    next(turns, None)
                    if t + 1 < NT:
                        index_scores(t + 1, 0, 2)
                    pe.wait_ge(*at("y_out", t))
                    fill(pe, "T0", "mix_rwkv", t)
                    for p in range(NPAIR):
                        mm = pe.transpose(g4(psum["T0"])[:, p, :], g4(yc)[:, p, :], ident[:, :])
                    mm.then_inc(*sig("y_turned", t))

                    next(turns, None)
                for _ in attention(NT - 1):
                    pass

        with ExitStack() as scope:
            S.phase(nc, scope, "route")
            A = Arena(arena_t, ARENA)
            wout = A.take(KD, D)
            mixT, xin, x1, xn, h2T = (A.take(2, D) for _ in range(5))
            gate_row, junk = A.take(D), A.take(D)
            L = A.take(NT, NG + NE)
            E12, M = A.take(NT, 2, NE), A.take(NT, NE)
            macc = A.take(NT + 1, NE)
            gcand, ghot, el, cand, h1, h2 = A.take(NT, NG), A.take(NT, NG), A.take(NT, EPG), A.take(NT, EPG), A.take(NT, EPG), A.take(NT, EPG)
            esel = A.take(NT, NG, EPG)
            gm, pg, v1, v2, e2, den = (A.take(NT) for _ in range(6))
            more, nblk, last, begin = A.take(NE, SEQ // BLK - 1), A.take(NE + 1), A.take(NE), A.take(NE)
            RS, picked, destf = A.take(NT, NE), A.take(NT, 2, NE), A.take(NT, 2)
            token_f, table, zeros = A.take(NT), A.take(BLK), A.take(ROWS // P)
            s_x = st[:, 0:32]
            assert A.at <= WEIGHTS_AT
            A.at = WEIGHTS_AT
            next_gate, next_up, next_down = A.take(KD, DE), A.take(KD, DE), A.take(KE, D)
            kt = lambda ap, t: ap[:, t % 2, :].rearrange("p (k s) -> p k s", k=KD)
            tile = lambda t: slice(P * t, P * t + P)
            groups = lambda ap: ap.rearrange("p t (g e) -> p t g e", g=NG)
            block = scope.enter_context(nc.Block())

            @block.sync
            def _(sp):
                sp.dma_start(gate_row, mod_d[0:1, :].to_broadcast([P, D])).then_inc(*sig("gate_loaded", 0, by=16))

                def load(t):
                    if t >= 2:
                        sp.wait_ge(*at("out_done", t - 2))
                    sp.dma_start(kt(mixT, t), mix_d[:, :, tile(t)].rearrange("c p s -> p c s")).then_inc(*sig(f"mix_loaded{t % 2}", t, by=16))
                    if t >= 2:
                        sp.wait_ge(*at("x1", t - 2))
                    sp.dma_start(xin[:, t % 2, :], x[0, tile(t), :]).then_inc(*sig(f"x_loaded{t % 2}", t, by=16))

                load(0)
                sp.dma_start(wout, w_out[0].rearrange("(k p) n -> p k n", p=P)).then_inc(*sig("wout_loaded", 0, by=16))
                for i, (dst, src) in enumerate(((next_gate, e_gate), (next_up, e_up), (next_down, e_down))):
                    sp.dma_start(dst, src[0, 0].rearrange("(k p) n -> p k n", p=P)).then_inc(*sig("weights_loaded", i, by=16))
                for t in range(NT):
                    if t + 1 < NT:
                        load(t + 1)
                    sp.wait_ge(*at("x1", t))
                    sp.dma_start(x1_d[tile(t), :], x1[:, t % 2, :]).then_inc(*sig(f"x1_stored{t % 2}", t, by=16))
                    sp.wait_ge(*at("xn", t))
                    sp.dma_start(xn2_d[tile(t), :], xn[:, t % 2, :]).then_inc(*sig(f"xn_stored{t % 2}", t, by=16))
                for t in (NT - 2, NT - 1):
                    sp.wait_ge(*at(f"x1_stored{t % 2}", t))
                    sp.wait_ge(*at(f"xn_stored{t % 2}", t))
                sp.wait_ge(*at("weights_loaded", 2))

            @block.gpsimd
            def _(pool):
                link(pool, pool.memset(zeros, 0.0), "zeros", 0)
                pool.dma_start(table_d.rearrange("(p b) o -> p (b o)", p=P), zeros).then_inc(*sig("table_zero", 0, by=16))
                link(pool, pool.tensor_copy(token_f, token_id[:, :]), "tokens", 0)
                for t in range(NT):
                    pool.wait_ge(*at("x_var", t))
                    pool.tensor_tensor(s_x[:, 16 + t:17 + t], s_x[:, 8 + t:9 + t], mhalf[:, 0:1], ALU.pow).then_inc(*sig("x_rstd", t))
                pool.wait_ge(*at("table_zero", 0))
                pool.wait_ge(*at("dest", 0))
                for t in range(NT):
                    for j in range(2):
                        pool.indirect_dma_start(table_d[:, :], bass.IndirectOffsetOnAxis(ap=dest[:, t, j:j + 1], axis=0), token_f[:, t:t + 1], None)\
                            .then_inc(*sig("scattered", t, j, by=16))
                pool.wait_ge(*at("scattered", NT - 1, 1))
                pool.dma_start(table[0:ALL_BLOCKS, :], table_d.rearrange("(b p) o -> b (p o)", p=BLK)).then_inc(*sig("table_loaded", 0, by=16))

            @block.scalar
            def _(act):
                for t in range(NT):
                    act.wait_ge(*at("x1", t))
                    link(act, act.activation(junk, x1[:, t % 2, :], ACT.Square, accum_out=s_x[:, t:t + 1]), "x_squares", t)
                    for k in range(KD):
                        if k == 0 and t >= 2:
                            act.wait_ge(*at("logits", t - 2))
                        if k % 4 == 0:
                            act.wait_ge(*at("xn_turned", t, k // 4))
                        link(act, act.activation(kt(h2T, t)[:, k, :], g4(psum[f"T{k // 4}"])[:, k % 4, :], ACT.Identity,
                                                 bias=mod_cols[:, 2, k:k + 1], scale=mod_cols[:, 3, k:k + 1]), "h2T", t, k)
                act.wait_ge(*at("gdiff", 0))
                link(act, act.activation(gcand, gcand, ACT.Exp), "gexp", 0)
                act.wait_ge(*at("ediff", 0))
                link(act, act.activation(e2, e2, ACT.Exp), "eexp", 0)

            @block.vector
            def _(dve):
                def step(ins):
                    link(dve, ins, "dve_step")

                def add_bias(t):
                    dve.wait_ge(*at("logits", t))
                    link(dve, dve.tensor_tensor(L[:, t, :], psum["X0"][:, 0:NG + NE], r_brt[:, :], ALU.add), "L", t)

                dve.wait_ge(*at("gate_loaded", 0))
                for t in range(NT):
                    b = t % 2
                    dve.wait_ge(*at("out_done", t))
                    dve.wait_ge(*at(f"x_loaded{b}", t))
                    if t >= 2:
                        dve.wait_ge(*at(f"x1_stored{b}", t - 2))
                        dve.wait_ge(*at("x_squares", t - 2))
                    step(dve.tensor_tensor(x1[:, b, :], psum["P"], gate_row, ALU.mult))
                    link(dve, dve.tensor_tensor(x1[:, b, :], x1[:, b, :], xin[:, b, :], ALU.add), "x1", t)
                    dve.wait_ge(*at("x_squares", t))
                    link(dve, dve.tensor_scalar(s_x[:, 8 + t:9 + t], s_x[:, t:t + 1], 1.0 / D, NORM_EPS, ALU.mult, ALU.add), "x_var", t)
                    dve.wait_ge(*at("x_rstd", t))
                    if t >= 2:
                        dve.wait_ge(*at(f"xn_stored{b}", t - 2))
                        dve.wait_ge(*at("xn_turned", t - 2, 1))
                    link(dve, dve.tensor_scalar(xn[:, b, :], x1[:, b, :], s_x[:, 16 + t:17 + t], None, ALU.mult), "xn", t)
                    if t >= 2:
                        add_bias(t - 2)
                for t in (NT - 2, NT - 1):
                    add_bias(t)

                def first_of(hot, cand_, values, top, n):
                    step(dve.tensor_reduce(top, values, AX_X, ALU.max))
                    step(dve.tensor_tensor(cand_, values, over(top, n), ALU.is_equal))
                    step(dve.tensor_tensor(cand_, cand_, each(iota8[:, EPG - n:], NT), ALU.mult))
                    step(dve.tensor_reduce(den, cand_, AX_X, ALU.max))
                    step(dve.tensor_tensor(hot, cand_, over(den, n), ALU.is_equal))

                first_of(ghot, gcand, L[:, :, 0:NG], gm, NG)
                link(dve, dve.tensor_tensor(gcand, L[:, :, 0:NG], over(gm, NG), ALU.subtract), "gdiff", 0)
                dve.wait_ge(*at("gexp", 0))
                step(dve.tensor_reduce(den, gcand, AX_X, ALU.add))
                step(dve.reciprocal(pg, den))
                ghot_wide = ghot.unsqueeze(3).to_broadcast([P, NT, NG, EPG])
                step(dve.tensor_tensor(esel, groups(L[:, :, NG:]), ghot_wide, ALU.mult))
                step(dve.tensor_reduce(el, esel.rearrange("p t g e -> p t e g"), AX_X, ALU.add))
                first_of(h1, cand, el, v1, EPG)
                step(dve.scalar_tensor_tensor(out=el, in0=h1, scalar=MASKED, in1=el, op0=ALU.mult, op1=ALU.add))
                first_of(h2, cand, el, v2, EPG)
                link(dve, dve.tensor_tensor(e2, v2, v1, ALU.subtract), "ediff", 0)
                dve.wait_ge(*at("eexp", 0))
                step(dve.tensor_scalar(den, e2, 1.0, None, ALU.add))
                step(dve.reciprocal(v1, den))
                step(dve.tensor_tensor(wgt[:, :, 0], pg, v1, ALU.mult))
                step(dve.tensor_tensor(wgt[:, :, 1], wgt[:, :, 0], e2, ALU.mult))
                for j, hot in enumerate((h1, h2)):
                    step(dve.tensor_tensor(groups(E12[:, :, j, :]), ghot_wide, hot.unsqueeze(2).to_broadcast([P, NT, NG, EPG]), ALU.mult))
                step(dve.tensor_tensor(M, E12[:, :, 0, :], E12[:, :, 1, :], ALU.add))
                step(dve.memset(macc[:, 0, :], 0.0))
                for t in range(NT):
                    link(dve, dve.tensor_tensor(macc[:, t + 1, :], macc[:, t, :], M[:, t, :], ALU.add), "macc", t)
                dve.wait_ge(*at("ranks", 0))
                counts = psum["W0"][:, NT * NE:(NT + 1) * NE]
                step(dve.tensor_tensor(more, over(counts, SEQ // BLK - 1), each(steps[:, :], NE), ALU.is_gt))
                step(dve.tensor_reduce(last, more, AX_X, ALU.add))
                step(dve.tensor_scalar(last, last, 1.0, None, ALU.add))
                step(dve.memset(nblk[:, 0:1], 0.0))
                step(dve.tensor_tensor_scan(nblk[:, 1:], ones[:, 0:NE], last, 0.0, ALU.mult, ALU.add))
                step(dve.tensor_copy(first_block[:, :], nblk))
                step(dve.tensor_scalar(begin, nblk[:, 0:NE], float(BLK), None, ALU.mult))
                step(dve.tensor_tensor(RS, psum["W0"][:, 0:NT * NE].rearrange("p (t e) -> p t e", t=NT), each(begin, NT), ALU.add))
                step(dve.tensor_tensor(picked, E12, RS.unsqueeze(2).to_broadcast([P, NT, 2, NE]), ALU.mult))
                step(dve.tensor_reduce(destf, picked, AX_X, ALU.add))
                link(dve, dve.tensor_copy(dest[:, :, :], destf), "dest", 0)
                dve.wait_ge(*at("table_turned", 0))
                link(dve, dve.tensor_copy(idx_all[:, :], psum["W1"][0:BLK, 0:ALL_BLOCKS]), "idx_all", 0)

            @block.tensor
            def _(pe):
                pe.wait_ge(*at("wout_loaded", 0))

                def project_out(t):
                    pe.wait_ge(*at(f"mix_loaded{t % 2}", t))
                    for half in range(2):
                        fill(pe, f"P{half}", "x1", t)
                        for k in range(KD):
                            mm = pe.matmul(psum[f"P{half}"], kt(mixT, t)[:, k, :], wout[:, k, 512 * half:512 * half + 512], start=(k == 0), stop=(k == KD - 1))
                    mm.then_inc(*sig("out_done", t))

                def route(t):
                    pe.wait_ge(*at("h2T", t, KD - 1))
                    fill(pe, "X0", "L", t)
                    for k in range(KD):
                        mm = pe.matmul(psum["X0"][:, 0:NG + NE], kt(h2T, t)[:, k, :], wrt[:, k, :], start=(k == 0), stop=(k == KD - 1))
                    mm.then_inc(*sig("logits", t))

                project_out(0)
                for t in range(NT):
                    if t + 1 < NT:
                        project_out(t + 1)
                    if t:
                        route(t - 1)
                    pe.wait_ge(*at("xn", t))
                    for g in range(2):
                        fill(pe, f"T{g}", "h2T", t, 4 * g + 3)
                        for k in range(4 * g, 4 * g + 4):
                            mm = pe.transpose(g4(psum[f"T{g}"])[:, k % 4, :], kt(xn, t)[:, k, :], ident[:, :])
                        mm.then_inc(*sig("xn_turned", t, g))
                route(NT - 1)
                for t in range(NT):
                    pe.wait_ge(*at("macc", t))
                    o = psum["W0"][:, NE * t:NE * t + NE]
                    pe.matmul(o, ones[:, :], macc[:, t, :], start=True, stop=False)
                    pe.matmul(o, before[:, :], M[:, t, :], start=False, stop=True)
                pe.matmul(psum["W0"][:, NT * NE:NT * NE + NE], ones[:, :], macc[:, NT, :], start=True, stop=True).then_inc(*sig("ranks", 0))
                pe.wait_ge(*at("table_loaded", 0))
                pe.transpose(psum["W1"][0:BLK, 0:ALL_BLOCKS], table[0:ALL_BLOCKS, :], ident[0:ALL_BLOCKS, 0:ALL_BLOCKS]).then_inc(*sig("table_turned", 0))

        with ExitStack() as scope:
            S.phase(nc, scope, "experts")
            A = Arena(arena_t, ARENA)
            others = [(A.take(KD, DE), A.take(KD, DE), A.take(KE, D)) for _ in range(SLOTS - 1)]
            rows, xT, y_sb = A.take(D)[0:BLK], A.take(KD, BLK), A.take(D // 2)
            th, hid, hidT = A.take(DE // 2), A.take(DE // 2), A.take(KE // 2, 2, BLK)
            rows_in = A.take(D)[0:BLK]
            index_now = A.take(1)[0:BLK].bitcast(I32)
            assert A.at <= WEIGHTS_AT
            A.at = WEIGHTS_AT
            gate_w, up_w, down_w = zip((A.take(KD, DE), A.take(KD, DE), A.take(KE, D)), *others)
            q = S.sem
            block = scope.enter_context(nc.Block())

            def bounds(eng, e):
                return (eng.value_load(first_block[0:1, bass.ds(e, 1)], min_val=0, max_val=MAX_BLOCKS),
                        eng.value_load(first_block[0:1, bass.ds(e + 1, 1)], min_val=1, max_val=MAX_BLOCKS))

            @block.sync
            def _(sp):
                sp.sem_inc(q("y_stored"), 16)
                def load(e, u):
                    sp.dma_start(gate_w[u], e_gate[0, bass.ds(e, 1)].rearrange("a (k p) n -> p (a k) n", p=P)).then_inc(q(f"gate_loaded{u}"), 16)
                    sp.dma_start(up_w[u], e_up[0, bass.ds(e, 1)].rearrange("a (k p) n -> p (a k) n", p=P)).then_inc(q(f"up_loaded{u}"), 16)
                    sp.dma_start(down_w[u], e_down[0, bass.ds(e, 1)].rearrange("a (k p) n -> p (a k) n", p=P)).then_inc(q(f"down_loaded{u}"), 16)

                def store_blocks(e):
                    first, end = bounds(sp, e)
                    with sp.Fori(first, end) as b:
                        sp.wait_ge(q("y_ready"), b + 2)
                        sp.dma_start(y_d[bass.ds(b * BLK, BLK), :].rearrange("r (h n) -> h r n", h=2), y_sb).then_inc(q("y_stored"), 16)
                    return end

                for name in ("gate_loaded0", "up_loaded0", "down_loaded0"):
                    sp.sem_inc(q(name), 16)
                for e in range(1, SLOTS):
                    load(e, e)

                def expert(e, u, reload):
                    end = store_blocks(e)
                    if reload:
                        sp.wait_ge(q("y_done"), end + 1)
                        load(e + SLOTS, u)

                trips = NE // SLOTS - 1
                with sp.Fori(0, trips) as trip:
                    for u in range(SLOTS):
                        expert(trip * SLOTS + u, u, True)
                for e in range(trips * SLOTS, NE):
                    expert(e, e % SLOTS, e + SLOTS < NE)

            @block.gpsimd
            def _(pool):
                total = pool.value_load(first_block[0:1, NE:NE + 1], min_val=1, max_val=MAX_BLOCKS)
                with pool.Fori(0, total + 1) as b:
                    pool.wait_ge(q("rows_ready"), b + 1)
                    pool.sem_inc(q("rows_seen"))
                    pool.tensor_copy(index_now, idx_all[:, bass.ds(b, 1)]).then_inc(q("index_ready"), 1)
                    pool.wait_ge(q("index_ready"), b + 1)
                    pool.sem_inc(q("index_seen"))
                    pool.indirect_dma_start(rows_in, None, xn2_d[:, :], bass.IndirectOffsetOnAxis(ap=index_now, axis=0)).then_inc(q("gathered"), 16)
                pool.wait_ge(q("gathered"), (total + 1) * 16)

            @block.scalar
            def _(act):
                act.sem_inc(q("y_ready"))
                act.sem_inc(q("rows_ready"))
                total = act.value_load(first_block[0:1, NE:NE + 1], min_val=1, max_val=MAX_BLOCKS)

                def take_rows(b):
                    act.wait_ge(q("gathered"), (b + 1) * 16)
                    act.wait_ge(q("turned"), b + 1)
                    act.activation(rows, rows_in, ACT.Copy).then_inc(q("rows_ready"), 1)

                take_rows(0)
                with act.Fori(0, total) as b:
                    take_rows(b + 1)
                    act.wait_ge(q("gate_done"), b + 1)
                    act.wait_ge(q("half_gated"), b + 1)
                    act.activation(th, psum["X0"][:, 0:DE // 2], ACT.Tanh, scale=0.5).then_inc(q("tanh_done"), 1)
                    act.wait_ge(q("y_done"), b + 2)
                    act.wait_ge(q("y_stored"), (b + 1) * 16)
                    act.activation(y_sb, psum["P0"], ACT.Copy).then_inc(q("y_ready"), 1)

            @block.vector
            def _(dve):
                for sem in (q("half_gated"), q("hidden")):
                    dve.sem_inc(sem)
                total = dve.value_load(first_block[0:1, NE:NE + 1], min_val=1, max_val=MAX_BLOCKS)

                def scale_rows(b):
                    dve.wait_ge(q("turned"), b + 2)
                    dve.tensor_tensor(xT, g8(psum["T0"]), over(mod_cols[:, 3, :], BLK), ALU.mult).then_inc(q("xT_scaled"), 1)
                    dve.wait_ge(q("xT_scaled"), b + 1)
                    dve.tensor_tensor(xT, xT, over(mod_cols[:, 2, :], BLK), ALU.add).then_inc(q("xT_ready"), 1)

                scale_rows(0)
                with dve.Fori(0, total) as b:
                    dve.wait_ge(q("tanh_done"), b + 1)
                    dve.wait_ge(q("hid_turned"), b + 1)
                    dve.scalar_tensor_tensor(out=hid, in0=th, scalar=1.0, in1=psum["X0"][:, 0:DE // 2], op0=ALU.add, op1=ALU.mult).then_inc(q("half_gated"), 1)
                    dve.wait_ge(q("half_gated"), b + 2)
                    dve.wait_ge(q("up_done"), b + 1)
                    dve.scalar_tensor_tensor(out=hid, in0=hid, scalar=0.5, in1=psum["X1"][:, 0:DE // 2], op0=ALU.mult, op1=ALU.mult).then_inc(q("hidden"), 1)
                    dve.wait_ge(q("y_done"), b + 1)
                    dve.wait_ge(q("hid_turned"), b + 2)
                    dve.tensor_copy(hidT, psum["W0"][:, 0:DE // 2].rearrange("p (f h r) -> p f h r", f=KE // 2, h=2)).then_inc(q("hidT_ready"), 1)
                    scale_rows(b + 1)
                dve.wait_ge(q("y_stored"), (total + 1) * 16)
                dve.tensor_copy(hid[:, 0:1], y_sb[:, 0:1])

            @block.tensor
            def _(pe):
                for sem in (q("turned"), q("hid_turned"), q("y_done")):
                    pe.sem_inc(sem)
                def turn_rows(b):
                    pe.wait_ge(q("rows_ready"), b + 2)
                    pe.sem_inc(q("rows_taken"))
                    for k in range(KD):
                        mm = pe.transpose(psum["T0"][:, BLK * k:BLK * k + BLK], rows[:, P * k:P * k + P], ident[0:BLK, 0:BLK])
                    mm.then_inc(q("turned"), 1)

                turn_rows(0)
                def expert(e, u, nth):
                    first, end = bounds(pe, e)
                    with pe.Fori(first, end) as b:
                        pe.wait_ge(q(f"gate_loaded{u}"), nth)
                        pe.wait_ge(q(f"up_loaded{u}"), nth)
                        pe.wait_ge(q(f"down_loaded{u}"), nth)
                        pe.wait_ge(q("xT_ready"), b + 1)
                        pe.wait_ge(q("hidden"), b + 1)
                        for bank, w, done in (("X0", gate_w[u], q("gate_done")), ("X1", up_w[u], q("up_done"))):
                            for k in range(KD):
                                for h in range(2):
                                    mm = pe.matmul(psum[bank][BLK * h:BLK * h + BLK, 0:DE // 2], xT[:, k, :], w[:, k, DE // 2 * h:DE // 2 * (h + 1)],
                                                   start=(k == 0), stop=(k == KD - 1))
                            mm.then_inc(done, 1)
                        turn_rows(b + 1)
                        pe.wait_ge(q("hidden"), b + 2)
                        for f in range(KE // 2):
                            mm = pe.transpose(psum["W0"][:, P * f:P * f + P], hid[:, P * f:P * f + P], ident[:, :])
                        mm.then_inc(q("hid_turned"), 1)
                        pe.wait_ge(q("hidT_ready"), b + 1)
                        pe.wait_ge(q("y_ready"), b + 1)
                        for i in range(KE):
                            f, h = i // 2, i % 2
                            for half in range(2):
                                mm = pe.matmul(psum["P0"][BLK * half:BLK * half + BLK, :], hidT[:, f, h, :],
                                               down_w[u][:, KE // 2 * h + f, D // 2 * half:D // 2 * (half + 1)], start=(i == 0), stop=(i == KE - 1))
                        mm.then_inc(q("y_done"), 1)

                with pe.Fori(0, NE // SLOTS) as trip:
                    for u in range(SLOTS):
                        expert(trip * SLOTS + u, u, (trip + 1) * 16)
                for e in range(NE // SLOTS * SLOTS, NE):
                    expert(e, e % SLOTS, (e // SLOTS + 1) * 16)

        with ExitStack() as scope:
            S.phase(nc, scope, "finish")
            A = Arena(arena_t, ARENA)
            first, second, x1, res, normed = (A.take(2, D) for _ in range(5))
            gate_row, shift_row, gain_row, junk = (A.take(D) for _ in range(4))
            s_x = st[:, 0:32]
            tile = lambda t: slice(P * t, P * t + P)
            block = scope.enter_context(nc.Block())

            @block.sync
            def _(sp):
                for i, dst in ((1, gate_row), (2, shift_row), (3, gain_row)):
                    sp.dma_start(dst, mod_d[i:i + 1, :].to_broadcast([P, D])).then_inc(*sig("rows_loaded", i, by=16))

                def load(t):
                    if t >= 2:
                        sp.wait_ge(*at("x2", t - 2))
                    sp.dma_start(x1[:, t % 2, :], x1_d[tile(t), :]).then_inc(*sig(f"x1_loaded{t % 2}", t, by=16))

                load(0)
                for t in range(NT):
                    if t + 1 < NT:
                        load(t + 1)
                    sp.wait_ge(*at("out", t))
                    sp.dma_start(out[0, tile(t), :], normed[:, t % 2, :]).then_inc(*sig(f"out_stored{t % 2}", t, by=16))
                for t in (NT - 2, NT - 1):
                    sp.wait_ge(*at(f"out_stored{t % 2}", t))

            @block.gpsimd
            def _(pool):
                def gather(t):
                    for j, (dst, used) in enumerate(((first, "moe"), (second, "moe"))):
                        if t >= 2:
                            pool.wait_ge(*at(used, t - 2))
                        pool.indirect_dma_start(dst[:, t % 2, :], None, y_d[:, :], bass.IndirectOffsetOnAxis(ap=dest[:, t, j:j + 1], axis=0))\
                            .then_inc(*sig(f"gathered{j}{t % 2}", t, by=16))

                gather(0)
                for t in range(NT):
                    if t + 1 < NT:
                        gather(t + 1)
                    pool.wait_ge(*at("x_var", t))
                    pool.tensor_tensor(s_x[:, 16 + t:17 + t], s_x[:, 8 + t:9 + t], mhalf[:, 0:1], ALU.pow).then_inc(*sig("x_rstd", t))

            @block.scalar
            def _(act):
                for t in range(NT):
                    act.wait_ge(*at(f"gathered0{t % 2}", t))
                    link(act, act.activation(first[:, t % 2, :], first[:, t % 2, :], ACT.Copy, scale=wgt[:, t, 0:1]), "weighted_first", t)
                    act.wait_ge(*at("x2", t))
                    link(act, act.activation(junk, res[:, t % 2, :], ACT.Square, accum_out=s_x[:, t:t + 1]), "x_squares", t)

            @block.vector
            def _(dve):
                def step(ins):
                    link(dve, ins, "dve_step")

                dve.wait_ge(*at("rows_loaded", 3))
                for t in range(NT):
                    b = t % 2
                    dve.wait_ge(*at("weighted_first", t))
                    dve.wait_ge(*at(f"gathered1{b}", t))
                    if t >= 2:
                        dve.wait_ge(*at("x_squares", t - 2))
                    link(dve, dve.scalar_tensor_tensor(out=res[:, b, :], in0=second[:, b, :], scalar=wgt[:, t, 1:2], in1=first[:, b, :], op0=ALU.mult, op1=ALU.add), "moe", t)
                    step(dve.tensor_tensor(res[:, b, :], res[:, b, :], gate_row, ALU.mult))
                    dve.wait_ge(*at(f"x1_loaded{b}", t))
                    link(dve, dve.tensor_tensor(res[:, b, :], res[:, b, :], x1[:, b, :], ALU.add), "x2", t)
                    dve.wait_ge(*at("x_squares", t))
                    link(dve, dve.tensor_scalar(s_x[:, 8 + t:9 + t], s_x[:, t:t + 1], 1.0 / D, NORM_EPS, ALU.mult, ALU.add), "x_var", t)
                    dve.wait_ge(*at("x_rstd", t))
                    if t >= 2:
                        dve.wait_ge(*at(f"out_stored{b}", t - 2))
                    step(dve.scalar_tensor_tensor(out=normed[:, b, :], in0=res[:, b, :], scalar=s_x[:, 16 + t:17 + t], in1=gain_row, op0=ALU.mult, op1=ALU.mult))
                    link(dve, dve.tensor_tensor(normed[:, b, :], normed[:, b, :], shift_row, ALU.add), "out", t)


_INS = ['x', 'c', 'ada_w', 'ada_b', 'norm1_g', 'w_in', 'shift_mu', 'w0', 'w_decay_up', 'a0', 'w_aaa_up', 'w_gate_up',
        'k_k', 'k_a', 'r_k', 'gn_g', 'gn_b', 'kv_norm_g', 'k_idx_norm_g', 'w_uk', 'w_uv', 'w_out', 'norm2_g',
        'w_group', 'b_group', 'w_expert', 'b_expert', 'e_gate', 'e_up', 'e_down',
        'final_ada_w', 'final_ada_b', 'final_norm_g']


def kernel(**inputs):
    import numpy as _np
    import concourse.bacc as _bacc
    from concourse import mybir as _mybir
    from concourse.bass_utils import run_bass_kernel_spmd as _run

    arrays = {f"in_{name}_dram": _np.ascontiguousarray(inputs[name]) for name in _INS}
    numbers = None
    for _ in range(2):
        nc = _bacc.Bacc("TRN2", target_bir_lowering=False, num_devices=1)
        args = [nc.dram_tensor(n, a.shape, _mybir.dt.from_np(a.dtype), kind="ExternalInput").ap() for n, a in arrays.items()]
        args.append(nc.dram_tensor("out_0_dram", (1, SEQ, D), _mybir.dt.float32, kind="ExternalOutput").ap())
        signals = Signals(numbers)
        sparse_attention_moe_layer(nc, *args, signals)
        numbers = signals.seen
    r = _run(nc, [arrays], core_ids=[0])
    return r.results[0]["out_0_dram"]
```
